# Optimizing a Trainium2 kernel written in Bass

```python
import math
import jax, jax.numpy as jnp
from jax import lax
import numpy as np

D_MODEL = 1024
BATCH = 1
SEQ = 256
DEPTH = 1

CHUNK = 64
RET_HEADS = 4
RET_HEAD_DIM = D_MODEL // 8
RET_WIDTH = RET_HEADS * RET_HEAD_DIM
POOL_WINDOWS = (2, 4, 8, 16)
POOL_GROUPS = len(POOL_WINDOWS)
POOL_GROUP_DIM = D_MODEL // 8
POOL_WIDTH = POOL_GROUPS * POOL_GROUP_DIM
MIX_WIDTH = RET_WIDTH + POOL_WIDTH
IN_WIDTH = 4 * RET_WIDTH + POOL_WIDTH
D_FF = ((8 * D_MODEL // 3 + 127) // 128) * 128
CONV_WIDTH = 3
ROPE_BASE = 10000.0
LN_EPS = 1e-5
RMS_EPS = 1e-6
DEEPNORM_ALPHA = (2.0 * DEPTH) ** 0.25
DEEPNORM_BETA = (8.0 * DEPTH) ** -0.25


def _layernorm(x, g, b):
    xf = x.astype(jnp.float32)
    mu = jnp.mean(xf, axis=-1, keepdims=True)
    var = jnp.mean(jnp.square(xf - mu), axis=-1, keepdims=True)
    y = (xf - mu) * lax.rsqrt(var + LN_EPS) * g.astype(jnp.float32) + b.astype(jnp.float32)
    return y.astype(x.dtype)

def _rope(t):
    s, dh = t.shape[1], t.shape[-1]
    inv_freq = ROPE_BASE ** (-jnp.arange(0, dh, 2, dtype=jnp.float32) / dh)
    ang = jnp.arange(s, dtype=jnp.float32)[:, None] * inv_freq[None, :]
    cos = jnp.cos(ang)[None, :, None, :]
    sin = jnp.sin(ang)[None, :, None, :]
    tf = t.astype(jnp.float32)
    t1, t2 = tf[..., : dh // 2], tf[..., dh // 2:]
    return jnp.concatenate([t1 * cos - t2 * sin, t1 * sin + t2 * cos], axis=-1)

def _retention(q, k, v):
    b, s, h, dh = q.shape
    nc = s // CHUNK
    log_gamma = jnp.log(1.0 - 2.0 ** (-5.0 - jnp.arange(h, dtype=jnp.float32)))
    idx = jnp.arange(CHUNK, dtype=jnp.float32)
    inner_decay = jnp.exp(log_gamma[:, None, None] * jnp.abs(idx[:, None] - idx[None, :]))
    q_decay = jnp.exp(log_gamma[None, :] * (idx[:, None] + 1.0))
    k_decay = jnp.exp(log_gamma[None, :] * (CHUNK - 1.0 - idx[:, None]))
    chunk_decay = jnp.exp(log_gamma * CHUNK)

    qc = q.reshape(b, nc, CHUNK, h, dh)
    kc = k.reshape(b, nc, CHUNK, h, dh)
    vc = v.reshape(b, nc, CHUNK, h, dh)

    scores = jnp.einsum('bnihd,bnjhd->bnhij', qc, kc) * inner_decay[None, None]
    inner = jnp.einsum('bnhij,bnjhe->bnihe', scores, vc)

    def step(state, inp):
        q_n, k_n, v_n = inp
        cross = jnp.einsum('bihd,bhde->bihe', q_n * q_decay[None, :, :, None], state)
        new_state = state * chunk_decay[None, :, None, None] + jnp.einsum(
            'bjhd,bjhe->bhde', k_n * k_decay[None, :, :, None], v_n)
        return new_state, cross

    state0 = jnp.zeros((b, h, dh, dh), jnp.float32)
    xs = (jnp.moveaxis(qc, 1, 0), jnp.moveaxis(kc, 1, 0), jnp.moveaxis(vc, 1, 0))
    _, cross = lax.scan(step, state0, xs)
    out = inner + jnp.moveaxis(cross, 0, 1)
    return out.reshape(b, s, h, dh)

def _pool_mixer(p, w_pool, pool_scale):
    b, s, _ = p.shape
    pf = p.astype(jnp.float32).reshape(b, s, POOL_GROUPS, POOL_GROUP_DIM)
    cs = jnp.cumsum(pf, axis=1)
    pos = jnp.arange(1, s + 1, dtype=jnp.float32)
    outs = []
    for gi, w in enumerate(POOL_WINDOWS):
        c = cs[:, :, gi]
        prev = jnp.pad(c, ((0, 0), (w, 0), (0, 0)))[:, :s]
        mean = (c - prev) / jnp.minimum(pos, float(w))[None, :, None]
        outs.append(mean - pf[:, :, gi])
    pooled = jnp.stack(outs, axis=2).astype(p.dtype)
    y = jnp.einsum('bsgc,gcd->bsgd', pooled, w_pool).reshape(b, s, POOL_WIDTH)
    return y * pool_scale

def _conv_ffn(x, w_up, conv_w, conv_b, w_down):
    s = x.shape[1]
    u = x @ w_up
    val, gate = u[..., :D_FF], u[..., D_FF:]
    gp = jnp.pad(gate, ((0, 0), (CONV_WIDTH - 1, 0), (0, 0)))
    h = conv_b + sum(gp[:, j:j + s] * conv_w[j] for j in range(CONV_WIDTH))
    return (jax.nn.silu(h) * val) @ w_down

def first_inputs(seed: int = 0) -> dict:
    key = jax.random.key(seed)
    ks = jax.random.split(key, 20)
    f32 = jnp.float32
    L = DEPTH
    x = jax.random.normal(ks[0], (BATCH, SEQ, D_MODEL), f32)
    sd = D_MODEL ** -0.5
    w_qk = jax.random.normal(ks[1], (L, D_MODEL, 2 * RET_WIDTH), f32) * sd
    w_v = jax.random.normal(ks[2], (L, D_MODEL, RET_WIDTH), f32) * sd * DEEPNORM_BETA
    w_g = jax.random.normal(ks[3], (L, D_MODEL, RET_WIDTH), f32) * sd
    w_p = jax.random.normal(ks[4], (L, D_MODEL, POOL_WIDTH), f32) * sd * DEEPNORM_BETA
    w_in = jnp.concatenate([w_qk, w_v, w_g, w_p], axis=-1)
    w_pool = jax.random.normal(ks[5], (L, POOL_GROUPS, POOL_GROUP_DIM, POOL_GROUP_DIM), f32) * POOL_GROUP_DIM ** -0.5
    pool_scale = 1.0 + 0.1 * jax.random.normal(ks[6], (L, POOL_WIDTH), f32)
    w_out = jax.random.normal(ks[7], (L, MIX_WIDTH, D_MODEL), f32) * MIX_WIDTH ** -0.5 * DEEPNORM_BETA
    ln1_g = 1.0 + 0.05 * jax.random.normal(ks[8], (L, D_MODEL), f32)
    ln1_b = 0.02 * jax.random.normal(ks[9], (L, D_MODEL), f32)
    w_up = jax.random.normal(ks[10], (L, D_MODEL, 2 * D_FF), f32) * sd * DEEPNORM_BETA
    conv_w = jax.random.normal(ks[11], (L, CONV_WIDTH, D_FF), f32) * CONV_WIDTH ** -0.5
    conv_b = 0.02 * jax.random.normal(ks[12], (L, D_FF), f32)
    w_down = jax.random.normal(ks[13], (L, D_FF, D_MODEL), f32) * D_FF ** -0.5 * DEEPNORM_BETA
    ln2_g = 1.0 + 0.05 * jax.random.normal(ks[14], (L, D_MODEL), f32)
    ln2_b = 0.02 * jax.random.normal(ks[15], (L, D_MODEL), f32)
    return {"x": x, "w_in": w_in, "w_pool": w_pool, "pool_scale": pool_scale, "w_out": w_out,
            "ln1_g": ln1_g, "ln1_b": ln1_b, "w_up": w_up, "conv_w": conv_w, "conv_b": conv_b,
            "w_down": w_down, "ln2_g": ln2_g, "ln2_b": ln2_b}

def first_block(x, w_in, w_pool, pool_scale, w_out, ln1_g, ln1_b, w_up, conv_w, conv_b,
              w_down, ln2_g, ln2_b):
    b, s, _ = x.shape
    for l in range(DEPTH):
        proj = x @ w_in[l]
        q, k, v, g, p = jnp.split(proj, [RET_WIDTH, 2 * RET_WIDTH, 3 * RET_WIDTH, 4 * RET_WIDTH], axis=-1)
        q = _rope(q.reshape(b, s, RET_HEADS, RET_HEAD_DIM))
        k = _rope(k.reshape(b, s, RET_HEADS, RET_HEAD_DIM)) * (RET_HEAD_DIM ** -0.5)
        v = v.reshape(b, s, RET_HEADS, RET_HEAD_DIM).astype(jnp.float32)
        ret = _retention(q, k, v)
        ret = ret * lax.rsqrt(jnp.mean(jnp.square(ret), axis=-1, keepdims=True) + RMS_EPS)
        ret = ret.reshape(b, s, RET_WIDTH).astype(x.dtype) * jax.nn.silu(g)
        pool = _pool_mixer(p, w_pool[l], pool_scale[l])
        mix = jnp.concatenate([ret, pool], axis=-1) @ w_out[l]
        x = _layernorm(DEEPNORM_ALPHA * x + mix, ln1_g[l], ln1_b[l])
        ffn = _conv_ffn(x, w_up[l], conv_w[l], conv_b[l], w_down[l])
        x = _layernorm(DEEPNORM_ALPHA * x + ffn, ln2_g[l], ln2_b[l])
    return x


Q_BLOCK = 128
HG_HEADS = 8
HG_DK = 128
HG_DV = D_MODEL // HG_HEADS
HG_KW = HG_HEADS * HG_DK
HG_VW = HG_HEADS * HG_DV
FOX_HEADS = 8
FOX_DH = 128
FOX_W = FOX_HEADS * FOX_DH
MEM_LEN = 256
MEM_HEADS = 4
MEM_DH = D_MODEL // MEM_HEADS
D_FF_2 = 2816
N_BRANCH = 2
EPS = 1e-6
IN_SPLITS = [HG_KW, HG_KW, HG_VW, HG_VW, FOX_W, FOX_W, FOX_W, FOX_HEADS, N_BRANCH * D_MODEL]
IN_COLS = sum(IN_SPLITS)
IN_OFFSETS = list(np.cumsum(IN_SPLITS)[:-1])


def rmsnorm(x, g):
    x32 = x.astype(jnp.float32)
    y = x32 * lax.rsqrt(jnp.mean(x32 * x32, axis=-1, keepdims=True) + EPS)
    return (y * g.astype(jnp.float32)).astype(x.dtype)

def swiglu(h, w_in, w_down):
    gate, up = jnp.split(h @ w_in, 2, axis=-1)
    return (jax.nn.silu(gate) * up) @ w_down

def hgrn2_chunkwise(q, f_logit, inp, lb):
    B, S = q.shape[0], q.shape[1]
    n = S // CHUNK
    f = lb + (1.0 - lb) * jax.nn.sigmoid(f_logit.astype(jnp.float32))
    logf = jnp.log(f)
    k = 1.0 - f
    q = jax.nn.silu(q.astype(jnp.float32))
    inp = inp.astype(jnp.float32)

    def to_chunks(t):
        return t.reshape(B, n, CHUNK, t.shape[2], t.shape[3]).transpose(1, 0, 3, 2, 4)

    qc, kc, ic = to_chunks(q), to_chunks(k), to_chunks(inp)
    bc = jnp.cumsum(to_chunks(logf), axis=3)
    mask = jnp.tril(jnp.ones((CHUNK, CHUNK), dtype=bool))[:, :, None]

    def step(state, xs):
        qt, kt, it, bt = xs
        diff = bt[:, :, :, None, :] - bt[:, :, None, :, :]
        decay = jnp.exp(jnp.where(mask, diff, -jnp.inf))
        a = jnp.einsum('bhtd,bhsd,bhtsd->bhts', qt, kt, decay)
        o_intra = jnp.einsum('bhts,bhsv->bhtv', a, it)
        o_inter = jnp.einsum('bhtd,bhdv->bhtv', qt * jnp.exp(bt), state)
        b_last = bt[:, :, -1:, :]
        new_state = jnp.exp(b_last[:, :, 0, :])[..., None] * state + jnp.einsum(
            'bhsd,bhsv->bhdv', kt * jnp.exp(b_last - bt), it)
        return new_state, o_intra + o_inter

    s0 = jnp.zeros((B, q.shape[2], HG_DK, HG_DV), jnp.float32)
    _, o = lax.scan(step, s0, (qc, kc, ic, bc))
    return o.transpose(1, 0, 3, 2, 4).reshape(B, S, HG_VW)

def fox_attention(q, k, v, f_logit):
    B, S, H, dh = q.shape
    n_blk = S // Q_BLOCK
    scale = 1.0 / math.sqrt(dh)
    c = jnp.cumsum(jax.nn.log_sigmoid(f_logit.astype(jnp.float32)), axis=1).transpose(0, 2, 1)
    k32 = k.astype(jnp.float32)
    v32 = v.astype(jnp.float32)
    qb = q.astype(jnp.float32).reshape(B, n_blk, Q_BLOCK, H, dh).transpose(1, 0, 3, 2, 4)
    cb = c.reshape(B, H, n_blk, Q_BLOCK).transpose(2, 0, 1, 3)
    kpos = jnp.arange(S)

    def block(args):
        qi, ci, blk = args
        s = jnp.einsum('bhqd,bkhd->bhqk', qi, k32) * scale
        s = s + ci[..., None] - c[:, :, None, :]
        qpos = blk * Q_BLOCK + jnp.arange(Q_BLOCK)
        s = jnp.where(kpos[None, :] <= qpos[:, None], s, -jnp.inf)
        p = jax.nn.softmax(s, axis=-1)
        return jnp.einsum('bhqk,bkhd->bqhd', p, v32)

    o = lax.map(block, (qb, cb, jnp.arange(n_blk)))
    return o.transpose(1, 0, 2, 3, 4).reshape(B, S, H * dh)

def mem_cross_attention(h, mem_n, w_mq, w_mkv, w_mo):
    B, S, _ = h.shape
    q = (h @ w_mq).reshape(B, S, MEM_HEADS, MEM_DH).astype(jnp.float32)
    k, v = jnp.split(mem_n @ w_mkv, 2, axis=-1)
    k = k.reshape(B, MEM_LEN, MEM_HEADS, MEM_DH).astype(jnp.float32)
    v = v.reshape(B, MEM_LEN, MEM_HEADS, MEM_DH).astype(jnp.float32)
    s = jnp.einsum('bqhd,bkhd->bhqk', q, k) * (1.0 / math.sqrt(MEM_DH))
    p = jax.nn.softmax(s, axis=-1)
    o = jnp.einsum('bhqk,bkhd->bqhd', p, v).reshape(B, S, D_MODEL).astype(h.dtype)
    return o @ w_mo

def second_inputs(seed: int = 0) -> dict:
    key = jax.random.key(seed)
    ks = iter(jax.random.split(key, 40))
    f32 = jnp.float32

    def w(shape, fan_in):
        return jax.random.normal(next(ks), shape, f32) * (fan_in ** -0.5)

    def gain(shape):
        return 1.0 + 0.05 * jax.random.normal(next(ks), shape, f32)

    L, D = DEPTH, D_MODEL
    return {
        "x": jax.random.normal(next(ks), (BATCH, SEQ, D), f32),
        "mem": jax.random.normal(next(ks), (BATCH, MEM_LEN, D), f32),
        "ffn1_pre_g": gain((L, D)),
        "ffn1_w_in": w((L, D, 2 * D_FF_2), D),
        "ffn1_w_down": w((L, D_FF_2, D), D_FF_2),
        "ffn1_post_g": gain((L, D)),
        "mix_pre_g": gain((L, D)),
        "w_in": w((L, D, IN_COLS), D),
        "hg_lb_logits": 0.5 * jax.random.normal(next(ks), (L + 1, HG_HEADS, HG_DK), f32),
        "hg_norm_g": gain((L, HG_VW)),
        "fox_f_bias": 1.0 + 0.5 * jax.random.normal(next(ks), (L, FOX_HEADS), f32),
        "w_branch_a": w((L, HG_VW, D), HG_VW),
        "w_branch_b": w((L, FOX_W, D), FOX_W),
        "b_gate": 0.02 * jax.random.normal(next(ks), (L, N_BRANCH * D), f32),
        "w_out": w((L, D, D), D),
        "mix_post_g": gain((L, D)),
        "mem_pre_g": gain((L, D)),
        "mem_kv_g": gain((L, D)),
        "w_mq": w((L, D, D), D),
        "w_mkv": w((L, D, 2 * D), D),
        "w_mo": w((L, D, D), D),
        "mem_post_g": gain((L, D)),
        "ffn2_pre_g": gain((L, D)),
        "ffn2_w_in": w((L, D, 2 * D_FF_2), D),
        "ffn2_w_down": w((L, D_FF_2, D), D_FF_2),
        "ffn2_post_g": gain((L, D)),
    }

def second_block(x, mem, ffn1_pre_g, ffn1_w_in, ffn1_w_down, ffn1_post_g,
              mix_pre_g, w_in, hg_lb_logits, hg_norm_g, fox_f_bias,
              w_branch_a, w_branch_b, b_gate, w_out, mix_post_g,
              mem_pre_g, mem_kv_g, w_mq, w_mkv, w_mo, mem_post_g,
              ffn2_pre_g, ffn2_w_in, ffn2_w_down, ffn2_post_g):
    B, S, D = x.shape
    lb_all = jnp.cumsum(jax.nn.softmax(hg_lb_logits.astype(jnp.float32), axis=0), axis=0)
    for l in range(DEPTH):
        h = rmsnorm(x, ffn1_pre_g[l])
        x = x + 0.5 * rmsnorm(swiglu(h, ffn1_w_in[l], ffn1_w_down[l]), ffn1_post_g[l])

        h = rmsnorm(x, mix_pre_g[l])
        q_a, f_a, i_a, g_a, q_b, k_b, v_b, f_b, gates = jnp.split(h @ w_in[l], IN_OFFSETS, axis=-1)

        o_a = hgrn2_chunkwise(q_a.reshape(B, S, HG_HEADS, HG_DK),
                              f_a.reshape(B, S, HG_HEADS, HG_DK),
                              i_a.reshape(B, S, HG_HEADS, HG_DV), lb_all[l])
        o_a = rmsnorm(o_a.astype(x.dtype), hg_norm_g[l]) * jax.nn.silu(g_a)
        y_a = o_a @ w_branch_a[l]

        o_b = fox_attention(q_b.reshape(B, S, FOX_HEADS, FOX_DH),
                            k_b.reshape(B, S, FOX_HEADS, FOX_DH),
                            v_b.reshape(B, S, FOX_HEADS, FOX_DH),
                            f_b + fox_f_bias[l])
        y_b = o_b.astype(x.dtype) @ w_branch_b[l]

        gate = jax.nn.sigmoid((gates + b_gate[l]).astype(jnp.float32)).reshape(B, S, N_BRANCH, D)
        y = (gate[:, :, 0] * y_a.astype(jnp.float32) + gate[:, :, 1] * y_b.astype(jnp.float32)).astype(x.dtype)
        x = x + rmsnorm(y @ w_out[l], mix_post_g[l])

        h = rmsnorm(x, mem_pre_g[l])
        mem_n = rmsnorm(mem, mem_kv_g[l])
        x = x + rmsnorm(mem_cross_attention(h, mem_n, w_mq[l], w_mkv[l], w_mo[l]), mem_post_g[l])

        h = rmsnorm(x, ffn2_pre_g[l])
        x = x + 0.5 * rmsnorm(swiglu(h, ffn2_w_in[l], ffn2_w_down[l]), ffn2_post_g[l])
    return x


def setup_inputs(seed=0):
    out = dict(first_inputs(seed))
    for name, value in second_inputs(seed + 1).items():
        if name != "x":
            out[name + "_2"] = value
    return out


def reference(
    x, w_in, w_pool, pool_scale, w_out, ln1_g, ln1_b, w_up, conv_w, conv_b, w_down, ln2_g,
    ln2_b, mem_2, ffn1_pre_g_2, ffn1_w_in_2, ffn1_w_down_2, ffn1_post_g_2, mix_pre_g_2, w_in_2,
    hg_lb_logits_2, hg_norm_g_2, fox_f_bias_2, w_branch_a_2, w_branch_b_2, b_gate_2, w_out_2,
    mix_post_g_2, mem_pre_g_2, mem_kv_g_2, w_mq_2, w_mkv_2, w_mo_2, mem_post_g_2, ffn2_pre_g_2,
    ffn2_w_in_2, ffn2_w_down_2, ffn2_post_g_2,
):
    x = first_block(
        x, w_in, w_pool, pool_scale, w_out, ln1_g, ln1_b, w_up, conv_w, conv_b, w_down, ln2_g,
        ln2_b,
    )
    return second_block(
        x, mem_2, ffn1_pre_g_2, ffn1_w_in_2, ffn1_w_down_2, ffn1_post_g_2, mix_pre_g_2, w_in_2,
        hg_lb_logits_2, hg_norm_g_2, fox_f_bias_2, w_branch_a_2, w_branch_b_2, b_gate_2,
        w_out_2, mix_post_g_2, mem_pre_g_2, mem_kv_g_2, w_mq_2, w_mkv_2, w_mo_2, mem_post_g_2,
        ffn2_pre_g_2, ffn2_w_in_2, ffn2_w_down_2, ffn2_post_g_2,
    )


_drawn_inputs = setup_inputs


def setup_inputs(seed=0):
    import zlib

    import numpy as np

    out = dict(_drawn_inputs(seed))
    spreads = {}
    factors = {'conv_b': 8.0, 'b_gate_2': 8.0, 'ffn2_pre_g_2': 3.106, 'ffn2_post_g_2': 4.236}
    for name, (base, spread) in spreads.items():
        noise = np.random.default_rng([zlib.crc32(name.encode()), seed]).standard_normal(out[name].shape)
        drawn = base * np.exp(spread * noise) if base else spread * noise
        out[name] = __import__('jax').numpy.asarray(drawn.astype(out[name].dtype))
    for name, factor in factors.items():
        out[name] = (out[name] * factor).astype(out[name].dtype)
    return out
```

```python
from contextlib import ExitStack

import numpy as np

import concourse.bass as bass
from concourse import mybir

ALU = mybir.AluOpType
ACT = mybir.ActivationFunctionType
F32 = mybir.dt.float32
F32R = mybir.dt.float32r
BF16 = mybir.dt.bfloat16
U8 = mybir.dt.uint8
AX_X = mybir.AxisListType.X

P = 128
S = 256
TT = S // P
D = 1024
KC = D // P
NB = 512
RH = 4
FF = 2816
FC = FF // P
FB = FF // 256
CHUNK = 64
HH = 8
HALF = HH // 2
MH = 4
ALPHA = 2.0 ** 0.25
LN_EPS, RMS_EPS = 1e-5, 1e-6
SLOTS = 4
GSLOTS = 3
LEVELS = (1, 2, 4, 8, 16, 32, 64)
NEG = -1e30

GAINS = ("ln1_g", "ln1_b", "ln2_g", "ln2_b", "ffn1_pre", "ffn1_post", "mix_pre", "hg_norm", "gate0",
         "gate1", "mem_kv", "mix_post", "mem_pre", "mem_post", "ffn2_pre", "ffn2_post")
NORMS = ("ret0", "ret1", "ret2", "ret3", "ln1", "ln2", "ffn1_pre", "ffn1_post", "mix_pre", "hg",
         "mem_kv", "mix_post", "mem_pre", "mem_post", "ffn2_pre", "ffn2_post")
BLOCKS = (("win1", 5), ("wout1", 2), ("up1", FB), ("down1", 0), ("upA", FB), ("downA", 0),
          ("win2", 18), ("brA", 2), ("brB", 2), ("wout2", 2), ("mkv", 4), ("mq", 2), ("mo", 2),
          ("upB", FB), ("downB", 0))
WIN2 = (("f", 1024), ("f", 1536), ("q", 0), ("q", 512), ("i", 2048), ("i", 2560),
        ("fq", 4096), ("fq", 4608), ("fk", 5120), ("fk", 5632), ("g", 3072), ("g", 3584),
        ("fv", 6144), ("fv", 6656), ("gate", 7176), ("gate", 7688), ("gate", 8200), ("gate", 8712))
FLOGIT = 7168
HG_STEPS = tuple((hf, lv) for hf in range(2) for lv in (0, *LEVELS, 128))
HG_SLOT = {u: [] for u in range(36)}
for _n, _step in enumerate(HG_STEPS):
    _hf, _k = divmod(_n, len(HG_STEPS) // 2)
    HG_SLOT[8 * (_hf + 1) + max(_k - 1, 0)].append(_n)
FOX_SLOT = {u: [] for u in range(36)}
for _n in range(HH + 2):
    FOX_SLOT[min(28 + _n, 35)].append(_n)


def unit_starts():
    out, n = {}, 0
    for name, k in BLOCKS:
        out[name] = n
        n += 2 * k if k else FB
    out["end"] = n
    return out


def pair_plan():
    out, used = {}, [0, 0]
    for name, k in BLOCKS:
        for j in range(k or 2):
            out[name, j] = (j % 2, used[j % 2])
            used[j % 2] += 1
    return out


def aux_plan():
    order, out, used = [], {}, [0] * 8

    def use(key, bank=None):
        n = len(order)
        bank = 4 + n % 4 if bank is None else bank
        order.append(key)
        out[key] = (n, bank, used[bank])
        used[bank] += 1

    def splits(name, n=4):
        for g in range(n):
            use((name, g))

    splits("x")
    for what in "qk":
        for g in range(2):
            use(("rT" + what, g))
    for h in range(RH):
        use(("rscore", h))
    for g in range(2):
        use(("poolT", g))
    for tt in range(TT):
        use(("rout", tt))
    for g in range(2):
        use(("pooly", g))
    splits("mixr", 2)
    splits("x1")
    for j in range(FB):
        use(("convg", j), 6)
        use(("convv", j), 7)
    splits("f1")
    for j in range(FB):
        use(("hA", j), 4 + j % 2)
    splits("m2")
    use(("flog", 0))
    for u in range(36):
        j, last = u // 2, u % 2 == 1
        if u == 1:
            use(("flog", 1))
        if u >= 2 and not last and WIN2[j - 1][0] in ("f", "q", "fq", "fk"):
            for g in range(2):
                use((WIN2[j - 1][0] + "T", 2 * ((j - 1) % 2) + g))
        for n in HG_SLOT[u]:
            hf, lv = HG_STEPS[n]
            for g in range(1 if lv == 128 else 2):
                use(("lv", hf, lv, g))
            if lv == 128:
                for tt in range(TT):
                    use(("hgo", hf, tt))
        for n in FOX_SLOT[u]:
            if n < HH:
                use(("fs", n))
            if 1 <= n < HH + 1:
                use(("fp", n - 1))
            if n >= 2:
                use(("fo", n - 2))
    splits("oa")
    splits("ob")
    splits("memn")
    splits("y2")
    splits("mpre")
    for what in ("mkT", "mqT"):
        for g in range(4):
            use((what, g))
    for n in range(MH + 2):
        if n < MH:
            use(("ms", n))
        if 1 <= n < MH + 1:
            use(("mp", n - 1))
        if n >= 2:
            use(("mo", n - 2))
    splits("om")
    splits("f2")
    for j in range(FB):
        use(("hB", j), 4 + j % 2)
    return out


UNIT = unit_starts()
PAIR = pair_plan()
AUX = aux_plan()
NS = {name: TT * n for n, name in enumerate(NORMS)}


def build(nc, dram, out_dram):
    ctx = ExitStack()
    with ctx:
        nc_sem = {}

        def sem(name):
            if name not in nc_sem:
                nc_sem[name] = ctx.enter_context(nc.semaphore(name))
            return nc_sem[name]

        base = -(-nc.sbuf_base // 32) * 32
        top = nc.sbuf_top
        marks = {}

        def place(name, shape, dt, at):
            size = int(np.prod(shape[1:])) * {F32: 4, F32R: 4, BF16: 2, U8: 1}[dt]
            marks[name] = (at, at + size)
            assert base <= at and at + size <= top, (name, at, size, top)
            return nc.alloc_sbuf_tensor_at(name, shape, dt, offset=at)

        KB = 1024
        raw = place("raw", [P, SLOTS, 4 * NB], F32, base)
        high = place("high", [P, SLOTS, 4 * NB], F32R, base + 32 * KB)
        rest = place("rest", [P, SLOTS, 4 * NB], F32R, base + 64 * KB)
        x = place("x", [P, TT, D], F32, base + 96 * KB)
        y = place("y", [P, TT, D], F32, base + 104 * KB)
        xt_high = place("xt_high", [P, KC, S], F32R, base + 112 * KB)
        xt_rest = place("xt_rest", [P, KC, S], F32R, base + 120 * KB)
        junk_x = place("junk_x", [P, TT, D], F32, base + 112 * KB)
        gains = place("gains", [P, GSLOTS, D], F32, base + 128 * KB)
        at = base + 140 * KB
        small = {}
        for name, shape, dt in (
            ("ident", [P, P], F32), ("identb", [P, P], BF16), ("causal", [P, P], BF16),
            ("levelmask", [P, 8, P], U8), ("starts", [P, S], BF16),
            ("sums", [P, TT * len(NORMS)], F32), ("roots", [P, TT * len(NORMS)], F32),
            ("recips", [P, TT * len(NORMS)], F32), ("moments", [P, TT, 12], F32),
            ("meanvar", [P, TT, 2], F32), ("eps", [P, 2], F32), ("lbl", [P, 2, HH], F32),
            ("lb", [P, 4, HH], F32), ("flb", [P, HH], F32), ("negmax", [P, HH, 2], F32),
            ("expsum", [P, HH, 2], F32), ("crossref", [P, HALF], F32), ("convw", [P, FC, 3], F32),
            ("convb", [P, FC], F32), ("pscale", [P, 4], F32)):
            small[name] = place(name, shape, dt, at)
            at = -(-marks[name][1] // 32) * 32
        ident, identb, causal = small["ident"], small["identb"], small["causal"]
        levelmask, scanstart = small["levelmask"], small["starts"]
        sums, roots, recips = small["sums"], small["roots"], small["recips"]
        moments, meanvar, eps = small["moments"], small["meanvar"], small["eps"]
        area = at

        ht_high = place("ht_high", [P, FC, S], F32R, area)
        ht_rest = place("ht_rest", [P, FC, S], F32R, area + 22 * KB)
        gv = place("gv", [P, 2, TT, NB], F32, area + 44 * KB)
        conv = place("conv", [P, 2, 2, S], F32, area + 52 * KB)
        convs = place("convs", [P, 2, S], F32, area + 56 * KB)
        act_ = place("act", [P, 2, TT, 256], F32, area + 44 * KB)
        hid = place("hid", [P, 2, TT, 256], F32, area + 48 * KB)

        rq = place("rq", [P, TT, NB], F32, area)
        rk = place("rk", [P, TT, NB], F32, area + 4 * KB)
        rv = place("rv", [P, TT, NB], F32, area + 8 * KB)
        rg = place("rg", [P, TT, NB], F32, area + 12 * KB)
        rp = place("rp", [P, TT, NB], F32, area + 16 * KB)
        ra = place("ra", [P, TT, NB], F32, area + 20 * KB)
        pooly = place("pooly", [P, RH, S], F32, area + 20 * KB)
        rqT = place("rqT", [P, RH, S], F32, area + 24 * KB)
        rkT = place("rkT", [P, RH, S], F32, area + 28 * KB)
        rsc = place("rsc", [P, RH, 384], F32, area + 32 * KB)
        decay = place("decay", [P, RH, 384], F32, area + 38 * KB)
        window = place("window", [P, TT, RH, S], F32, area + 44 * KB)
        ropec = place("ropec", [P, TT, P], F32, area + 52 * KB)
        ropes = place("ropes", [P, TT, P], F32, area + 53 * KB)
        wpool = place("wpool", [P, RH, P], F32, area + 54 * KB)
        pooled = place("pooled", [P, RH, S], F32, area + 56 * KB)
        rout = place("rout", [P, TT, NB], F32, area)
        rsq = place("rsq", [P, TT, NB], F32, area + 4 * KB)

        hq = place("hq", [P, HH, S], F32, area)
        hk = place("hk", [P, HH, S], F32, area + 8 * KB)
        hb = place("hb", [P, HH, S], F32, area + 16 * KB)
        he = place("he", [P, HALF, S], F32, area + 24 * KB)
        hqk = place("hqk", [P, HALF, S], F32, area + 28 * KB)
        ha = place("ha", [P, HALF, 384], F32, area + 32 * KB)
        hi_ = place("hi", [P, TT, D], F32, area + 38 * KB)
        fqT = place("fqT", [P, HH, S], F32, area + 46 * KB)
        fkT = place("fkT", [P, HH, S], F32, area + 54 * KB)
        stage = place("stage", [P, 2, TT, NB], F32, base + 104 * KB)
        hg = place("hg", [P, TT, D], F32, base + 104 * KB)
        ho = place("ho", [P, 2, TT, NB], F32, area)
        fv = place("fv", [P, TT, D], F32, area + 16 * KB)
        gate = [place("gate0", [P, TT, D], F32, area + 8 * KB),
                place("gate1", [P, TT, D], F32, area + 24 * KB)]
        fp = place("fp", [P, 2, 384], F32, area + 32 * KB)
        fpT = place("fpT", [P, 2, 384], F32, area + 35 * KB)
        fo = place("fo", [P, HH, TT, P], F32, area + 46 * KB)
        levels32 = place("levels32", [P, 8, P], F32, area + 54 * KB)
        wf_raw = place("wf_raw", [P, KC, HH], F32, area + 62 * KB)
        wf_high = place("wf_high", [P, KC, HH], F32R, area + 62 * KB + 256)
        wf_rest = place("wf_rest", [P, KC, HH], F32R, area + 62 * KB + 512)
        flog = place("flog", [P, TT, HH], F32, area + 62 * KB + 768)
        flabs = place("flabs", [P, TT, HH], F32, area + 62 * KB + 832)
        flmin = place("flmin", [P, TT, HH], F32, area + 62 * KB + 896)
        fcum = place("fcum", [HH, S], F32, area + 63 * KB)
        fones = place("fones", [HH, S], F32, area + 38 * KB)
        junk_h = place("junk_h", [P, TT, D], F32, area + 38 * KB)

        junk_m = place("junk_m", [P, TT, D], F32, area + 16 * KB)
        mem = place("mem", [P, TT, D], F32, area)
        mt_high = place("mt_high", [P, KC, S], F32R, area + 8 * KB)
        mt_rest = place("mt_rest", [P, KC, S], F32R, area + 16 * KB)
        mkT = place("mkT", [P, KC, S], F32, area + 24 * KB)
        mv = place("mv", [P, TT, D], F32, area + 32 * KB)
        mstage = place("mstage", [P, TT, D], F32, area + 40 * KB)
        mqT = place("mqT", [P, KC, S], F32, area + 48 * KB)
        mo = place("mo", [P, TT, D], F32, area + 40 * KB)
        mp = place("mp", [P, TT, S], F32, area + 56 * KB)
        mpT = place("mpT", [P, 2, TT, S], F32, area + 58 * KB)

        ps = ctx.enter_context(nc.psum_tensor("ps", [P, 8, NB], F32))
        pair_of = [ps[:, 2 * n:2 * n + 2, :] for n in range(2)]
        tile_of = [ps[:, 0:4, :].rearrange("p (n t) c -> p n t c", t=TT)[:, :, tt, :] for tt in range(TT)]

        unit_landed = [sem(f"unit_landed{n}") for n in range(SLOTS)]
        unit_high, unit_rest, unit_used = sem("unit_high"), sem("unit_rest"), sem("unit_used")
        pair_taken = [sem(f"pair_taken{n}") for n in range(2)]
        aux_done = sem("aux_done")
        aux_taken = [None] * 4 + [sem(f"aux_taken{n}") for n in range(4, 8)]
        group_high = sem("group_high")
        gain_landed = [sem(f"gain_landed{n}") for n in range(GSLOTS)]
        x_landed, consts1_landed, consts2_landed = sem("x_landed"), sem("consts1_landed"), sem("consts2_landed")
        mem_landed, out_stored, levels_landed = sem("mem_landed"), sem("out_stored"), sem("levels_landed")
        eps_ready = sem("eps_ready")
        roots_ready = sem("roots_ready")
        x_ready = sem("x_ready")
        normed = sem("normed")
        CONSTS1, CONSTS2 = 10, 4

        ROOT_ORDER = ("ret", "ln1", "ln2", "ffn1_pre", "ffn1_post", "mix_pre", "hg", "mem_kv", "mix_post",
                      "mem_pre", "mem_post", "ffn2_pre", "ffn2_post")
        root_count = {name: n + 1 for n, name in enumerate(ROOT_ORDER)}
        x_count = {name: TT * (n + 1) for n, name in
                   enumerate(("ln1", "ln2", "ffn1_post", "mix_post", "mem_post", "ffn2_post"))}
        normed_count = {name: TT * (n + 1) for n, name in
                        enumerate(("ffn1_pre", "mix_pre", "mem_pre", "ffn2_pre"))}

        def gain_free(name):
            if name.startswith("ln"):
                return x_ready, x_count[name[:3]]
            if name in normed_count:
                return normed, normed_count[name]
            if name in x_count:
                return x_ready, x_count[name]
            if name == "hg_norm":
                return sem("oa_ready"), TT
            if name == "mem_kv":
                return sem("mem_normed"), TT
            j = 15 if name == "gate0" else 17
            return pair_taken[j % 2], PAIR["win2", j][1] + 1

        def taken(name, j):
            n, used = PAIR[name, j]
            return n, used + 1

        def filled(name, j):
            if dict(BLOCKS)[name]:
                return UNIT[name] + 2 * j + 2
            return UNIT[name] + FB

        block = ctx.enter_context(nc.Block())

        @block.sync
        def _(sync):
            sync.dma_start(small["ident"][:, :], dram["c_ident"]).then_inc(x_landed, 16)
            sync.dma_start(x[:, :, :], dram["x"].rearrange("(t p) c -> p t c", p=P)).then_inc(x_landed, 16)

            def load(u, parts):
                slot = u % SLOTS
                if u >= SLOTS:
                    sync.wait_ge(unit_rest, u - SLOTS + 1)
                for dst, src in parts(raw[:, slot, :]):
                    sync.dma_start(dst, src).then_inc(unit_landed[slot], 16)

            def load_block(u, w, c0):
                wv = w.rearrange("(k p) n -> p k n", p=P)
                for half in range(2):
                    k = 4 * half
                    load(u + half, lambda d: [(d.rearrange("p (k n) -> p k n", k=4)[:, n:n + 2, :],
                                               wv[:, k + n:k + n + 2, c0:c0 + NB]) for n in (0, 2)])

            def load_up(u, w, j):
                wv = w.rearrange("(k p) n -> p k n", p=P)
                for half in range(2):
                    k = 4 * half
                    load(u + half, lambda d: [(d.rearrange("p (k g n) -> p k g n", k=4, g=2)[:, :, g, :],
                                               wv[:, k:k + 4, g * FF + 256 * j:g * FF + 256 * j + 256])
                                              for g in range(2)])

            def load_down(u, w, i):
                wv = w.rearrange("(k p) n -> p k n", p=P)
                load(u, lambda d: [(d[:, k * D:(k + 1) * D], wv[:, 2 * i + k, :]) for k in range(2)])

            for name, k in BLOCKS:
                w = dram[{"win1": "w_in", "wout1": "w_out", "up1": "w_up", "down1": "w_down",
                          "upA": "ffn1_w_in_2", "downA": "ffn1_w_down_2", "win2": "w_in_2",
                          "brA": "w_branch_a_2", "brB": "w_branch_b_2", "wout2": "w_out_2",
                          "mkv": "w_mkv_2", "mq": "w_mq_2", "mo": "w_mo_2", "upB": "ffn2_w_in_2",
                          "downB": "ffn2_w_down_2"}[name]]
                for j in range(k or FB):
                    if not k:
                        load_down(UNIT[name] + j, w, j)
                    elif name.startswith("up"):
                        load_up(UNIT[name] + 2 * j, w, j)
                    else:
                        load_block(UNIT[name] + 2 * j, w, WIN2[j][1] if name == "win2" else j * NB)
            for tt in range(TT):
                sync.wait_ge(x_ready, x_count["ffn2_post"] - TT + tt + 1)
                sync.dma_start(out_dram[tt * P:(tt + 1) * P, :], x[:, tt, :]).then_inc(out_stored, 16)
            sync.wait_ge(out_stored, 16 * TT)

        @block.gpsimd
        def _(pool):
            for name, src in (("convw", "conv_w"), ("convb", "conv_b"), ("pscale", "pool_scale")):
                pool.dma_start(small[name][:], dram[src]).then_inc(consts1_landed, 16)
            for t, src in ((decay, "c_decay"), (window, "c_window"), (ropec, "c_ropec"), (ropes, "c_ropes")):
                pool.dma_start(t[:], dram[src]).then_inc(consts1_landed, 16)
            pool.dma_start(wpool[:, :, :], dram["w_pool"].rearrange("g c d -> c g d")).then_inc(consts1_landed, 16)
            pool.dma_start(small["causal"][:, :], dram["c_causal"]).then_inc(consts1_landed, 16)
            pool.dma_start(small["starts"][:, :], dram["c_starts"]).then_inc(consts1_landed, 16)
            pool.dma_start(small["lbl"][:, :, :], dram["hg_lb_logits_2"]).then_inc(consts2_landed, 16)
            pool.dma_start(small["flb"][:, :], dram["fox_f_bias_2"].partition_broadcast(P)).then_inc(consts2_landed, 16)
            pool.dma_start(wf_raw[:, :, :], dram["w_in_2"].rearrange("(k p) n -> p k n", p=P)
                           [:, :, FLOGIT:FLOGIT + HH]).then_inc(consts2_landed, 16)
            pool.dma_start(identb[:, :], dram["c_identb"]).then_inc(consts2_landed, 16)
            for n, name in enumerate(GAINS):
                if n >= GSLOTS:
                    pool.wait_ge(*gain_free(GAINS[n - GSLOTS]))
                if name == "hg_norm":
                    pool.dma_start(levels32[:, :, :], dram["c_levels"]).then_inc(levels_landed, 16)
                if name == "mem_kv":
                    pool.wait_ge(aux_done, AUX["oa", 3][0] + 1)
                    pool.dma_start(mem[:, :, :], dram["mem_2"].rearrange("(t p) c -> p t c", p=P))\
                        .then_inc(mem_landed, 16)
                pool.dma_start(gains[:, n % GSLOTS, :], dram["gain_" + name].partition_broadcast(P))\
                    .then_inc(gain_landed[n % GSLOTS], 16)

        @block.tensor
        def _(pe):
            done = [0]

            def unit(u, products, wait=None):
                slot = u % SLOTS
                pe.wait_ge(unit_rest, u + 1)
                for sh, sr, c, out, first, last in products:
                    wh, wr = high[:, slot, c:c + NB], rest[:, slot, c:c + NB]
                    pe.matmul(out, sh, wh, start=first, stop=False)
                    pe.matmul(out, sh, wr, start=False, stop=False)
                    mm = pe.matmul(out, sr, wh, start=False, stop=last)
                mm.then_inc(unit_used, 1)

            def half_block(name, j, half, th=xt_high, tr=xt_rest):
                n, used = PAIR[name, j]
                if used and half == 0:
                    pe.wait_ge(pair_taken[n], used)
                unit(UNIT[name] + 2 * j + half,
                     [(th[:, kc, tt * P:(tt + 1) * P], tr[:, kc, tt * P:(tt + 1) * P], (kc % 4) * NB,
                       pair_of[n][:, tt, :], kc == 0, kc == KC - 1)
                      for kc in range(4 * half, 4 * half + 4) for tt in range(TT)])

            def full_block(name, j, th=xt_high, tr=xt_rest):
                half_block(name, j, 0, th, tr)
                half_block(name, j, 1, th, tr)

            def down(name, i):
                if i == 0:
                    for n in range(2):
                        pe.wait_ge(pair_taken[n], PAIR[name, n][1])
                unit(UNIT[name] + i,
                     [(ht_high[:, kc, tt * P:(tt + 1) * P], ht_rest[:, kc, tt * P:(tt + 1) * P],
                       (kc % 2) * 2 * NB + n * NB, pair_of[n][:, tt, :], kc == 0, kc == FC - 1)
                      for kc in (2 * i, 2 * i + 1) for tt in range(TT) for n in range(2)])

            def aux(key):
                n, bank, used = AUX[key]
                assert n == done[0], (key, n, done[0])
                done[0] += 1
                if used:
                    pe.wait_ge(aux_taken[bank], used)
                return ps[:, bank, :]

            def wait_taken(*keys):
                for key in keys:
                    _, bank, used = AUX[key]
                    pe.wait_ge(aux_taken[bank], used + 1)

            def transposes(key, sources, then=None):
                out = aux(key)
                for n, src in enumerate(sources):
                    mm = pe.transpose(out[:, n * P:(n + 1) * P], src, ident[:, :])
                mm.then_inc(aux_done, 1)

            def token_groups(name, src, wait, kq=2, order=None):
                for g in range(TT * kq):
                    tt, q = divmod(g, kq)
                    wait(tt, q)
                    transposes((name, g), [src(tt, 4 * q + c) for c in range(4)])

            def from_x(tt, c):
                return x[:, tt, c * P:(c + 1) * P]

            def from_y(tt, c):
                return y[:, tt, c * P:(c + 1) * P]

            def head_pairs(name, src, g):
                transposes((name, g), [src[:, tt, c * P:(c + 1) * P]
                                       for c in (2 * (g % 2), 2 * (g % 2) + 1) for tt in range(TT)])

            pe.wait_ge(x_landed, 32)
            token_groups("x", from_x, lambda tt, q: None)
            wait_taken(*(("x", g) for g in range(4)))
            full_block("win1", 0)
            full_block("win1", 1)
            full_block("win1", 2)
            pe.wait_ge(sem("rope_done"), 1)
            for g in range(2):
                head_pairs("rTq", rq, g)
            full_block("win1", 3)
            pe.wait_ge(sem("rope_done"), 2)
            for g in range(2):
                head_pairs("rTk", rk, g)
            full_block("win1", 4)
            wait_taken(("rTq", 0), ("rTq", 1), ("rTk", 0), ("rTk", 1))
            for h in range(RH):
                out = aux(("rscore", h))
                pe.matmul(out[:, 0:S], rkT[:, h, 0:P], rqT[:, h, :], start=True, stop=True)
                pe.matmul(out[:, S:S + P], rkT[:, h, P:S], rqT[:, h, P:S], start=True, stop=True)\
                    .then_inc(aux_done, 1)
            pe.wait_ge(pair_taken[0], taken("win1", 4)[1])
            pe.wait_ge(consts1_landed, 16 * CONSTS1)
            for g in range(2):
                out = aux(("poolT", g))
                for c in range(2):
                    for tt in range(TT):
                        mm = pe.matmul(out[:, c * S:(c + 1) * S], rp[:, tt, (2 * g + c) * P:(2 * g + c + 1) * P],
                                       window[:, tt, 2 * g + c, :], start=(tt == 0), stop=(tt == TT - 1))
                mm.then_inc(aux_done, 1)
            wait_taken(*(("rscore", h) for h in range(RH)))
            for tt in range(TT):
                out = aux(("rout", tt))
                for h in range(RH):
                    o = out[:, h * P:(h + 1) * P]
                    v = [rv[:, t, h * P:(h + 1) * P] for t in range(TT)]
                    if tt == 0:
                        mm = pe.matmul(o, rsc[:, h, 0:P], v[0], start=True, stop=True)
                    else:
                        pe.matmul(o, rsc[:, h, P:S], v[0], start=True, stop=False)
                        mm = pe.matmul(o, rsc[:, h, S:S + P], v[1], start=False, stop=True)
                mm.then_inc(aux_done, 1)
            wait_taken(("poolT", 0), ("poolT", 1))
            for g in range(2):
                out = aux(("pooly", g))
                for c in range(2):
                    mm = pe.matmul(out[:, c * S:(c + 1) * S], wpool[:, 2 * g + c, :], pooled[:, 2 * g + c, :],
                                   start=True, stop=True)
                mm.then_inc(aux_done, 1)
            for tt in range(TT):
                pe.wait_ge(sem("ret_ready"), tt + 1)
                transposes(("mixr", tt), [rout[:, tt, c * P:(c + 1) * P] for c in range(4)])
            wait_taken(("mixr", 0), ("mixr", 1))
            pe.wait_ge(sem("pool_rest"), 2)
            full_block("wout1", 0)
            full_block("wout1", 1)

            token_groups("x1", from_x, lambda tt, q: pe.wait_ge(x_ready, x_count["ln1"] - TT + tt + 1))
            wait_taken(*(("x1", g) for g in range(4)))

            def conv_transposes(j):
                pe.wait_ge(pair_taken[j % 2], taken("up1", j)[1])
                for key, off in ((("convg", j), 256), (("convv", j), 0)):
                    transposes(key, [gv[:, j % 2, tt, off + c * P:off + (c + 1) * P]
                                     for c in range(2) for tt in range(TT)])

            for j in range(FB):
                full_block("up1", j)
                if j:
                    conv_transposes(j - 1)
            conv_transposes(FB - 1)
            for i in range(FB):
                pe.wait_ge(sem("ffn_rest"), min(i + 1, FB))
                down("down1", i)

            def ffn(u_name, d_name, h_name, base_count):
                for j in range(FB):
                    full_block(u_name, j)
                    if j:
                        hidden_transposes(u_name, h_name, j - 1)
                for i in range(FB):
                    if i == 2:
                        hidden_transposes(u_name, h_name, FB - 1)
                    wait_taken((h_name, i))
                    down(d_name, i)

            def hidden_transposes(u_name, h_name, j):
                n, count = taken(u_name, j)
                pe.wait_ge(pair_taken[n], count)
                transposes((h_name, j), [hid[:, j % 2, tt, c * P:(c + 1) * P]
                                         for c in range(2) for tt in range(TT)])

            def from_normed(name, key, stage_name):
                token_groups(key, from_y, lambda tt, q:
                             pe.wait_ge(normed, normed_count[stage_name] - TT + tt + 1))

            from_normed("", "f1", "ffn1_pre")
            wait_taken(*(("f1", g) for g in range(4)))
            ffn("upA", "downA", "hA", 0)

            from_normed("", "m2", "mix_pre")
            wait_taken(*(("m2", g) for g in range(4)))
            out = aux(("flog", 0))
            pe.wait_ge(sem("wf_rest"), 1)
            for tt in range(TT):
                for kc in range(KC):
                    xh, xr = xt_high[:, kc, tt * P:(tt + 1) * P], xt_rest[:, kc, tt * P:(tt + 1) * P]
                    o = out[:, tt * HH:(tt + 1) * HH]
                    pe.matmul(o, xh, wf_high[:, kc, :], start=(kc == 0), stop=False)
                    pe.matmul(o, xh, wf_rest[:, kc, :], start=False, stop=False)
                    mm = pe.matmul(o, xr, wf_high[:, kc, :], start=False, stop=(kc == KC - 1))
            mm.then_inc(aux_done, 1)

            def levels(n):
                hf, lv = HG_STEPS[n]
                pe.wait_ge(sem("level_ready"), n + 1)
                for g in range(1 if lv == 128 else 2):
                    out = aux(("lv", hf, lv, g))
                    for c in range(4):
                        o = out[:, c * P:(c + 1) * P]
                        h, tt = (c, None) if lv == 128 else (2 * g + c // 2, c % 2)
                        t = slice(0, P) if tt is None else slice(tt * P, (tt + 1) * P)
                        if lv == 0:
                            mm = pe.matmul(o, hk[:, HALF * hf + h, t], hq[:, HALF * hf + h, t], start=True, stop=True)
                        else:
                            mm = pe.matmul(o, hqk[:, h, t], hqk[:, h, P:S] if tt is None else hqk[:, h, t],
                                           start=True, stop=True)
                    mm.then_inc(aux_done, 1)
                if lv == 128:
                    wait_taken(*(("lv", hf, v, g) for v in (0, *LEVELS) for g in range(2)), ("lv", hf, 128, 0))
                    for tt in range(TT):
                        out = aux(("hgo", hf, tt))
                        for h in range(HALF):
                            o = out[:, h * P:(h + 1) * P]
                            c = slice((HALF * hf + h) * P, (HALF * hf + h + 1) * P)
                            if tt == 0:
                                mm = pe.matmul(o, ha[:, h, 0:P], hi_[:, 0, c], start=True, stop=True)
                            else:
                                pe.matmul(o, ha[:, h, P:S], hi_[:, 0, c], start=True, stop=False)
                                mm = pe.matmul(o, ha[:, h, S:S + P], hi_[:, 1, c], start=False, stop=True)
                        mm.then_inc(aux_done, 1)

            def fox(n):
                if n < HH:
                    out = aux(("fs", n))
                    for tt in range(TT):
                        o = out[:, 0:P] if tt == 0 else out[:, P:P + S]
                        w = (tt + 1) * P
                        pe.matmul(o, fqT[:, n, tt * P:(tt + 1) * P], fkT[:, n, 0:w], start=True, stop=False)
                        pe.matmul(o, ident[0:HH, n:n + 1].to_broadcast([HH, P]), fcum[:, 0:w], start=False, stop=False)
                        mm = pe.matmul(o[:, w - P:w], identb[:, :], causal[:, :], start=False, stop=True)
                    mm.then_inc(aux_done, 1)
                if 1 <= n < HH + 1:
                    h = n - 1
                    wait_taken(("fs", h))
                    transposes(("fp", h), [fp[:, h % 2, c * P:(c + 1) * P] for c in range(3)])
                if n >= 2:
                    h = n - 2
                    wait_taken(("fp", h))
                    out = aux(("fo", h))
                    v = [fv[:, t, h * P:(h + 1) * P] for t in range(TT)]
                    pe.matmul(out[:, 0:P], fpT[:, h % 2, 0:P], v[0], start=True, stop=True)
                    pe.matmul(out[:, P:S], fpT[:, h % 2, P:S], v[0], start=True, stop=False)
                    pe.matmul(out[:, P:S], fpT[:, h % 2, S:S + P], v[1], start=False, stop=True).then_inc(aux_done, 1)

            for u in range(36):
                j, half = divmod(u, 2)
                half_block("win2", j, half)
                if u == 1:
                    out = aux(("flog", 1))
                    pe.wait_ge(sem("flog_ready"), 1)
                    for tt in range(TT):
                        mm = pe.transpose(out[0:HH, tt * P:(tt + 1) * P], flog[:, tt, :], ident[:, :])
                    mm.then_inc(aux_done, 1)
                if u >= 2 and half == 0 and WIN2[j - 1][0] in ("f", "q", "fq", "fk"):
                    n, count = taken("win2", j - 1)
                    pe.wait_ge(pair_taken[n], count)
                    for g in range(2):
                        transposes((WIN2[j - 1][0] + "T", 2 * ((j - 1) % 2) + g),
                                   [stage[:, (j - 1) % 2, tt, c * P:(c + 1) * P]
                                    for c in (2 * g, 2 * g + 1) for tt in range(TT)])
                for n in HG_SLOT[u]:
                    levels(n)
                for n in FOX_SLOT[u]:
                    if n == 0:
                        wait_taken(*((w + "T", g) for w in ("fq", "fk") for g in range(4)))
                        wait_taken(("flog", 1))
                        pe.wait_ge(consts1_landed, 16 * CONSTS1)
                        pe.wait_ge(consts2_landed, 16 * CONSTS2)
                    fox(n)

            token_groups("oa", lambda tt, c: ho[:, c // 4, tt, (c % 4) * P:(c % 4 + 1) * P],
                         lambda tt, q: pe.wait_ge(sem("oa_ready"), tt + 1))
            wait_taken(*(("oa", g) for g in range(4)))
            full_block("brA", 0)
            full_block("brA", 1)
            wait_taken(("fo", HH - 1), ("fo", HH - 2))
            token_groups("ob", lambda tt, c: fo[:, c, tt, :], lambda tt, q: None)
            wait_taken(*(("ob", g) for g in range(4)))
            full_block("brB", 0)
            full_block("brB", 1)
            token_groups("memn", lambda tt, c: mem[:, tt, c * P:(c + 1) * P],
                         lambda tt, q: pe.wait_ge(sem("mem_normed"), tt + 1))
            token_groups("y2", from_y, lambda tt, q: pe.wait_ge(sem("y2_ready"), 2))
            wait_taken(*(("y2", g) for g in range(4)))
            full_block("wout2", 0)
            full_block("wout2", 1)

            wait_taken(*(("memn", g) for g in range(4)))
            for j in range(4):
                full_block("mkv", j, mt_high, mt_rest)
            from_normed("", "mpre", "mem_pre")
            pe.wait_ge(pair_taken[0], taken("mkv", 0)[1])
            pe.wait_ge(pair_taken[1], taken("mkv", 1)[1])
            for g in range(4):
                transposes(("mkT", g), [mstage[:, tt, c * P:(c + 1) * P] for c in (2 * g, 2 * g + 1) for tt in range(TT)])
            wait_taken(*(("mpre", g) for g in range(4)))
            full_block("mq", 0)
            full_block("mq", 1)
            for g in range(4):
                if g % 2 == 0:
                    n, count = taken("mq", g // 2)
                    pe.wait_ge(pair_taken[n], count)
                transposes(("mqT", g), [mstage[:, tt, c * P:(c + 1) * P] for c in (2 * g, 2 * g + 1) for tt in range(TT)])
            wait_taken(*((w, g) for w in ("mkT", "mqT") for g in range(4)))
            for n in range(MH + 2):
                if n < MH:
                    out = aux(("ms", n))
                    for tt in range(TT):
                        for c in range(2):
                            mm = pe.matmul(out[:, tt * S:(tt + 1) * S], mqT[:, 2 * n + c, tt * P:(tt + 1) * P],
                                           mkT[:, 2 * n + c, :], start=(c == 0), stop=(c == 1))
                    mm.then_inc(aux_done, 1)
                if 1 <= n < MH + 1:
                    wait_taken(("ms", n - 1))
                    transposes(("mp", n - 1), [mp[:, tt, t * P:(t + 1) * P] for t in range(TT) for tt in range(TT)])
                if n >= 2:
                    h = n - 2
                    wait_taken(("mp", h))
                    out = aux(("mo", h))
                    for tt in range(TT):
                        for t in range(TT):
                            mm = pe.matmul(out[:, tt * S:(tt + 1) * S], mpT[:, h % 2, t, tt * P:(tt + 1) * P],
                                           mv[:, t, h * S:(h + 1) * S], start=(t == 0), stop=(t == TT - 1))
                    mm.then_inc(aux_done, 1)
            wait_taken(*(("mo", h) for h in range(MH)))
            token_groups("om", lambda tt, c: mo[:, tt, c * P:(c + 1) * P], lambda tt, q: None)
            wait_taken(*(("om", g) for g in range(4)))
            full_block("mo", 0)
            full_block("mo", 1)
            from_normed("", "f2", "ffn2_pre")
            wait_taken(*(("f2", g) for g in range(4)))
            ffn("upB", "downB", "hB", 0)
            assert done[0] == len(AUX)

        @block.scalar
        def _(act):
            split = [0]
            mine = sem("scalar_steps")
            steps = [0]

            def step(ins):
                ins.then_inc(mine, 1)
                steps[0] += 1

            def settle():
                act.wait_ge(mine, steps[0])

            def split_to(n):
                while split[0] < min(n, UNIT["end"]):
                    u = split[0]
                    act.wait_ge(unit_landed[u % SLOTS], 32 * (u // SLOTS + 1))
                    if u >= SLOTS:
                        act.wait_ge(unit_used, u - SLOTS + 1)
                    act.activation(high[:, u % SLOTS, :], raw[:, u % SLOTS, :], ACT.Copy).then_inc(unit_high, 1)
                    split[0] += 1

            def aux(key):
                n, bank, _ = AUX[key]
                act.wait_ge(aux_done, n + 1)
                return ps[:, bank, :]

            def group_to_high(key, dst):
                src = aux(key)
                if len(dst.shape) == 3:
                    src = src.rearrange("p (k n) -> p k n", k=dst.shape[1])
                act.activation(dst, src, ACT.Copy).then_inc(group_high, 1)

            def token_groups(name, dst=xt_high, kq=2):
                for g in range(TT * kq):
                    tt, q = divmod(g, kq)
                    group_to_high((name, g), dst[:, 4 * q:4 * q + 4, tt * P:(tt + 1) * P])

            def take(key, dst, **how):
                _, bank, _ = AUX[key]
                src = aux(key)[:, 0:int(np.prod(dst.shape[1:]))]
                if len(dst.shape) == 3:
                    src = src.rearrange("p (k n) -> p k n", k=dst.shape[1])
                act.activation(dst, src, ACT.Copy, **how).then_inc(aux_taken[bank], 1)

            def block_values(name, j):
                act.wait_ge(unit_used, filled(name, j))
                return pair_of[taken(name, j)[0]]

            def take_block(name, j, dst, func=ACT.Copy, **how):
                n, _ = taken(name, j)
                act.activation(dst, block_values(name, j), func, **how).then_inc(pair_taken[n], 1)

            def roots_of(src, name, width, eps_col):
                act.activation(roots[:, NS[name]:NS[name] + width], src, ACT.Sqrt, bias=eps[:, eps_col:eps_col + 1])\
                    .then_inc(roots_ready, 1)

            def roots_of_sums(name):
                settle()
                roots_of(sums[:, NS[name]:NS[name] + TT], name, TT, 1)

            def square_tiles(name, src, junk):
                for tt in range(TT):
                    step(act.activation(junk(tt), src(tt), ACT.Square, scale=D ** -0.5,
                                        accum_out=sums[:, NS[name] + tt:NS[name] + tt + 1]))
                roots_of_sums(name)

            def pre_norm(name, after):
                def src(tt):
                    act.wait_ge(x_ready, x_count[after] - TT + tt + 1)
                    return x[:, tt, :]
                square_tiles(name, src, lambda tt: junk_x[:, tt, :])

            def post_norm(name, count):
                act.wait_ge(unit_used, count)
                square_tiles(name, lambda tt: tile_of[tt], lambda tt: junk_x[:, tt, :].rearrange("p (n c) -> p n c", n=2))

            act.wait_ge(eps_ready, 2)
            token_groups("x")
            split_to(UNIT["win1"] + 4)
            split_to(UNIT["win1"] + 6)
            take_block("win1", 2, rv[:, :, :])
            for g in range(2):
                take(("rTq", g), rqT[:, 2 * g:2 * g + 2, :])
            split_to(UNIT["win1"] + 8)
            take_block("win1", 3, rg[:, :, :], ACT.Silu)
            for g in range(2):
                take(("rTk", g), rkT[:, 2 * g:2 * g + 2, :])
            split_to(UNIT["win1"] + 10)
            take_block("win1", 4, rp[:, :, :])
            for g in range(2):
                take(("poolT", g), pooled[:, 2 * g:2 * g + 2, :])
            for tt in range(TT):
                act.activation(rsq[:, tt, :], aux(("rout", tt)), ACT.Square, scale=P ** -0.5).then_inc(sem("ret_squares"), 1)
            act.wait_ge(sem("ret_sums"), TT)
            roots_of(sums[:, 0:TT * RH], "ret0", TT * RH, 1)
            for g in range(2):
                out = aux(("pooly", g))
                for c in range(2):
                    ins = act.activation(pooly[:, 2 * g + c, :], out[:, c * S:(c + 1) * S], ACT.Copy,
                                         scale=small["pscale"][:, 2 * g + c:2 * g + c + 1])
                    if c == 0:
                        step(ins)
                ins.then_inc(aux_taken[AUX["pooly", g][1]], 1)
                settle()
                act.wait_ge(aux_taken[AUX["pooly", g][1]], AUX["pooly", g][2] + 1)
                act.activation(xt_high[:, 4 + 2 * g:6 + 2 * g, :], pooly[:, 2 * g:2 * g + 2, :], ACT.Copy)\
                    .then_inc(sem("pool_high"), 1)
            split_to(UNIT["wout1"] + 4)
            for tt in range(TT):
                group_to_high(("mixr", tt), xt_high[:, 0:4, tt * P:(tt + 1) * P])
            act.wait_ge(sem("var_ready"), TT)
            roots_of(meanvar[:, :, 1], "ln1", TT, 0)
            split_to(UNIT["up1"] + 2)
            token_groups("x1")

            def conv_values(j):
                out = aux(("convg", j))
                if j >= 2:
                    act.wait_ge(sem("ffn_rest"), j - 1)
                for c in range(2):
                    f = 2 * j + c
                    act.activation(conv[:, j % 2, c, :], out[:, c * S:(c + 1) * S], ACT.Identity,
                                   scale=small["convw"][:, f, 2:3], bias=small["convb"][:, f:f + 1])\
                        .then_inc(sem("conv_last"), 1)
                act.wait_ge(aux_taken[6], AUX["convg", j][2] + 1)
                act.activation(convs[:, :, :], conv[:, j % 2, :, :], ACT.Silu).then_inc(sem("conv_silu"), 1)
                act.wait_ge(aux_taken[7], AUX["convv", j][2] + 1)
                act.activation(ht_high[:, 2 * j:2 * j + 2, :], conv[:, j % 2, :, :], ACT.Copy)\
                    .then_inc(sem("ffn_high"), 1)

            act.wait_ge(consts1_landed, 16 * CONSTS1)
            for j in range(FB):
                split_to(UNIT["up1"] + 2 * j + 4)
                take_block("up1", j, gv[:, j % 2, :, :])
                if j:
                    conv_values(j - 1)
            conv_values(FB - 1)
            split_to(UNIT["upA"] + 2)
            act.wait_ge(sem("var_ready"), 2 * TT)
            roots_of(meanvar[:, :, 1], "ln2", TT, 0)

            def ffn(u_name, d_name, h_name, post, following):
                def hidden_high(j):
                    group_to_high((h_name, j), ht_high[:, 2 * j:2 * j + 2, :])

                for j in range(FB):
                    split_to(UNIT[u_name] + 2 * j + 4)
                    act.activation(act_[:, j % 2, :, :], block_values(u_name, j)[:, :, 0:256], ACT.Silu)\
                        .then_inc(sem("silu_done"), 1)
                    if j:
                        hidden_high(j - 1)
                split_to(UNIT[d_name] + 4)
                hidden_high(FB - 1)
                split_to(UNIT[following] + 2)
                post_norm(post, UNIT[following])

            pre_norm("ffn1_pre", "ln2")
            token_groups("f1")
            ffn("upA", "downA", "hA", "ffn1_post", "win2")

            pre_norm("mix_pre", "ffn1_post")
            token_groups("m2")
            act.wait_ge(consts2_landed, 16 * CONSTS2)
            act.activation(wf_high[:, :, :], wf_raw[:, :, :], ACT.Copy).then_inc(sem("wf_high"), 1)
            act.wait_ge(sem("lb_shifted"), 1)
            act.activation(small["lbl"][:, :, :], small["lbl"][:, :, :], ACT.Exp).then_inc(sem("lb_exp"), 1)
            act.wait_ge(aux_taken[AUX["flog", 0][1]], AUX["flog", 0][2] + 1)
            step(act.activation(flabs[:, :, :], flog[:, :, :], ACT.Abs))
            settle()
            act.activation(flabs[:, :, :], flabs[:, :, :], ACT.Exp, scale=-1.0).then_inc(sem("flog_exp"), 1)
            act.wait_ge(sem("flog_exp"), 1)
            act.activation(flabs[:, :, :], flabs[:, :, :], ACT.Ln, bias=1.0).then_inc(sem("flog_ln"), 1)

            def level_exp(n):
                hf, lv = HG_STEPS[n]
                hs = slice(HALF * hf, HALF * hf + HALF)
                if lv == 0:
                    return
                act.wait_ge(sem("level_diff"), n - hf)
                if lv == 128:
                    act.activation(he[:, :, 0:P], he[:, :, 0:P], ACT.Exp, scale=-1.0)
                    act.activation(he[:, :, P:P + CHUNK], hb[:, hs, P:P + CHUNK], ACT.Exp)
                    ins = act.activation(he[:, :, P + CHUNK:S], he[:, :, P + CHUNK:S], ACT.Exp)
                else:
                    e = he[:, :, :].rearrange("p h (n t) -> p (h n) t", t=2 * lv)
                    b = hb[:, hs, :].rearrange("p h (n t) -> p (h n) t", t=2 * lv) if lv == 64 else e
                    act.activation(e[:, :, 0:lv], e[:, :, 0:lv], ACT.Exp, scale=-1.0)
                    ins = act.activation(e[:, :, lv:2 * lv], b[:, :, lv:2 * lv], ACT.Exp)
                ins.then_inc(sem("level_exp"), 1)

            for u in range(36):
                split_to(UNIT["win2"] + u + 3)
                j, half = divmod(u, 2)
                what = WIN2[j][0]
                c = slice((j % 2) * NB, (j % 2 + 1) * NB)
                if half:
                    if what == "f":
                        take_block("win2", j, stage[:, j % 2, :, :], ACT.Sigmoid)
                    elif what == "q":
                        act.activation(stage[:, j % 2, :, :], block_values("win2", j), ACT.Tanh, scale=0.5)\
                            .then_inc(sem("q_tanh"), 1)
                    elif what == "g":
                        act.activation(hg[:, :, c], block_values("win2", j), ACT.Tanh, scale=0.5)\
                            .then_inc(sem("g_tanh"), 1)
                    elif what == "fq":
                        take_block("win2", j, stage[:, j % 2, :, :], scale=P ** -0.5)
                    elif what == "fk":
                        take_block("win2", j, stage[:, j % 2, :, :])
                    elif what == "i":
                        take_block("win2", j, hi_[:, :, c])
                    elif what == "fv":
                        take_block("win2", j, fv[:, :, c])
                    else:
                        g = j - 14
                        act.wait_ge(pair_taken[j % 2], taken("win2", j)[1])
                        d = gate[g // 2][:, :, c]
                        act.activation(d, d, ACT.Tanh, scale=0.5).then_inc(sem("gate_tanh"), 1)
                elif j and WIN2[j - 1][0] in ("f", "q", "fq", "fk"):
                    w, k = WIN2[j - 1][0], (j - 1) % 2
                    if w == "f":
                        act.wait_ge(sem("f_ready"), k + 1)
                        act.activation(hb[:, HALF * k:HALF * k + HALF, :], he[:, :, :], ACT.Ln).then_inc(sem("f_log"), 1)
                    else:
                        for g in range(2):
                            dst = {"q": hq, "fq": fqT, "fk": fkT}[w][:, HALF * k + 2 * g:HALF * k + 2 * g + 2, :]
                            take((w + "T", 2 * k + g), dst, **({"scale": 0.5} if w == "q" else {}))
                for n in HG_SLOT[u]:
                    if n == 0:
                        level_exp(1)
                    elif n + 1 < len(HG_STEPS):
                        level_exp(n + 1)
                    if n == len(HG_STEPS) - 1:
                        def src(tt):
                            for key in (("hgo", a, b) for a in range(2) for b in range(TT)):
                                act.wait_ge(aux_taken[AUX[key][1]], AUX[key][2] + 1)
                            return ho[:, :, tt, :]
                        square_tiles("hg", src, lambda tt: junk_h[:, tt, :].rearrange("p (n c) -> p n c", n=2))
                for n in FOX_SLOT[u]:
                    if 1 <= n < HH + 1:
                        take(("fp", n - 1), fpT[:, (n - 1) % 2, :])
                    if n < HH:
                        act.wait_ge(sem("fox_max"), TT * (n + 1))
                        _, bank, _ = AUX["fs", n]
                        out = aux(("fs", n))
                        for tt in range(TT):
                            c0, c1 = (0, P) if tt == 0 else (P, P + S)
                            ins = act.activation(fp[:, n % 2, c0:c1], out[:, c0:c1], ACT.Exp,
                                                 bias=small["negmax"][:, n, tt:tt + 1],
                                                 accum_out=small["expsum"][:, n, tt:tt + 1])
                        ins.then_inc(aux_taken[bank], 1)

            split_to(UNIT["brA"] + 2)
            token_groups("oa")
            split_to(UNIT["brA"] + 4)
            split_to(UNIT["brB"] + 2)
            act.wait_ge(unit_used, filled("brA", 1))
            token_groups("ob")
            act.wait_ge(mem_landed, 16)
            square_tiles("mem_kv", lambda tt: mem[:, tt, :], lambda tt: junk_m[:, tt, :])
            split_to(UNIT["brB"] + 4)
            split_to(UNIT["wout2"] + 2)
            act.wait_ge(sem("y2_ready"), 2)
            token_groups("memn", mt_high)
            token_groups("y2")
            split_to(UNIT["wout2"] + 4)
            split_to(UNIT["mkv"] + 2)
            post_norm("mix_post", filled("wout2", 1))
            split_to(UNIT["mkv"] + 4)
            pre_norm("mem_pre", "mix_post")
            for j in range(4):
                split_to(UNIT["mkv"] + 2 * j + 4)
                c = slice((j % 2) * NB, (j % 2 + 1) * NB)
                take_block("mkv", j, (mstage if j < 2 else mv)[:, :, c])
            token_groups("mpre")
            for g in range(4):
                take(("mkT", g), mkT[:, 2 * g:2 * g + 2, :])
            split_to(UNIT["mq"] + 4)
            for j in range(2):
                c = slice(j * NB, (j + 1) * NB)
                take_block("mq", j, mstage[:, :, c], scale=S ** -0.5)
            split_to(UNIT["mo"] + 2)
            for g in range(4):
                take(("mqT", g), mqT[:, 2 * g:2 * g + 2, :])
            for n in range(MH + 2):
                if 1 <= n < MH + 1:
                    take(("mp", n - 1), mpT[:, (n - 1) % 2, :, :].rearrange("p t s -> p (t s)"))
                if n < MH:
                    act.wait_ge(sem("mem_max"), n + 1)
                    _, bank, _ = AUX["ms", n]
                    out = aux(("ms", n))
                    for tt in range(TT):
                        ins = act.activation(mp[:, tt, :], out[:, tt * S:(tt + 1) * S], ACT.Exp,
                                             bias=small["negmax"][:, n, tt:tt + 1],
                                             accum_out=small["expsum"][:, n, tt:tt + 1])
                    ins.then_inc(aux_taken[bank], 1)
            split_to(UNIT["mo"] + 4)
            token_groups("om")
            split_to(UNIT["upB"] + 2)
            post_norm("mem_post", filled("mo", 1))
            pre_norm("ffn2_pre", "mem_post")
            token_groups("f2")
            ffn("upB", "downB", "hB", "ffn2_post", "end")
            assert split[0] == UNIT["end"]

        @block.vector
        def _(vec):
            split, groups = [0], [0]
            mine = sem("vector_steps")
            steps = [0]

            def step(ins):
                ins.then_inc(mine, 1)
                steps[0] += 1

            def settle():
                vec.wait_ge(mine, steps[0])

            def split_to(n):
                while split[0] < min(n, UNIT["end"]):
                    u = split[0]
                    slot = u % SLOTS
                    vec.wait_ge(unit_high, u + 1)
                    vec.tensor_tensor(rest[:, slot, :], raw[:, slot, :], high[:, slot, :].bitcast(F32),
                                      ALU.subtract).then_inc(unit_rest, 1)
                    split[0] += 1

            def aux(key):
                n, bank, _ = AUX[key]
                vec.wait_ge(aux_done, n + 1)
                return ps[:, bank, :]

            def took(key, ins):
                ins.then_inc(aux_taken[AUX[key][1]], 1)

            def group_to_rest(key, dst_high, dst_rest):
                _, bank, _ = AUX[key]
                groups[0] += 1
                vec.wait_ge(group_high, groups[0])
                src = ps[:, bank, :].rearrange("p (k n) -> p k n", k=dst_high.shape[1])
                vec.tensor_tensor(dst_rest, src, dst_high.bitcast(F32), ALU.subtract).then_inc(aux_taken[bank], 1)

            def token_groups(name, th=xt_high, tr=xt_rest, kq=2):
                for g in range(TT * kq):
                    tt, q = divmod(g, kq)
                    at = (slice(None), slice(4 * q, 4 * q + 4), slice(tt * P, (tt + 1) * P))
                    group_to_rest((name, g), th[at], tr[at])

            def block_values(name, j):
                vec.wait_ge(unit_used, filled(name, j))
                return pair_of[taken(name, j)[0]]

            def took_block(name, j, ins):
                ins.then_inc(pair_taken[taken(name, j)[0]], 1)

            def gain(name):
                n = GAINS.index(name)
                vec.wait_ge(gain_landed[n % GSLOTS], 16 * (n // GSLOTS + 1))
                return gains[:, n % GSLOTS, :]

            def recip_roots(name, cols, first=None):
                vec.wait_ge(roots_ready, root_count[name])
                n = NS[first or name]
                step(vec.reciprocal(recips[:, n:n + cols], roots[:, n:n + cols]))
                settle()
                return [recips[:, n + c:n + c + 1] for c in range(cols)]

            def halves(ap):
                return ap.rearrange("p (n c) -> p n c", n=2)

            def pre_norm(name):
                r, g = recip_roots(name, TT), gain(name)
                for tt in range(TT):
                    vec.scalar_tensor_tensor(y[:, tt, :], x[:, tt, :], r[tt], g, ALU.mult, ALU.mult).then_inc(normed, 1)

            def post_norm(name, scale):
                r, g = recip_roots(name, TT), gain(name)
                for tt in range(TT):
                    for n in range(2):
                        c = slice(n * NB, (n + 1) * NB)
                        ins = vec.scalar_tensor_tensor(y[:, tt, c], pair_of[n][:, tt, :], r[tt], g[:, c], ALU.mult, ALU.mult)
                        if tt == 0:
                            step(ins)
                        else:
                            ins.then_inc(pair_taken[n], 1)
                    if tt == 0:
                        settle()
                    else:
                        for n in range(2):
                            vec.wait_ge(pair_taken[n], PAIR[post_block[name], n][1] + 1)
                    vec.scalar_tensor_tensor(x[:, tt, :], y[:, tt, :], scale, x[:, tt, :], ALU.mult, ALU.add)\
                        .then_inc(x_ready, 1)

            def attention_out(scores, key, dst, width, h):
                _, bank, used = AUX[scores]
                vec.wait_ge(aux_taken[bank], used + 1)
                sums_ = small["expsum"][:, h, :]
                step(vec.reciprocal(sums_, sums_))
                settle()
                src = aux(key)[:, 0:TT * width].rearrange("p (t c) -> p t c", t=TT)
                took(key, vec.tensor_tensor(dst, src, sums_.unsqueeze(2).to_broadcast([P, TT, width]), ALU.mult))

            post_block = {"ffn1_post": "downA", "mix_post": "wout2", "mem_post": "mo", "ffn2_post": "downB"}

            def layer_norm(name, block, count):
                vec.wait_ge(unit_used, count)
                for n in range(2):
                    c = slice(n * NB, (n + 1) * NB)
                    vec.scalar_tensor_tensor(y[:, :, c], x[:, :, c], ALPHA, pair_of[n], ALU.mult, ALU.add)\
                        .then_inc(pair_taken[n], 1)
                for n in range(2):
                    vec.wait_ge(pair_taken[n], PAIR[block, n][1] + 1)
                for tt in range(TT):
                    for n in range(2):
                        step(vec.bn_stats(moments[:, tt, 6 * n:6 * n + 6], y[:, tt, n * NB:(n + 1) * NB]))
                settle()
                for tt in range(TT):
                    vec.bn_aggr(meanvar[:, tt, :], moments[:, tt, :].rearrange("p (n c) -> p n c", n=2)).then_inc(sem("var_ready"), 1)
                r, g, b = recip_roots(name, TT), gain(name + "_g"), gain(name + "_b")
                for tt in range(TT):
                    step(vec.tensor_scalar(y[:, tt, :], y[:, tt, :], meanvar[:, tt, 0:1], r[tt], ALU.subtract, ALU.mult))
                    settle()
                    step(vec.tensor_tensor(y[:, tt, :], y[:, tt, :], g, ALU.mult))
                    settle()
                    vec.tensor_tensor(x[:, tt, :], y[:, tt, :], b, ALU.add).then_inc(x_ready, 1)

            vec.memset(eps[:, 0:1], LN_EPS).then_inc(eps_ready, 1)
            vec.memset(eps[:, 1:2], RMS_EPS).then_inc(eps_ready, 1)

            token_groups("x")
            split_to(UNIT["win1"] + 4)
            vec.wait_ge(consts1_landed, 16 * CONSTS1)

            def rope(j, dst):
                src = block_values("win1", j)
                for tt in range(TT):
                    s4 = src[:, tt, :].rearrange("p (h d) -> p h d", h=RH)
                    c4 = ropec[:, tt, :].unsqueeze(1).to_broadcast([P, RH, P])
                    a4 = ra[:, tt, :].rearrange("p (h d) -> p h d", h=RH)
                    d4 = dst[:, tt, :].rearrange("p (h d) -> p h d", h=RH)
                    step(vec.tensor_tensor(d4, s4, c4, ALU.mult))
                    for half in range(2):
                        o = slice(half * 64, half * 64 + 64)
                        i = slice(64 - half * 64, 128 - half * 64)
                        sn = ropes[:, tt, o].unsqueeze(1).to_broadcast([P, RH, 64])
                        ins = vec.tensor_tensor(a4[:, :, o], s4[:, :, i], sn, ALU.mult)
                        if tt == 1 and half == 1:
                            took_block("win1", j, ins)
                        else:
                            step(ins)
                settle()
                vec.wait_ge(pair_taken[j % 2], taken("win1", j)[1])
                vec.tensor_tensor(dst[:, :, :], dst[:, :, :], ra[:, :, :], ALU.add).then_inc(sem("rope_done"), 1)

            rope(0, rq)
            split_to(UNIT["win1"] + 6)
            vec.wait_ge(sem("rope_done"), 1)
            rope(1, rk)
            split_to(UNIT["win1"] + 10)
            for h in range(RH):
                src = aux(("rscore", h))
                took(("rscore", h), vec.tensor_tensor(rsc[:, h, :], src[:, 0:384], decay[:, h, :], ALU.mult))
            for tt in range(TT):
                vec.wait_ge(sem("ret_squares"), tt + 1)
                vec.tensor_reduce(sums[:, RH * tt:RH * tt + RH], rsq[:, tt, :].rearrange("p (h d) -> p h d", h=RH),
                                  AX_X, ALU.add).then_inc(sem("ret_sums"), 1)
            recip_roots("ret", TT * RH, "ret0")
            for tt in range(TT):
                r4 = recips[:, RH * tt:RH * tt + RH].unsqueeze(2).to_broadcast([P, RH, P])
                o = rout[:, tt, :]
                took(("rout", tt), vec.tensor_tensor(o.rearrange("p (h d) -> p h d", h=RH),
                                                     aux(("rout", tt)).rearrange("p (h d) -> p h d", h=RH), r4, ALU.mult))
                vec.wait_ge(aux_taken[AUX["rout", tt][1]], AUX["rout", tt][2] + 1)
                vec.wait_ge(pair_taken[1], taken("win1", 3)[1])
                vec.tensor_tensor(o, o, rg[:, tt, :], ALU.mult).then_inc(sem("ret_ready"), 1)
            for g in range(2):
                vec.wait_ge(sem("pool_high"), g + 1)
                k = slice(4 + 2 * g, 6 + 2 * g)
                vec.tensor_tensor(xt_rest[:, k, :], pooly[:, 2 * g:2 * g + 2, :], xt_high[:, k, :].bitcast(F32),
                                  ALU.subtract).then_inc(sem("pool_rest"), 1)
            split_to(UNIT["wout1"] + 4)
            for tt in range(TT):
                at = (slice(None), slice(0, 4), slice(tt * P, (tt + 1) * P))
                group_to_rest(("mixr", tt), xt_high[at], xt_rest[at])
            layer_norm("ln1", "wout1", filled("wout1", 1))
            split_to(UNIT["up1"] + 2)
            token_groups("x1")

            def conv_values(j):
                src = aux(("convg", j)).rearrange("p (c s) -> p c s", c=2)
                val = ps[:, 7, :].rearrange("p (c s) -> p c s", c=2)
                vec.wait_ge(sem("conv_last"), 2 * j + 2)
                for tap, back in ((1, 1), (0, 2)):
                    for c in range(2):
                        d = conv[:, j % 2, c, back:S]
                        ins = vec.scalar_tensor_tensor(d, src[:, c, 0:S - back], small["convw"][:, 2 * j + c, tap:tap + 1],
                                                       d, ALU.mult, ALU.add)
                        if (tap, c) == (0, 1):
                            took(("convg", j), ins)
                        else:
                            step(ins)
                    if tap == 1:
                        settle()
                vec.wait_ge(sem("conv_silu"), j + 1)
                aux(("convv", j))
                took(("convv", j), vec.tensor_tensor(conv[:, j % 2, :, :], convs[:, :, :], val, ALU.mult))
                vec.wait_ge(sem("ffn_high"), j + 1)
                k = slice(2 * j, 2 * j + 2)
                vec.tensor_tensor(ht_rest[:, k, :], conv[:, j % 2, :, :], ht_high[:, k, :].bitcast(F32),
                                  ALU.subtract).then_inc(sem("ffn_rest"), 1)

            for j in range(FB):
                split_to(UNIT["up1"] + 2 * j + 4)
                if j:
                    conv_values(j - 1)
            conv_values(FB - 1)
            split_to(UNIT["upA"] + 2)
            layer_norm("ln2", "down1", UNIT["upA"])

            def ffn(u_name, d_name, h_name, post, following):
                def hidden_rest(j):
                    k = slice(2 * j, 2 * j + 2)
                    group_to_rest((h_name, j), ht_high[:, k, :], ht_rest[:, k, :])

                for j in range(FB):
                    split_to(UNIT[u_name] + 2 * j + 4)
                    silus[0] += 1
                    vec.wait_ge(sem("silu_done"), silus[0])
                    took_block(u_name, j, vec.tensor_tensor(hid[:, j % 2, :, :], act_[:, j % 2, :, :],
                                                            block_values(u_name, j)[:, :, 256:NB], ALU.mult))
                    if j:
                        hidden_rest(j - 1)
                split_to(UNIT[d_name] + 4)
                hidden_rest(FB - 1)
                split_to(UNIT[following] + 2)
                post_norm(post, 0.5)

            silus = [0]
            pre_norm("ffn1_pre")
            token_groups("f1")
            ffn("upA", "downA", "hA", "ffn1_post", "win2")

            pre_norm("mix_pre")
            token_groups("m2")
            vec.wait_ge(sem("wf_high"), 1)
            vec.tensor_tensor(wf_rest[:, :, :], wf_raw[:, :, :], wf_high[:, :, :].bitcast(F32), ALU.subtract)\
                .then_inc(sem("wf_rest"), 1)
            lbl, lb = small["lbl"], small["lb"]
            vec.wait_ge(consts2_landed, 16 * CONSTS2)
            step(vec.tensor_tensor(lb[:, 2, :], lbl[:, 0, :], lbl[:, 1, :], ALU.max))
            settle()
            vec.tensor_tensor(lbl[:, :, :], lbl[:, :, :], lb[:, 2, :].unsqueeze(1).to_broadcast([P, 2, HH]),
                              ALU.subtract).then_inc(sem("lb_shifted"), 1)
            vec.wait_ge(sem("lb_exp"), 1)
            step(vec.tensor_tensor(lb[:, 2, :], lbl[:, 0, :], lbl[:, 1, :], ALU.add))
            settle()
            step(vec.reciprocal(lb[:, 3, :], lb[:, 2, :]))
            settle()
            for n in range(2):
                step(vec.tensor_tensor(lb[:, n, :], lbl[:, n, :], lb[:, 3, :], ALU.mult))
            settle()
            step(vec.memset(fones[:, :], 1.0))
            z = aux(("flog", 0))[:, 0:TT * HH].rearrange("p (t h) -> p t h", t=TT)
            took(("flog", 0), vec.tensor_tensor(flog[:, :, :], z, small["flb"][:, :].unsqueeze(1).to_broadcast([P, TT, HH]), ALU.add))
            vec.wait_ge(aux_taken[AUX["flog", 0][1]], AUX["flog", 0][2] + 1)
            step(vec.tensor_scalar(flmin[:, :, :], flog[:, :, :], 0.0, None, ALU.min))
            settle()
            vec.wait_ge(sem("flog_ln"), 1)
            vec.tensor_tensor(flog[:, :, :], flabs[:, :, :], flmin[:, :, :], ALU.subtract).then_inc(sem("flog_ready"), 1)

            vec.wait_ge(levels_landed, 16)
            step(vec.tensor_copy(levelmask[:, :, :], levels32[:, :, :]))
            settle()

            def diff(n):
                hf, lv = HG_STEPS[n]
                b = hb[:, HALF * hf:HALF * hf + HALF, :]
                vec.wait_ge(sem("level_ready"), n)
                if lv == 128:
                    cr = small["crossref"]
                    step(vec.tensor_tensor(cr[:, :], b[:, :, CHUNK - 1], b[:, :, P - 1], ALU.add))
                    settle()
                    last = lambda ap: ap.unsqueeze(2).to_broadcast([P, HALF, CHUNK])
                    vec.tensor_tensor(he[:, :, 0:CHUNK], b[:, :, 0:CHUNK], last(cr[:, :]), ALU.subtract)
                    vec.tensor_tensor(he[:, :, CHUNK:P], b[:, :, CHUNK:P], last(b[:, :, P - 1]), ALU.subtract)
                    ins = vec.tensor_tensor(he[:, :, P + CHUNK:S], b[:, :, P + CHUNK:S], last(b[:, :, P + CHUNK - 1]), ALU.add)
                else:
                    e = he[:, :, :].rearrange("p h (n t) -> p (h n) t", t=2 * lv)
                    b = b.rearrange("p h (n t) -> p (h n) t", t=2 * lv)
                    w = lv if lv == 64 else 2 * lv
                    ref = b[:, :, lv - 1].unsqueeze(2).to_broadcast([P, HALF * S // (2 * lv), w])
                    ins = vec.tensor_tensor(e[:, :, 0:w], b[:, :, 0:w], ref, ALU.subtract)
                ins.then_inc(sem("level_diff"), 1)

            def apply_decays(n):
                hf, lv = HG_STEPS[n]
                hs = slice(HALF * hf, HALF * hf + HALF)
                vec.wait_ge(sem("level_exp"), n - hf)
                t = P if lv == 128 else lv
                view = lambda ap: ap.rearrange("p h (n t) -> p (h n) t", t=2 * t)
                e, o, q, k = view(he[:, :, :]), view(hqk[:, :, :]), view(hq[:, hs, :]), view(hk[:, hs, :])
                step(vec.tensor_tensor(o[:, :, 0:t], e[:, :, 0:t], k[:, :, 0:t], ALU.mult))
                settle()
                vec.tensor_tensor(o[:, :, t:2 * t], e[:, :, t:2 * t], q[:, :, t:2 * t], ALU.mult)\
                    .then_inc(sem("level_ready"), 1)

            def place_scores(n):
                hf, lv = HG_STEPS[n]
                if lv == 128:
                    src = aux(("lv", hf, lv, 0)).rearrange("p (h t) -> p h t", h=HALF)
                    took(("lv", hf, lv, 0), vec.tensor_copy(ha[:, :, P:S], src))
                    return
                m = levelmask[:, (0, *LEVELS).index(lv), :].unsqueeze(1).to_broadcast([P, TT, P])
                for g in range(2):
                    src = aux(("lv", hf, lv, g))
                    for c in range(2):
                        d = ha[:, 2 * g + c, :].rearrange("p (t s) -> p t s", t=3)[:, 0:3:2, :]
                        ins = vec.copy_predicated(d, m, src[:, 2 * c * P:2 * (c + 1) * P].rearrange("p (t s) -> p t s", t=2))
                        if c == 0:
                            step(ins)
                    took(("lv", hf, lv, g), ins)
                settle()

            for u in range(36):
                split_to(UNIT["win2"] + u + 3)
                j, half = divmod(u, 2)
                what = WIN2[j][0]
                c = slice((j % 2) * NB, (j % 2 + 1) * NB)
                if half:
                    if what == "q":
                        vec.wait_ge(sem("q_tanh"), j % 2 + 1)
                        d = stage[:, j % 2, :, :]
                        took_block("win2", j, vec.scalar_tensor_tensor(d, d, 1.0, block_values("win2", j), ALU.add, ALU.mult))
                    elif what == "g":
                        vec.wait_ge(sem("g_tanh"), j % 2 + 1)
                        d = hg[:, :, c]
                        took_block("win2", j, vec.scalar_tensor_tensor(d, d, 1.0, block_values("win2", j), ALU.add, ALU.mult))
                    elif what == "gate":
                        g = (j - 14) // 2
                        bias = gain(f"gate{g}")[:, c].unsqueeze(1).to_broadcast([P, TT, NB])
                        took_block("win2", j, vec.tensor_tensor(gate[g][:, :, c], block_values("win2", j), bias, ALU.add))
                elif j and WIN2[j - 1][0] == "f":
                    k = (j - 1) % 2
                    if k:
                        vec.wait_ge(sem("f_log"), k)
                    for g in range(2):
                        src = aux(("fT", 2 * k + g))
                        for c in range(2):
                            h = HALF * k + 2 * g + c
                            ins = vec.tensor_scalar(he[:, 2 * g + c, :], src[:, c * S:(c + 1) * S], lb[:, 1, h:h + 1],
                                                    lb[:, 0, h:h + 1], ALU.mult, ALU.add)
                            if c == 0:
                                step(ins)
                        took(("fT", 2 * k + g), ins)
                    settle()
                    for g in range(2):
                        vec.wait_ge(aux_taken[AUX["fT", 2 * k + g][1]], AUX["fT", 2 * k + g][2] + 1)
                    vec.tensor_scalar(hk[:, HALF * k:HALF * k + HALF, :], he[:, :, :], -1.0, 1.0, ALU.mult, ALU.add)\
                        .then_inc(sem("f_ready"), 1)
                    vec.wait_ge(sem("f_log"), k + 1)
                    for h in range(HALF * k, HALF * k + HALF):
                        step(vec.tensor_tensor_scan(hb[:, h, :], scanstart[:, :], hb[:, h, :], 0.0, ALU.mult, ALU.add))
                    settle()
                if u == 1:
                    src = ps[0:HH, AUX["flog", 1][1], 0:S]
                    aux(("flog", 1))
                    took(("flog", 1), vec.tensor_tensor_scan(fcum[:, :], fones[:, :], src, 0.0, ALU.mult, ALU.add))
                for n in HG_SLOT[u]:
                    hf, lv = HG_STEPS[n]
                    if lv == 0:
                        for g in range(2):
                            key = ("qT", 2 * hf + g)
                            vec.wait_ge(aux_taken[AUX[key][1]], AUX[key][2] + 1)
                        if hf:
                            vec.wait_ge(aux_done, AUX["hgo", 0, 1][0] + 1)
                        vec.memset(ha[:, :, :], 0.0).then_inc(sem("level_ready"), 1)
                    else:
                        apply_decays(n)
                    if n + 1 < len(HG_STEPS) and HG_STEPS[n + 1][1]:
                        diff(n + 1)
                    if lv == 0:
                        vec.wait_ge(sem("level_ready"), n + 1)
                    place_scores(n)
                    if lv == 128:
                        for tt in range(TT):
                            took(("hgo", hf, tt), vec.tensor_copy(ho[:, hf, tt, :], aux(("hgo", hf, tt))))
                if u == 24:
                    r = recip_roots("hg", TT)
                    n = NS["hg"]
                    step(vec.tensor_scalar(recips[:, n:n + TT], recips[:, n:n + TT], 0.5, None, ALU.mult))
                    settle()
                    g = gain("hg_norm")
                    for n in range(2):
                        vec.wait_ge(pair_taken[n], taken("win2", 10 + n)[1])
                    for tt in range(TT):
                        o = ho[:, :, tt, :]
                        step(vec.scalar_tensor_tensor(o, o, r[tt], halves(g), ALU.mult, ALU.mult))
                        settle()
                        vec.tensor_tensor(o, o, halves(hg[:, tt, :]), ALU.mult).then_inc(sem("oa_ready"), 1)
                for n in FOX_SLOT[u]:
                    if n < HH:
                        src = aux(("fs", n))
                        for tt in range(TT):
                            c0, c1 = (0, P) if tt == 0 else (P, P + S)
                            ins = vec.tensor_reduce(small["negmax"][:, n, tt:tt + 1], src[:, c0:c1], AX_X, ALU.max, negate=True)
                            ins.then_inc(sem("fox_max"), 1)
                    if n >= 2:
                        attention_out(("fs", n - 2), ("fo", n - 2), fo[:, n - 2, :, :], P, n - 2)

            split_to(UNIT["brA"] + 2)
            token_groups("oa")
            split_to(UNIT["brA"] + 4)
            split_to(UNIT["brB"] + 2)
            for g in range(2):
                vec.wait_ge(sem("gate_tanh"), 2 * g + 2)
                step(vec.tensor_scalar(gate[g][:, :, :], gate[g][:, :, :], 0.5, 0.5, ALU.mult, ALU.add))
            settle()
            for j in range(2):
                d = gate[0][:, :, j * NB:(j + 1) * NB]
                took_block("brA", j, vec.tensor_tensor(d, d, block_values("brA", j), ALU.mult))
            token_groups("ob")
            r, g = recip_roots("mem_kv", TT), gain("mem_kv")
            for tt in range(TT):
                vec.scalar_tensor_tensor(mem[:, tt, :], mem[:, tt, :], r[tt], g, ALU.mult, ALU.mult)\
                    .then_inc(sem("mem_normed"), 1)
            split_to(UNIT["brB"] + 4)
            split_to(UNIT["wout2"] + 2)
            for j in range(2):
                c = slice(j * NB, (j + 1) * NB)
                d = gate[1][:, :, c]
                took_block("brB", j, vec.tensor_tensor(d, d, block_values("brB", j), ALU.mult))
                vec.wait_ge(pair_taken[j], taken("brB", j)[1])
                vec.tensor_tensor(y[:, :, c], gate[0][:, :, c], d, ALU.add).then_inc(sem("y2_ready"), 1)
            token_groups("memn", mt_high, mt_rest)
            token_groups("y2")
            split_to(UNIT["wout2"] + 4)
            split_to(UNIT["mkv"] + 2)
            post_norm("mix_post", 1.0)
            split_to(UNIT["mkv"] + 4)
            pre_norm("mem_pre")

            split_to(UNIT["mkv"] + 10)
            token_groups("mpre")
            split_to(UNIT["mq"] + 4)
            split_to(UNIT["mo"] + 2)
            for n in range(MH + 2):
                if n < MH:
                    src = aux(("ms", n)).rearrange("p (t s) -> p t s", t=TT)
                    vec.tensor_reduce(small["negmax"][:, n, :], src, AX_X, ALU.max, negate=True).then_inc(sem("mem_max"), 1)
                if n >= 2:
                    attention_out(("ms", n - 2), ("mo", n - 2), mo[:, :, (n - 2) * S:(n - 1) * S], S, n - 2)
            split_to(UNIT["mo"] + 4)
            token_groups("om")
            split_to(UNIT["upB"] + 2)
            post_norm("mem_post", 1.0)
            pre_norm("ffn2_pre")
            token_groups("f2")
            ffn("upB", "downB", "hB", "ffn2_post", "end")
            assert split[0] == UNIT["end"]


def constants():
    f32 = np.float32
    tok = np.arange(S)
    out = {"c_ident": np.eye(P, dtype=f32), "c_identb": np.eye(P, dtype=f32).astype(np.dtype("bfloat16"))}
    causal = np.where(np.arange(P)[None, :] <= np.arange(P)[:, None], 0.0, NEG).astype(f32)
    out["c_causal"] = causal.astype(np.dtype("bfloat16"))
    starts = np.broadcast_to((tok % CHUNK != 0).astype(f32), (P, S))
    out["c_starts"] = np.ascontiguousarray(starts).astype(np.dtype("bfloat16"))
    s, t = np.arange(P)[:, None], np.arange(P)[None, :]
    levels = [s == t] + [(s // (2 * n) == t // (2 * n)) & (s % (2 * n) < n) & (t % (2 * n) >= n) for n in LEVELS]
    out["c_levels"] = np.ascontiguousarray(np.stack(levels, 1).astype(f32))
    gamma = 1.0 - 2.0 ** (-5.0 - np.arange(RH))
    i, j = tok[None, :], tok[:, None]
    seen = (i // CHUNK >= j // CHUNK)
    full = np.where(seen, gamma[:, None, None] ** np.abs(i - j), 0.0) * P ** -0.5
    decay = np.concatenate([full[:, 0:P, :], full[:, P:S, P:S]], axis=2)
    out["c_decay"] = np.ascontiguousarray(decay.transpose(1, 0, 2).astype(f32))
    win = []
    for w in (2, 4, 8, 16):
        m = ((j <= i) & (j > i - w)) / np.minimum(i + 1, w) - (i == j)
        win.append(m)
    win = np.stack(win).reshape(RH, TT, P, S).transpose(2, 1, 0, 3)
    out["c_window"] = np.ascontiguousarray(win.astype(f32))
    inv = (f32(10000.0) ** (-np.arange(0, P, 2, dtype=f32) / f32(P))).astype(f32)
    ang = (tok.astype(f32)[:, None] * inv[None, :]).astype(f32).astype(np.float64)
    cos, sin = np.cos(ang), np.sin(ang)
    for name, a, b in (("c_ropec", cos, cos), ("c_ropes", -sin, sin)):
        v = np.concatenate([a, b], axis=1).reshape(TT, P, P).transpose(1, 0, 2)
        out[name] = np.ascontiguousarray(v.astype(f32))
    return out


_VECTORS = {"ln1_g": "ln1_g", "ln1_b": "ln1_b", "ln2_g": "ln2_g", "ln2_b": "ln2_b",
            "ffn1_pre": "ffn1_pre_g_2", "ffn1_post": "ffn1_post_g_2", "mix_pre": "mix_pre_g_2",
            "hg_norm": "hg_norm_g_2", "mem_kv": "mem_kv_g_2", "mix_post": "mix_post_g_2",
            "mem_pre": "mem_pre_g_2", "mem_post": "mem_post_g_2", "ffn2_pre": "ffn2_pre_g_2",
            "ffn2_post": "ffn2_post_g_2"}
_WEIGHTS = ["w_in", "w_out", "w_up", "w_down", "ffn1_w_in_2", "ffn1_w_down_2", "w_in_2", "w_branch_a_2",
            "w_branch_b_2", "w_out_2", "w_mq_2", "w_mkv_2", "w_mo_2", "ffn2_w_in_2", "ffn2_w_down_2", "w_pool"]


def kernel(**inputs):
    import concourse.bacc as _bacc
    from concourse.bass_utils import run_bass_kernel_spmd as _run

    nc = _bacc.Bacc("TRN2", target_bir_lowering=False, num_devices=1)
    laid = {name: np.asarray(inputs[name])[0] for name in _WEIGHTS}
    laid["x"] = np.asarray(inputs["x"])[0]
    laid["mem_2"] = np.asarray(inputs["mem_2"])[0]
    for name, src in _VECTORS.items():
        laid["gain_" + name] = np.asarray(inputs[src])[0]
    bias = np.asarray(inputs["b_gate_2"])[0]
    laid["gain_gate0"], laid["gain_gate1"] = bias[:D], bias[D:]
    laid["fox_f_bias_2"] = np.asarray(inputs["fox_f_bias_2"])[0]
    laid["conv_w"] = np.asarray(inputs["conv_w"])[0].reshape(3, FC, P).transpose(2, 1, 0)
    laid["conv_b"] = np.asarray(inputs["conv_b"])[0].reshape(FC, P).T
    laid["pool_scale"] = np.asarray(inputs["pool_scale"])[0].reshape(RH, P).T
    laid["hg_lb_logits_2"] = np.asarray(inputs["hg_lb_logits_2"]).transpose(2, 0, 1)
    laid.update(constants())
    arrays, dram = {}, {}
    for name, a in laid.items():
        a = np.ascontiguousarray(a)
        arrays[f"in_{name}_dram"] = a
        dram[name] = nc.dram_tensor(f"in_{name}_dram", a.shape, mybir.dt.from_np(a.dtype), kind="ExternalInput").ap()
    out = nc.dram_tensor("out_0_dram", (S, D), F32, kind="ExternalOutput").ap()
    build(nc, dram, out)
    r = _run(nc, [arrays], core_ids=[0])
    return r.results[0]["out_0_dram"].reshape(1, S, D)
```

```python
from contextlib import ExitStack

import numpy as np

import concourse.bass as bass
from concourse import mybir

ALU = mybir.AluOpType
ACT = mybir.ActivationFunctionType
F32 = mybir.dt.float32
F32R = mybir.dt.float32r
BF16 = mybir.dt.bfloat16
U8 = mybir.dt.uint8
AX_X = mybir.AxisListType.X

P = 128
S = 256
TT = S // P
D = 1024
KC = D // P
NB = 512
RH = 4
FF = 2816
FC = FF // P
FB = FF // 256
CHUNK = 64
HH = 8
HALF = HH // 2
MH = 4
ALPHA = 2.0 ** 0.25
LN_EPS, RMS_EPS = 1e-5, 1e-6
SLOTS = 4
GSLOTS = 3
LEVELS = (1, 2, 4, 8, 16, 32, 64)
NEG = -1e30

GAINS = ("ln1_g", "ln1_b", "ln2_g", "ln2_b", "ffn1_pre", "ffn1_post", "mix_pre", "hg_norm", "gate0",
         "gate1", "mem_kv", "mix_post", "mem_pre", "mem_post", "ffn2_pre", "ffn2_post")
NORMS = ("ret0", "ret1", "ret2", "ret3", "ln1", "ln2", "ffn1_pre", "ffn1_post", "mix_pre", "hg",
         "mem_kv", "mix_post", "mem_pre", "mem_post", "ffn2_pre", "ffn2_post")
BLOCKS = (("win1", 5), ("wout1", 2), ("up1", FB), ("down1", 0), ("upA", FB), ("downA", 0),
          ("win2", 18), ("brA", 2), ("brB", 2), ("wout2", 2), ("mkv", 4), ("mq", 2), ("mo", 2),
          ("upB", FB), ("downB", 0))
WIN1 = (("q", 0), ("k", 512), ("v", 1024), ("p", 2048), ("g", 1536))
WIN2 = (("f", 1024), ("f", 1536), ("q", 0), ("q", 512), ("i", 2048), ("i", 2560),
        ("fq", 4096), ("fq", 4608), ("fk", 5120), ("fk", 5632), ("g", 3072), ("g", 3584),
        ("fv", 6144), ("fv", 6656), ("gate", 7176), ("gate", 7688), ("gate", 8200), ("gate", 8712))
FLOGIT = 7168
HG_STEPS = tuple((hf, lv) for hf in range(2) for lv in (0, *LEVELS, 128))
HG_SLOT = {u: [] for u in range(36)}
for _n, _step in enumerate(HG_STEPS):
    _hf, _k = divmod(_n, len(HG_STEPS) // 2)
    HG_SLOT[8 * (_hf + 1) + max(_k - 1, 0)].append(_n)
FOX_SLOT = {u: [] for u in range(36)}
for _n in range(HH + 2):
    FOX_SLOT[min(28 + _n, 35)].append(_n)


def unit_starts():
    out, n = {}, 0
    for name, k in BLOCKS:
        out[name] = n
        n += 2 * k if k else FB
    out["end"] = n
    return out


def pair_plan():
    out, used = {}, [0, 0]
    for name, k in BLOCKS:
        for j in range(k or 2):
            out[name, j] = (j % 2, used[j % 2])
            used[j % 2] += 1
    return out


def aux_plan():
    order, out, used = [], {}, [0] * 8

    def use(key, bank=None):
        n = len(order)
        bank = 4 + n % 4 if bank is None else bank
        order.append(key)
        out[key] = (n, bank, used[bank])
        used[bank] += 1

    def splits(name, n=4):
        for g in range(n):
            use((name, g))

    splits("x")
    for what in "qk":
        for g in range(2):
            use(("rT" + what, g))
    for h in range(RH):
        use(("rscore", h))
    for g in range(2):
        use(("poolT", g))
    for tt in range(TT):
        use(("rout", tt))
    for g in range(2):
        use(("pooly", g))
    splits("mixr", 2)
    splits("x1")
    for j in range(FB):
        use(("convg", j), 6)
        use(("convv", j), 7)
    splits("f1")
    for j in range(FB):
        use(("hA", j), 4 + j % 2)
    splits("m2")
    for u in range(36):
        j, last = u // 2, u % 2 == 1
        if u == 1:
            use(("flog", 0))
        if u == 3:
            use(("flog", 1))
        if u >= 2 and not last and WIN2[j - 1][0] in ("f", "q", "fq", "fk"):
            for g in range(2):
                use((WIN2[j - 1][0] + "T", 2 * ((j - 1) % 2) + g))
        for n in HG_SLOT[u]:
            hf, lv = HG_STEPS[n]
            for g in range(1 if lv == 128 else 2):
                use(("lv", hf, lv, g))
            if lv == 128:
                for tt in range(TT):
                    use(("hgo", hf, tt))
        for n in FOX_SLOT[u]:
            if n < HH:
                use(("fs", n))
            if 1 <= n < HH + 1:
                use(("fp", n - 1))
            if n >= 2:
                use(("fo", n - 2))
    splits("oa")
    splits("ob")
    splits("memn")
    splits("y2")
    splits("mpre")
    for what in ("mkT", "mqT"):
        for g in range(4):
            use((what, g))
    for n in range(MH + 2):
        if n < MH:
            use(("ms", n))
        if 1 <= n < MH + 1:
            use(("mp", n - 1))
        if n >= 2:
            use(("mo", n - 2))
    splits("om")
    splits("f2")
    for j in range(FB):
        use(("hB", j), 4 + j % 2)
    return out


HALVES = {"wout1": (1, 0)}
UNIT = unit_starts()
PAIR = pair_plan()
AUX = aux_plan()
NS = {name: TT * n for n, name in enumerate(NORMS)}


def build(nc, dram, out_dram):
    ctx = ExitStack()
    with ctx:
        nc_sem = {}

        def sem(name):
            if name not in nc_sem:
                nc_sem[name] = ctx.enter_context(nc.semaphore(name))
            return nc_sem[name]

        base = -(-nc.sbuf_base // 32) * 32
        top = nc.sbuf_top
        marks = {}

        def place(name, shape, dt, at):
            size = int(np.prod(shape[1:])) * {F32: 4, F32R: 4, BF16: 2, U8: 1}[dt]
            marks[name] = (at, at + size)
            assert base <= at and at + size <= top, (name, at, size, top)
            return nc.alloc_sbuf_tensor_at(name, shape, dt, offset=at)

        KB = 1024
        raw = place("raw", [P, SLOTS, 4 * NB], F32, base)
        high = place("high", [P, SLOTS, 4 * NB], F32R, base + 32 * KB)
        rest = place("rest", [P, SLOTS, 4 * NB], F32R, base + 64 * KB)
        x = place("x", [P, TT, D], F32, base + 96 * KB)
        y = place("y", [P, TT, D], F32, base + 104 * KB)
        xt_high = place("xt_high", [P, KC, S], F32R, base + 112 * KB)
        xt_rest = place("xt_rest", [P, KC, S], F32R, base + 120 * KB)
        gains = place("gains", [P, GSLOTS, D], F32, base + 128 * KB)
        at = base + 140 * KB
        small = {}
        for name, shape, dt in (
            ("ident", [P, P], F32), ("identb", [P, P], BF16), ("causal", [P, P], BF16),
            ("levelmask", [P, 8, P], U8), ("starts", [P, S], BF16),
            ("sums", [P, TT * len(NORMS)], F32), ("roots", [P, TT * len(NORMS)], F32),
            ("recips", [P, TT * len(NORMS)], F32), ("moments", [P, TT, 12], F32),
            ("meanvar", [P, TT, 2], F32), ("eps", [P, 2], F32), ("partsum", [P, 2], F32), ("lbl", [P, 2, HH], F32),
            ("lb", [P, 4, HH], F32), ("flb", [P, HH], F32), ("negmax", [P, HH, 2], F32),
            ("expsum", [P, HH, 2], F32), ("crossref", [P, HALF], F32), ("convw", [P, FC, 3], F32),
            ("convb", [P, FC], F32), ("pscale", [P, 4], F32)):
            small[name] = place(name, shape, dt, at)
            at = -(-marks[name][1] // 32) * 32
        ident, identb, causal = small["ident"], small["identb"], small["causal"]
        levelmask, scanstart = small["levelmask"], small["starts"]
        sums, roots, recips = small["sums"], small["roots"], small["recips"]
        moments, meanvar, eps = small["moments"], small["meanvar"], small["eps"]
        area = at

        junk_a = place("junk_a", [P, TT, D], F32, area)
        ht_high = place("ht_high", [P, FC, S], F32R, area)
        ht_rest = place("ht_rest", [P, FC, S], F32R, area + 22 * KB)
        gv = place("gv", [P, 2, TT, NB], F32, area + 44 * KB)
        conv = place("conv", [P, 2, 2, S], F32, area + 52 * KB)
        convs = place("convs", [P, 2, S], F32, area + 56 * KB)
        act_ = place("act", [P, 2, TT, 256], F32, area + 44 * KB)
        hid = place("hid", [P, 2, TT, 256], F32, area + 48 * KB)

        rq = place("rq", [P, TT, NB], F32, area)
        rk = place("rk", [P, TT, NB], F32, area + 4 * KB)
        rv = place("rv", [P, TT, NB], F32, area + 8 * KB)
        rg = place("rg", [P, TT, NB], F32, area + 12 * KB)
        rp = place("rp", [P, TT, NB], F32, area + 16 * KB)
        ra = place("ra", [P, TT, NB], F32, area + 20 * KB)
        pooly = place("pooly", [P, RH, S], F32, area + 20 * KB)
        rqT = place("rqT", [P, RH, S], F32, area + 24 * KB)
        rkT = place("rkT", [P, RH, S], F32, area + 28 * KB)
        rsc = place("rsc", [P, RH, 384], F32, area + 32 * KB)
        decay = place("decay", [P, RH, 384], F32, area + 38 * KB)
        window = place("window", [P, TT, RH, S], F32, area + 44 * KB)
        ropec = place("ropec", [P, TT, P], F32, area + 52 * KB)
        ropes = place("ropes", [P, TT, P], F32, area + 53 * KB)
        wpool = place("wpool", [P, RH, P], F32, area + 54 * KB)
        pooled = place("pooled", [P, RH, S], F32, area + 56 * KB)
        rout = place("rout", [P, TT, NB], F32, area)
        rsq = place("rsq", [P, TT, NB], F32, area + 4 * KB)

        hq = place("hq", [P, HH, S], F32, area)
        hk = place("hk", [P, HH, S], F32, area + 8 * KB)
        hb = place("hb", [P, HH, S], F32, area + 16 * KB)
        he = place("he", [P, HALF, S], F32, area + 24 * KB)
        hqk = place("hqk", [P, HALF, S], F32, area + 28 * KB)
        ha = place("ha", [P, HALF, 384], F32, area + 32 * KB)
        hi_ = place("hi", [P, TT, D], F32, area + 38 * KB)
        fqT = place("fqT", [P, HH, S], F32, area + 46 * KB)
        fkT = place("fkT", [P, HH, S], F32, area + 54 * KB)
        stage = place("stage", [P, 2, TT, NB], F32, base + 104 * KB)
        hg = place("hg", [P, TT, D], F32, base + 104 * KB)
        ho = place("ho", [P, 2, TT, NB], F32, area)
        fv = place("fv", [P, TT, D], F32, area + 16 * KB)
        gate = [place("gate0", [P, TT, D], F32, area + 8 * KB),
                place("gate1", [P, TT, D], F32, area + 24 * KB)]
        fp = place("fp", [P, 2, 384], F32, area + 32 * KB)
        fpT = place("fpT", [P, 2, 384], F32, area + 35 * KB)
        fo = place("fo", [P, HH, TT, P], F32, area + 46 * KB)
        levels32 = place("levels32", [P, 8, P], F32, area + 54 * KB)
        wf_raw = place("wf_raw", [P, KC, HH], F32, area + 62 * KB)
        wf_high = place("wf_high", [P, KC, HH], F32R, area + 62 * KB + 256)
        wf_rest = place("wf_rest", [P, KC, HH], F32R, area + 62 * KB + 512)
        flog = place("flog", [P, TT, HH], F32, area + 62 * KB + 768)
        flabs = place("flabs", [P, TT, HH], F32, area + 62 * KB + 832)
        flmin = place("flmin", [P, TT, HH], F32, area + 62 * KB + 896)
        fcum = place("fcum", [HH, S], F32, area + 63 * KB)
        fones = place("fones", [HH, S], F32, area + 38 * KB)
        junk_h = place("junk_h", [P, TT, D], F32, area + 38 * KB)

        junk_m = place("junk_m", [P, TT, D], F32, area + 16 * KB)
        mem = place("mem", [P, TT, D], F32, area)
        mt_high = place("mt_high", [P, KC, S], F32R, area + 8 * KB)
        mt_rest = place("mt_rest", [P, KC, S], F32R, area + 16 * KB)
        mkT = place("mkT", [P, KC, S], F32, area + 24 * KB)
        mv = place("mv", [P, TT, D], F32, area + 32 * KB)
        mstage = place("mstage", [P, TT, D], F32, area + 40 * KB)
        mqT = place("mqT", [P, KC, S], F32, area + 48 * KB)
        mo = place("mo", [P, TT, D], F32, area + 40 * KB)
        mp = place("mp", [P, TT, S], F32, area + 56 * KB)
        mpT = place("mpT", [P, 2, TT, S], F32, area + 58 * KB)

        ps = ctx.enter_context(nc.psum_tensor("ps", [P, 8, NB], F32))
        pair_of = [ps[:, 2 * n:2 * n + 2, :] for n in range(2)]

        unit_landed = [sem(f"unit_landed{n}") for n in range(SLOTS)]
        unit_high, unit_rest, unit_used = sem("unit_high"), sem("unit_rest"), sem("unit_used")
        pair_taken = [sem(f"pair_taken{n}") for n in range(2)]
        aux_done = sem("aux_done")
        aux_taken = [None] * 4 + [sem(f"aux_taken{n}") for n in range(4, 8)]
        group_high = sem("group_high")
        gain_landed = [sem(f"gain_landed{n}") for n in range(GSLOTS)]
        x_landed, consts1_landed, consts2_landed = sem("x_landed"), sem("consts1_landed"), sem("consts2_landed")
        mem_landed, out_stored, levels_landed = sem("mem_landed"), sem("out_stored"), sem("levels_landed")
        eps_ready = sem("eps_ready")
        roots_ready = sem("roots_ready")
        tile_done = sem("tile_done")
        x_ready = sem("x_ready")
        normed = sem("normed")
        CONSTS1, CONSTS2 = 10, 4

        ROOT_ORDER = (("ret", 0),) + tuple((name, tt) for names in (
            ("ln1",), ("ln2",), ("ffn1_pre",), ("ffn1_post", "mix_pre"), ("hg",), ("mem_kv",), ("mix_post", "mem_pre"),
            ("mem_post",), ("ffn2_pre",), ("ffn2_post",)) for tt in range(TT) for name in names)
        root_count = {key: n + 1 for n, key in enumerate(ROOT_ORDER)}
        tile_count = {name: n + 1 for n, name in enumerate(("wout1", "down1", "downA", "wout2", "mo", "downB"))}
        x_count = {name: TT * (n + 1) for n, name in
                   enumerate(("ln1", "ln2", "ffn1_post", "mix_post", "mem_post", "ffn2_post"))}
        normed_count = {name: TT * (n + 1) for n, name in
                        enumerate(("ffn1_pre", "mix_pre", "mem_pre", "ffn2_pre"))}

        def gain_free(name):
            if name.startswith("ln"):
                return x_ready, x_count[name[:3]]
            if name in normed_count:
                return normed, normed_count[name]
            if name in x_count:
                return x_ready, x_count[name]
            if name == "hg_norm":
                return sem("oa_ready"), TT
            if name == "mem_kv":
                return sem("mem_normed"), TT
            j = 15 if name == "gate0" else 17
            return pair_taken[j % 2], PAIR["win2", j][1] + 1

        def taken(name, j):
            n, used = PAIR[name, j]
            return n, used + 1

        def filled(name, j):
            if dict(BLOCKS)[name]:
                return UNIT[name] + 2 * j + 2
            return UNIT[name] + FB

        block = ctx.enter_context(nc.Block())

        @block.sync
        def _(sync):
            sync.dma_start(small["ident"][:, :], dram["c_ident"]).then_inc(x_landed, 16)
            sync.dma_start(x[:, :, :], dram["x"].rearrange("(t p) c -> p t c", p=P)).then_inc(x_landed, 16)

            def load(u, parts):
                slot = u % SLOTS
                if u >= SLOTS:
                    sync.wait_ge(unit_rest, u - SLOTS + 1)
                for dst, src in parts(raw[:, slot, :]):
                    sync.dma_start(dst, src).then_inc(unit_landed[slot], 16)

            def load_block(u, w, c0, halves=(0, 1)):
                wv = w.rearrange("(k p) n -> p k n", p=P)
                for n_half, half in enumerate(halves):
                    k = 4 * half
                    load(u + n_half, lambda d: [(d.rearrange("p (k n) -> p k n", k=4)[:, n:n + 2, :],
                                               wv[:, k + n:k + n + 2, c0:c0 + NB]) for n in (0, 2)])

            def load_up(u, w, j):
                wv = w.rearrange("(k p) n -> p k n", p=P)
                for half in range(2):
                    k = 4 * half
                    load(u + half, lambda d: [(d.rearrange("p (k g n) -> p k g n", k=4, g=2)[:, :, g, :],
                                               wv[:, k:k + 4, g * FF + 256 * j:g * FF + 256 * j + 256])
                                              for g in range(2)])

            def load_down(u, w, i):
                wv = w.rearrange("(k p) n -> p k n", p=P)
                load(u, lambda d: [(d[:, k * D:(k + 1) * D], wv[:, 2 * i + k, :]) for k in range(2)])

            for name, k in BLOCKS:
                w = dram[{"win1": "w_in", "wout1": "w_out", "up1": "w_up", "down1": "w_down",
                          "upA": "ffn1_w_in_2", "downA": "ffn1_w_down_2", "win2": "w_in_2",
                          "brA": "w_branch_a_2", "brB": "w_branch_b_2", "wout2": "w_out_2",
                          "mkv": "w_mkv_2", "mq": "w_mq_2", "mo": "w_mo_2", "upB": "ffn2_w_in_2",
                          "downB": "ffn2_w_down_2"}[name]]
                for j in range(k or FB):
                    if not k:
                        load_down(UNIT[name] + j, w, j)
                    elif name.startswith("up"):
                        load_up(UNIT[name] + 2 * j, w, j)
                    else:
                        c0 = {"win1": WIN1, "win2": WIN2}[name][j][1] if name.startswith("win") else j * NB
                        load_block(UNIT[name] + 2 * j, w, c0, HALVES.get(name, (0, 1)))
            for tt in range(TT):
                sync.wait_ge(x_ready, x_count["ffn2_post"] - TT + tt + 1)
                sync.dma_start(out_dram[tt * P:(tt + 1) * P, :], x[:, tt, :]).then_inc(out_stored, 16)
            sync.wait_ge(out_stored, 16 * TT)

        @block.gpsimd
        def _(pool):
            for name, src in (("convw", "conv_w"), ("convb", "conv_b"), ("pscale", "pool_scale")):
                pool.dma_start(small[name][:], dram[src]).then_inc(consts1_landed, 16)
            for t, src in ((decay, "c_decay"), (window, "c_window"), (ropec, "c_ropec"), (ropes, "c_ropes")):
                pool.dma_start(t[:], dram[src]).then_inc(consts1_landed, 16)
            pool.dma_start(wpool[:, :, :], dram["w_pool"].rearrange("g c d -> c g d")).then_inc(consts1_landed, 16)
            pool.dma_start(small["causal"][:, :], dram["c_causal"]).then_inc(consts1_landed, 16)
            pool.dma_start(small["starts"][:, :], dram["c_starts"]).then_inc(consts1_landed, 16)
            pool.dma_start(small["lbl"][:, :, :], dram["hg_lb_logits_2"]).then_inc(consts2_landed, 16)
            pool.dma_start(small["flb"][:, :], dram["fox_f_bias_2"].partition_broadcast(P)).then_inc(consts2_landed, 16)
            pool.dma_start(wf_raw[:, :, :], dram["w_in_2"].rearrange("(k p) n -> p k n", p=P)
                           [:, :, FLOGIT:FLOGIT + HH]).then_inc(consts2_landed, 16)
            pool.dma_start(identb[:, :], dram["c_identb"]).then_inc(consts2_landed, 16)
            rotated = sem("rotated")
            for n, name in enumerate(GAINS):
                if n == GSLOTS:
                    pool.wait_ge(consts1_landed, 16 * CONSTS1)
                    by_head = lambda ap: ap.rearrange("p t (h d) -> p t h d", h=RH)
                    for j, dst in enumerate((rq, rk)):
                        pool.wait_ge(pair_taken[j], taken("win1", j)[1])
                        s4, a4, d4 = by_head(stage[:, j, :, :]), by_head(ra[:, :, :]), by_head(dst[:, :, :])
                        for tt in range(TT):
                            c4 = ropec[:, tt, :].unsqueeze(1).to_broadcast([P, RH, P])
                            pool.tensor_tensor(d4[:, tt], s4[:, tt], c4, ALU.mult).then_inc(rotated, 1)
                            for half in range(2):
                                o = slice(half * 64, half * 64 + 64)
                                i = slice(64 - half * 64, 128 - half * 64)
                                sn = ropes[:, tt, o].unsqueeze(1).to_broadcast([P, RH, 64])
                                pool.tensor_tensor(a4[:, tt, :, o], s4[:, tt, :, i], sn, ALU.mult).then_inc(rotated, 1)
                        pool.wait_ge(rotated, 3 * TT * (j + 1))
                        pool.tensor_tensor(dst[:, :, :], dst[:, :, :], ra[:, :, :], ALU.add).then_inc(sem("rope_done"), 1)
                        pool.wait_ge(sem("rope_done"), j + 1)
                if n >= GSLOTS:
                    pool.wait_ge(*gain_free(GAINS[n - GSLOTS]))
                if name == "hg_norm":
                    pool.dma_start(levels32[:, :, :], dram["c_levels"]).then_inc(levels_landed, 16)
                if name == "mem_kv":
                    pool.wait_ge(aux_done, AUX["oa", 3][0] + 1)
                    pool.dma_start(mem[:, :, :], dram["mem_2"].rearrange("(t p) c -> p t c", p=P))\
                        .then_inc(mem_landed, 16)
                pool.dma_start(gains[:, n % GSLOTS, :], dram["gain_" + name].partition_broadcast(P))\
                    .then_inc(gain_landed[n % GSLOTS], 16)

        @block.tensor
        def _(pe):
            done = [0]

            def unit(u, products, wait=None):
                slot = u % SLOTS
                pe.wait_ge(unit_rest, u + 1)
                for sh, sr, c, out, first, last in products:
                    wh, wr = high[:, slot, c:c + NB], rest[:, slot, c:c + NB]
                    pe.matmul(out, sh, wh, start=first, stop=False)
                    pe.matmul(out, sh, wr, start=False, stop=False)
                    mm = pe.matmul(out, sr, wh, start=False, stop=last)
                mm.then_inc(unit_used, 1)

            def chunk_products(name, j, half, tt, th=xt_high, tr=xt_rest):
                n, _ = PAIR[name, j]
                at = HALVES.get(name, (0, 1))[half]
                return [(th[:, 4 * at + k, tt * P:(tt + 1) * P], tr[:, 4 * at + k, tt * P:(tt + 1) * P], k * NB,
                         pair_of[n][:, tt, :], half == 0 and k == 0, half == 1 and k == 3) for k in range(4)]

            def wait_pair(name, j):
                n, used = PAIR[name, j]
                if used:
                    pe.wait_ge(pair_taken[n], used)

            def half_block(name, j, half, th=xt_high, tr=xt_rest):
                if half == 0:
                    wait_pair(name, j)
                tiles = [chunk_products(name, j, half, tt, th, tr) for tt in range(TT)]
                unit(UNIT[name] + 2 * j + half, [tiles[tt][k] for k in range(4) for tt in range(TT)])

            def by_tiles(u, products, before=None, between=None, signal=False):
                for tt in range(TT):
                    if before:
                        before(tt)
                    for half in range(2):
                        slot = (u + half) % SLOTS
                        if tt == 0:
                            pe.wait_ge(unit_rest, u + half + 1)
                        for sh, sr, c, out, first, last in products(half, tt):
                            wh, wr = high[:, slot, c:c + NB], rest[:, slot, c:c + NB]
                            pe.matmul(out, sh, wh, start=first, stop=False)
                            pe.matmul(out, sh, wr, start=False, stop=False)
                            mm = pe.matmul(out, sr, wh, start=False, stop=last)
                        if tt == TT - 1:
                            mm.then_inc(unit_used, 1)
                        elif half == 0 and between:
                            between()
                        elif half == 1 and signal:
                            mm.then_inc(tile_done, 1)

            def first_block(name, key, src, ready):
                for q in range(2):
                    ready(0)
                    transposes((key, q), [src(0, 4 * q + c) for c in range(4)])
                wait_pair(name, 0)

                def before(tt):
                    wait_taken((key, 2 * tt), (key, 2 * tt + 1))

                def between():
                    for q in range(2):
                        ready(1)
                        transposes((key, 2 + q), [src(1, 4 * q + c) for c in range(4)])

                by_tiles(UNIT[name], lambda half, tt: chunk_products(name, 0, half, tt), before, between)

            def last_block(name, j):
                wait_pair(name, j)
                by_tiles(UNIT[name] + 2 * j, lambda half, tt: chunk_products(name, j, half, tt), signal=True)

            def full_block(name, j, th=xt_high, tr=xt_rest):
                half_block(name, j, 0, th, tr)
                half_block(name, j, 1, th, tr)

            def down_products(i, kc, tt):
                return [(ht_high[:, kc, tt * P:(tt + 1) * P], ht_rest[:, kc, tt * P:(tt + 1) * P],
                         (kc % 2) * 2 * NB + n * NB, pair_of[n][:, tt, :], kc == 0, kc == FC - 1) for n in range(2)]

            def down(name, i):
                if i == 0:
                    for n in range(2):
                        wait_pair(name, n)
                if i < FB - 2:
                    unit(UNIT[name] + i, [p for kc in (2 * i, 2 * i + 1) for tt in range(TT)
                                          for p in down_products(i, kc, tt)])
                elif i == FB - 1:
                    by_tiles(UNIT[name] + i - 1,
                             lambda half, tt: [p for kc in (2 * (i - 1 + half), 2 * (i - 1 + half) + 1)
                                               for p in down_products(i - 1 + half, kc, tt)], signal=True)

            def aux(key):
                n, bank, used = AUX[key]
                assert n == done[0], (key, n, done[0])
                done[0] += 1
                if used:
                    pe.wait_ge(aux_taken[bank], used)
                return ps[:, bank, :]

            def wait_taken(*keys):
                for key in keys:
                    _, bank, used = AUX[key]
                    pe.wait_ge(aux_taken[bank], used + 1)

            def transposes(key, sources, then=None):
                out = aux(key)
                for n, src in enumerate(sources):
                    mm = pe.transpose(out[:, n * P:(n + 1) * P], src, ident[:, :])
                mm.then_inc(aux_done, 1)

            def token_groups(name, src, wait, kq=2, order=None):
                for g in range(TT * kq):
                    tt, q = divmod(g, kq)
                    wait(tt, q)
                    transposes((name, g), [src(tt, 4 * q + c) for c in range(4)])

            def from_x(tt, c):
                return x[:, tt, c * P:(c + 1) * P]

            def from_y(tt, c):
                return y[:, tt, c * P:(c + 1) * P]

            def head_pairs(name, src, g):
                transposes((name, g), [src[:, tt, c * P:(c + 1) * P]
                                       for c in (2 * (g % 2), 2 * (g % 2) + 1) for tt in range(TT)])

            pe.wait_ge(x_landed, 32)
            first_block("win1", "x", from_x, lambda tt: None)
            full_block("win1", 1)
            full_block("win1", 2)
            for n, (what, src) in enumerate((("q", rq), ("k", rk))):
                pe.wait_ge(sem("rope_done"), n + 1)
                for g in range(2):
                    head_pairs("rT" + what, src, g)
            half_block("win1", 3, 0)
            wait_taken(("rTq", 0), ("rTq", 1), ("rTk", 0), ("rTk", 1))
            for h in range(RH):
                out = aux(("rscore", h))
                pe.matmul(out[:, 0:S], rkT[:, h, 0:P], rqT[:, h, :], start=True, stop=True)
                pe.matmul(out[:, S:S + P], rkT[:, h, P:S], rqT[:, h, P:S], start=True, stop=True)\
                    .then_inc(aux_done, 1)
            half_block("win1", 3, 1)
            half_block("win1", 4, 0)
            pe.wait_ge(pair_taken[1], taken("win1", 3)[1])
            pe.wait_ge(consts1_landed, 16 * CONSTS1)
            for g in range(2):
                out = aux(("poolT", g))
                for c in range(2):
                    for tt in range(TT):
                        mm = pe.matmul(out[:, c * S:(c + 1) * S], rp[:, tt, (2 * g + c) * P:(2 * g + c + 1) * P],
                                       window[:, tt, 2 * g + c, :], start=(tt == 0), stop=(tt == TT - 1))
                mm.then_inc(aux_done, 1)
            wait_taken(*(("rscore", h) for h in range(RH)))
            for tt in range(TT):
                out = aux(("rout", tt))
                for h in range(RH):
                    o = out[:, h * P:(h + 1) * P]
                    v = [rv[:, t, h * P:(h + 1) * P] for t in range(TT)]
                    if tt == 0:
                        mm = pe.matmul(o, rsc[:, h, 0:P], v[0], start=True, stop=True)
                    else:
                        pe.matmul(o, rsc[:, h, P:S], v[0], start=True, stop=False)
                        mm = pe.matmul(o, rsc[:, h, S:S + P], v[1], start=False, stop=True)
                mm.then_inc(aux_done, 1)
            half_block("win1", 4, 1)
            wait_taken(("poolT", 0), ("poolT", 1))
            for g in range(2):
                out = aux(("pooly", g))
                for c in range(2):
                    mm = pe.matmul(out[:, c * S:(c + 1) * S], wpool[:, 2 * g + c, :], pooled[:, 2 * g + c, :],
                                   start=True, stop=True)
                mm.then_inc(aux_done, 1)
            pe.wait_ge(sem("pool_rest"), 2)
            half_block("wout1", 0, 0)
            for tt in range(TT):
                pe.wait_ge(sem("ret_ready"), tt + 1)
                transposes(("mixr", tt), [rout[:, tt, c * P:(c + 1) * P] for c in range(4)])
            wait_taken(("mixr", 0), ("mixr", 1))
            half_block("wout1", 0, 1)
            last_block("wout1", 1)

            def conv_transposes(j):
                pe.wait_ge(pair_taken[j % 2], taken("up1", j)[1])
                for key, off in ((("convg", j), 256), (("convv", j), 0)):
                    transposes(key, [gv[:, j % 2, tt, off + c * P:off + (c + 1) * P]
                                     for c in range(2) for tt in range(TT)])

            first_block("up1", "x1", from_x, lambda tt: pe.wait_ge(x_ready, x_count["ln1"] - TT + tt + 1))
            for j in range(1, FB):
                full_block("up1", j)
                conv_transposes(j - 1)
            conv_transposes(FB - 1)
            for i in range(FB):
                pe.wait_ge(sem("ffn_rest"), min(i + 1, FB))
                down("down1", i)

            def ffn(u_name, d_name, h_name, key, pre):
                first_block(u_name, key, from_y, lambda tt: pe.wait_ge(normed, normed_count[pre] - TT + tt + 1))
                for j in range(1, FB):
                    full_block(u_name, j)
                    hidden_transposes(u_name, h_name, j - 1)
                for i in range(FB):
                    if i == 2:
                        hidden_transposes(u_name, h_name, FB - 1)
                    wait_taken((h_name, i))
                    down(d_name, i)

            def hidden_transposes(u_name, h_name, j):
                n, count = taken(u_name, j)
                pe.wait_ge(pair_taken[n], count)
                transposes((h_name, j), [hid[:, j % 2, tt, c * P:(c + 1) * P]
                                         for c in range(2) for tt in range(TT)])

            def from_normed(name, key, stage_name):
                token_groups(key, from_y, lambda tt, q:
                             pe.wait_ge(normed, normed_count[stage_name] - TT + tt + 1))

            ffn("upA", "downA", "hA", "f1", "ffn1_pre")

            def fox_logits():
                out = aux(("flog", 0))
                pe.wait_ge(sem("wf_rest"), 1)
                for tt in range(TT):
                    for kc in range(KC):
                        xh, xr = xt_high[:, kc, tt * P:(tt + 1) * P], xt_rest[:, kc, tt * P:(tt + 1) * P]
                        o = out[:, tt * HH:(tt + 1) * HH]
                        pe.matmul(o, xh, wf_high[:, kc, :], start=(kc == 0), stop=False)
                        pe.matmul(o, xh, wf_rest[:, kc, :], start=False, stop=False)
                        mm = pe.matmul(o, xr, wf_high[:, kc, :], start=False, stop=(kc == KC - 1))
                mm.then_inc(aux_done, 1)

            def levels(n):
                hf, lv = HG_STEPS[n]
                pe.wait_ge(sem("level_ready"), n + 1)
                for g in range(1 if lv == 128 else 2):
                    out = aux(("lv", hf, lv, g))
                    for c in range(4):
                        o = out[:, c * P:(c + 1) * P]
                        h, tt = (c, None) if lv == 128 else (2 * g + c // 2, c % 2)
                        t = slice(0, P) if tt is None else slice(tt * P, (tt + 1) * P)
                        if lv == 0:
                            mm = pe.matmul(o, hk[:, HALF * hf + h, t], hq[:, HALF * hf + h, t], start=True, stop=True)
                        else:
                            mm = pe.matmul(o, hqk[:, h, t], hqk[:, h, P:S] if tt is None else hqk[:, h, t],
                                           start=True, stop=True)
                    mm.then_inc(aux_done, 1)
                if lv == 128:
                    wait_taken(*(("lv", hf, v, g) for v in (0, *LEVELS) for g in range(2)), ("lv", hf, 128, 0))
                    for tt in range(TT):
                        out = aux(("hgo", hf, tt))
                        for h in range(HALF):
                            o = out[:, h * P:(h + 1) * P]
                            c = slice((HALF * hf + h) * P, (HALF * hf + h + 1) * P)
                            if tt == 0:
                                mm = pe.matmul(o, ha[:, h, 0:P], hi_[:, 0, c], start=True, stop=True)
                            else:
                                pe.matmul(o, ha[:, h, P:S], hi_[:, 0, c], start=True, stop=False)
                                mm = pe.matmul(o, ha[:, h, S:S + P], hi_[:, 1, c], start=False, stop=True)
                        mm.then_inc(aux_done, 1)

            def fox(n):
                if n < HH:
                    out = aux(("fs", n))
                    for tt in range(TT):
                        o = out[:, 0:P] if tt == 0 else out[:, P:P + S]
                        w = (tt + 1) * P
                        pe.matmul(o, fqT[:, n, tt * P:(tt + 1) * P], fkT[:, n, 0:w], start=True, stop=False)
                        pe.matmul(o, ident[0:HH, n:n + 1].to_broadcast([HH, P]), fcum[:, 0:w], start=False, stop=False)
                        mm = pe.matmul(o[:, w - P:w], identb[:, :], causal[:, :], start=False, stop=True)
                    mm.then_inc(aux_done, 1)
                if 1 <= n < HH + 1:
                    h = n - 1
                    wait_taken(("fs", h))
                    transposes(("fp", h), [fp[:, h % 2, c * P:(c + 1) * P] for c in range(3)])
                if n >= 2:
                    h = n - 2
                    wait_taken(("fp", h))
                    out = aux(("fo", h))
                    v = [fv[:, t, h * P:(h + 1) * P] for t in range(TT)]
                    pe.matmul(out[:, 0:P], fpT[:, h % 2, 0:P], v[0], start=True, stop=True)
                    pe.matmul(out[:, P:S], fpT[:, h % 2, P:S], v[0], start=True, stop=False)
                    pe.matmul(out[:, P:S], fpT[:, h % 2, S:S + P], v[1], start=False, stop=True).then_inc(aux_done, 1)

            for u in range(36):
                j, half = divmod(u, 2)
                if u == 0:
                    first_block("win2", "m2", from_y, lambda tt: pe.wait_ge(normed, normed_count["mix_pre"] - TT + tt + 1))
                if u >= 2:
                    half_block("win2", j, half)
                if u == 1:
                    fox_logits()
                if u == 3:
                    out = aux(("flog", 1))
                    pe.wait_ge(sem("flog_ready"), 1)
                    for tt in range(TT):
                        mm = pe.transpose(out[0:HH, tt * P:(tt + 1) * P], flog[:, tt, :], ident[:, :])
                    mm.then_inc(aux_done, 1)
                if u >= 2 and half == 0 and WIN2[j - 1][0] in ("f", "q", "fq", "fk"):
                    n, count = taken("win2", j - 1)
                    pe.wait_ge(pair_taken[n], count)
                    for g in range(2):
                        transposes((WIN2[j - 1][0] + "T", 2 * ((j - 1) % 2) + g),
                                   [stage[:, (j - 1) % 2, tt, c * P:(c + 1) * P]
                                    for c in (2 * g, 2 * g + 1) for tt in range(TT)])
                for n in HG_SLOT[u]:
                    levels(n)
                for n in FOX_SLOT[u]:
                    if n == 0:
                        wait_taken(*((w + "T", g) for w in ("fq", "fk") for g in range(4)))
                        wait_taken(("flog", 1))
                        pe.wait_ge(consts1_landed, 16 * CONSTS1)
                        pe.wait_ge(consts2_landed, 16 * CONSTS2)
                    fox(n)

            token_groups("oa", lambda tt, c: ho[:, c // 4, tt, (c % 4) * P:(c % 4 + 1) * P],
                         lambda tt, q: pe.wait_ge(sem("oa_ready"), tt + 1))
            wait_taken(*(("oa", g) for g in range(4)))
            full_block("brA", 0)
            full_block("brA", 1)
            wait_taken(("fo", HH - 1), ("fo", HH - 2))
            token_groups("ob", lambda tt, c: fo[:, c, tt, :], lambda tt, q: None)
            wait_taken(*(("ob", g) for g in range(4)))
            full_block("brB", 0)
            full_block("brB", 1)
            token_groups("memn", lambda tt, c: mem[:, tt, c * P:(c + 1) * P],
                         lambda tt, q: pe.wait_ge(sem("mem_normed"), tt + 1))
            token_groups("y2", from_y, lambda tt, q: pe.wait_ge(sem("y2_ready"), 2))
            wait_taken(*(("y2", g) for g in range(4)))
            full_block("wout2", 0)
            last_block("wout2", 1)

            wait_taken(*(("memn", g) for g in range(4)))
            for j in range(4):
                full_block("mkv", j, mt_high, mt_rest)
            from_normed("", "mpre", "mem_pre")
            pe.wait_ge(pair_taken[0], taken("mkv", 0)[1])
            pe.wait_ge(pair_taken[1], taken("mkv", 1)[1])
            for g in range(4):
                transposes(("mkT", g), [mstage[:, tt, c * P:(c + 1) * P] for c in (2 * g, 2 * g + 1) for tt in range(TT)])
            wait_taken(*(("mpre", g) for g in range(4)))
            full_block("mq", 0)
            full_block("mq", 1)
            for g in range(4):
                if g % 2 == 0:
                    n, count = taken("mq", g // 2)
                    pe.wait_ge(pair_taken[n], count)
                transposes(("mqT", g), [mstage[:, tt, c * P:(c + 1) * P] for c in (2 * g, 2 * g + 1) for tt in range(TT)])
            wait_taken(*((w, g) for w in ("mkT", "mqT") for g in range(4)))
            for n in range(MH + 2):
                if n < MH:
                    out = aux(("ms", n))
                    for tt in range(TT):
                        for c in range(2):
                            mm = pe.matmul(out[:, tt * S:(tt + 1) * S], mqT[:, 2 * n + c, tt * P:(tt + 1) * P],
                                           mkT[:, 2 * n + c, :], start=(c == 0), stop=(c == 1))
                    mm.then_inc(aux_done, 1)
                if 1 <= n < MH + 1:
                    wait_taken(("ms", n - 1))
                    transposes(("mp", n - 1), [mp[:, tt, t * P:(t + 1) * P] for t in range(TT) for tt in range(TT)])
                if n >= 2:
                    h = n - 2
                    wait_taken(("mp", h))
                    out = aux(("mo", h))
                    for tt in range(TT):
                        for t in range(TT):
                            mm = pe.matmul(out[:, tt * S:(tt + 1) * S], mpT[:, h % 2, t, tt * P:(tt + 1) * P],
                                           mv[:, t, h * S:(h + 1) * S], start=(t == 0), stop=(t == TT - 1))
                    mm.then_inc(aux_done, 1)
            wait_taken(*(("mo", h) for h in range(MH)))
            token_groups("om", lambda tt, c: mo[:, tt, c * P:(c + 1) * P], lambda tt, q: None)
            wait_taken(*(("om", g) for g in range(4)))
            full_block("mo", 0)
            last_block("mo", 1)
            ffn("upB", "downB", "hB", "f2", "ffn2_pre")
            assert done[0] == len(AUX)

        @block.scalar
        def _(act):
            split = [0]
            mine = sem("scalar_steps")
            steps = [0]

            def step(ins):
                ins.then_inc(mine, 1)
                steps[0] += 1

            def settle():
                act.wait_ge(mine, steps[0])

            def split_to(n):
                while split[0] < min(n, UNIT["end"]):
                    u = split[0]
                    act.wait_ge(unit_landed[u % SLOTS], 32 * (u // SLOTS + 1))
                    if u >= SLOTS:
                        act.wait_ge(unit_used, u - SLOTS + 1)
                    act.activation(high[:, u % SLOTS, :], raw[:, u % SLOTS, :], ACT.Copy).then_inc(unit_high, 1)
                    split[0] += 1

            def aux(key):
                n, bank, _ = AUX[key]
                act.wait_ge(aux_done, n + 1)
                return ps[:, bank, :]

            def group_to_high(key, dst):
                src = aux(key)
                if len(dst.shape) == 3:
                    src = src.rearrange("p (k n) -> p k n", k=dst.shape[1])
                act.activation(dst, src, ACT.Copy).then_inc(group_high, 1)

            def tile_groups(name, tt, dst=xt_high):
                for q in range(2):
                    group_to_high((name, 2 * tt + q), dst[:, 4 * q:4 * q + 4, tt * P:(tt + 1) * P])

            def token_groups(name, dst=xt_high):
                for tt in range(TT):
                    tile_groups(name, tt, dst)

            def take(key, dst, **how):
                _, bank, _ = AUX[key]
                src = aux(key)[:, 0:int(np.prod(dst.shape[1:]))]
                if len(dst.shape) == 3:
                    src = src.rearrange("p (k n) -> p k n", k=dst.shape[1])
                act.activation(dst, src, ACT.Copy, **how).then_inc(aux_taken[bank], 1)

            def block_values(name, j):
                act.wait_ge(unit_used, filled(name, j))
                return pair_of[taken(name, j)[0]]

            def take_block(name, j, dst, func=ACT.Copy, **how):
                n, _ = taken(name, j)
                act.activation(dst, block_values(name, j), func, **how).then_inc(pair_taken[n], 1)

            def roots_of(src, name, tt, width, offset):
                assert ROOT_ORDER[root[0]] == (name, tt), (name, tt, ROOT_ORDER[root[0]])
                root[0] += 1
                c = NS.get(name, 0) + tt
                act.activation(roots[:, c:c + width], src, ACT.Sqrt, bias=offset)\
                    .then_inc(roots_ready, 1)

            root = [0]

            def square_tile(name, tt, src, junk):
                c = NS[name] + tt
                step(act.activation(junk, src, ACT.Square, scale=D ** -0.5, accum_out=sums[:, c:c + 1]))
                settle()
                roots_of(sums[:, c:c + 1], name, tt, 1, eps[:, 1:2])

            def wait_x(after, tt):
                act.wait_ge(x_ready, x_count[after] - TT + tt + 1)

            def pre_norm(name, after, tt):
                wait_x(after, tt)
                square_tile(name, tt, x[:, tt, :], y[:, tt, :])

            def late_pre_norm(name, after):
                for tt in range(TT):
                    wait_x(after, tt)
                    square_tile(name, tt, x[:, tt, :], junk_a[:, tt, :])

            def wait_tile(product, tt):
                if tt == 0:
                    act.wait_ge(tile_done, tile_count[product])
                else:
                    act.wait_ge(unit_used, filled(product, 1))

            def post_norm(name, product, tt):
                wait_tile(product, tt)
                c, part = NS[name] + tt, small["partsum"]
                step(act.activation(y[:, tt, 0:NB], pair_of[0][:, tt, :], ACT.Square, scale=D ** -0.5, accum_out=part[:, 0:1]))
                step(act.activation(y[:, tt, NB:D], pair_of[1][:, tt, :], ACT.Square, scale=D ** -0.5,
                                    accum_out=sums[:, c:c + 1]))
                act.wait_ge(mine, steps[0] - 1)
                step(act.activation(part[:, 1:2], part[:, 0:1], ACT.Identity, bias=eps[:, 1:2]))
                settle()
                roots_of(sums[:, c:c + 1], name, tt, 1, part[:, 1:2])

            def layer_root(name, tt):
                act.wait_ge(sem("var_ready"), x_count[name] - TT + tt + 1)
                roots_of(meanvar[:, tt, 1:2], name, tt, 1, eps[:, 0:1])

            act.wait_ge(eps_ready, 2)
            split_to(UNIT["win1"] + 1)
            token_groups("x")
            for j, dst in enumerate((stage[:, 0, :, :], stage[:, 1, :, :], rv[:, :, :])):
                split_to(UNIT["win1"] + 2 * j + 4)
                take_block("win1", j, dst)
            for what, dst in (("rTq", rqT), ("rTk", rkT)):
                for g in range(2):
                    take((what, g), dst[:, 2 * g:2 * g + 2, :])
            split_to(UNIT["win1"] + 10)
            take_block("win1", 3, rp[:, :, :])
            split_to(UNIT["wout1"] + 2)
            for g in range(2):
                take(("poolT", g), pooled[:, 2 * g:2 * g + 2, :])
            for tt in range(TT):
                act.activation(rsq[:, tt, :], aux(("rout", tt)), ACT.Square, scale=P ** -0.5).then_inc(sem("ret_squares"), 1)
            act.wait_ge(sem("ret_sums"), TT)
            roots_of(sums[:, 0:TT * RH], "ret", 0, TT * RH, eps[:, 1:2])
            take_block("win1", 4, rg[:, :, :], ACT.Silu)
            for g in range(2):
                out = aux(("pooly", g))
                for c in range(2):
                    ins = act.activation(pooly[:, 2 * g + c, :], out[:, c * S:(c + 1) * S], ACT.Copy,
                                         scale=small["pscale"][:, 2 * g + c:2 * g + c + 1])
                    if c == 0:
                        step(ins)
                ins.then_inc(aux_taken[AUX["pooly", g][1]], 1)
                settle()
                act.wait_ge(aux_taken[AUX["pooly", g][1]], AUX["pooly", g][2] + 1)
                act.activation(xt_high[:, 4 + 2 * g:6 + 2 * g, :], pooly[:, 2 * g:2 * g + 2, :], ACT.Copy)\
                    .then_inc(sem("pool_high"), 1)
            split_to(UNIT["wout1"] + 4)
            for tt in range(TT):
                group_to_high(("mixr", tt), xt_high[:, 0:4, tt * P:(tt + 1) * P])
            split_to(UNIT["up1"] + 2)
            layer_root("ln1", 0)
            layer_root("ln1", 1)
            token_groups("x1")

            def conv_values(j):
                out = aux(("convg", j))
                if j >= 2:
                    act.wait_ge(sem("ffn_rest"), j - 1)
                for c in range(2):
                    f = 2 * j + c
                    act.activation(conv[:, j % 2, c, :], out[:, c * S:(c + 1) * S], ACT.Identity,
                                   scale=small["convw"][:, f, 2:3], bias=small["convb"][:, f:f + 1])\
                        .then_inc(sem("conv_last"), 1)
                act.wait_ge(aux_taken[6], AUX["convg", j][2] + 1)
                act.activation(convs[:, :, :], conv[:, j % 2, :, :], ACT.Silu).then_inc(sem("conv_silu"), 1)
                act.wait_ge(aux_taken[7], AUX["convv", j][2] + 1)
                act.activation(ht_high[:, 2 * j:2 * j + 2, :], conv[:, j % 2, :, :], ACT.Copy)\
                    .then_inc(sem("ffn_high"), 1)

            act.wait_ge(consts1_landed, 16 * CONSTS1)
            for j in range(FB):
                split_to(UNIT["up1"] + 2 * j + 4)
                take_block("up1", j, gv[:, j % 2, :, :])
                if j:
                    conv_values(j - 1)
            conv_values(FB - 1)
            split_to(UNIT["upA"] + 2)
            layer_root("ln2", 0)
            layer_root("ln2", 1)

            scales = [0]

            def ffn(u_name, d_name, h_name, pre, after, key, following):
                def hidden_high(j):
                    group_to_high((h_name, j), ht_high[:, 2 * j:2 * j + 2, :])

                token_groups(key)
                late_pre_norm(pre, after)
                scales[0] += 1
                for j in range(FB):
                    split_to(UNIT[u_name] + 2 * j + 4)
                    if j == 0:
                        act.wait_ge(sem("scales_ready"), scales[0])
                    gate_values = block_values(u_name, j)[:, :, 0:256]
                    for tt in range(TT):
                        c = NS[pre] + tt
                        act.activation(act_[:, j % 2, tt, :], gate_values[:, tt, :], ACT.Silu, scale=recips[:, c:c + 1])\
                            .then_inc(sem("silu_done"), 1)
                    if j:
                        hidden_high(j - 1)
                split_to(UNIT[d_name] + 4)
                hidden_high(FB - 1)
                split_to(UNIT[following] + 2)

            ffn("upA", "downA", "hA", "ffn1_pre", "ln2", "f1", "win2")

            post_norm("ffn1_post", "downA", 0)
            pre_norm("mix_pre", "ffn1_post", 0)
            post_norm("ffn1_post", "downA", 1)
            tile_groups("m2", 0)
            pre_norm("mix_pre", "ffn1_post", 1)
            tile_groups("m2", 1)

            def fox_logits():
                act.wait_ge(consts2_landed, 16 * CONSTS2)
                act.activation(wf_high[:, :, :], wf_raw[:, :, :], ACT.Copy).then_inc(sem("wf_high"), 1)
                act.wait_ge(sem("lb_shifted"), 1)
                act.activation(small["lbl"][:, :, :], small["lbl"][:, :, :], ACT.Exp).then_inc(sem("lb_exp"), 1)

            def fox_log_sigmoids():
                act.wait_ge(aux_taken[AUX["flog", 0][1]], AUX["flog", 0][2] + 1)
                step(act.activation(flabs[:, :, :], flog[:, :, :], ACT.Abs))
                settle()
                act.activation(flabs[:, :, :], flabs[:, :, :], ACT.Exp, scale=-1.0).then_inc(sem("flog_exp"), 1)
                act.wait_ge(sem("flog_exp"), 1)
                act.activation(flabs[:, :, :], flabs[:, :, :], ACT.Ln, bias=1.0).then_inc(sem("flog_ln"), 1)

            def level_exp(n):
                hf, lv = HG_STEPS[n]
                hs = slice(HALF * hf, HALF * hf + HALF)
                if lv == 0:
                    return
                act.wait_ge(sem("level_diff"), n - hf)
                if lv == 128:
                    act.activation(he[:, :, 0:P], he[:, :, 0:P], ACT.Exp, scale=-1.0)
                    act.activation(he[:, :, P:P + CHUNK], hb[:, hs, P:P + CHUNK], ACT.Exp)
                    ins = act.activation(he[:, :, P + CHUNK:S], he[:, :, P + CHUNK:S], ACT.Exp)
                else:
                    e = he[:, :, :].rearrange("p h (n t) -> p (h n) t", t=2 * lv)
                    b = hb[:, hs, :].rearrange("p h (n t) -> p (h n) t", t=2 * lv) if lv == 64 else e
                    act.activation(e[:, :, 0:lv], e[:, :, 0:lv], ACT.Exp, scale=-1.0)
                    ins = act.activation(e[:, :, lv:2 * lv], b[:, :, lv:2 * lv], ACT.Exp)
                ins.then_inc(sem("level_exp"), 1)

            for u in range(36):
                split_to(UNIT["win2"] + u + 3)
                j, half = divmod(u, 2)
                what = WIN2[j][0]
                c = slice((j % 2) * NB, (j % 2 + 1) * NB)
                if u == 0:
                    fox_logits()
                if u == 3:
                    fox_log_sigmoids()
                if half:
                    if what == "f":
                        take_block("win2", j, stage[:, j % 2, :, :], ACT.Sigmoid)
                    elif what == "q":
                        act.activation(stage[:, j % 2, :, :], block_values("win2", j), ACT.Tanh, scale=0.5)\
                            .then_inc(sem("q_tanh"), 1)
                    elif what == "g":
                        act.activation(hg[:, :, c], block_values("win2", j), ACT.Tanh, scale=0.5)\
                            .then_inc(sem("g_tanh"), 1)
                    elif what == "fq":
                        take_block("win2", j, stage[:, j % 2, :, :], scale=P ** -0.5)
                    elif what == "fk":
                        take_block("win2", j, stage[:, j % 2, :, :])
                    elif what == "i":
                        take_block("win2", j, hi_[:, :, c])
                    elif what == "fv":
                        take_block("win2", j, fv[:, :, c])
                    else:
                        g = j - 14
                        act.wait_ge(pair_taken[j % 2], taken("win2", j)[1])
                        d = gate[g // 2][:, :, c]
                        act.activation(d, d, ACT.Tanh, scale=0.5).then_inc(sem("gate_tanh"), 1)
                elif j and WIN2[j - 1][0] in ("f", "q", "fq", "fk"):
                    w, k = WIN2[j - 1][0], (j - 1) % 2
                    if w == "f":
                        act.wait_ge(sem("f_ready"), k + 1)
                        act.activation(hb[:, HALF * k:HALF * k + HALF, :], he[:, :, :], ACT.Ln).then_inc(sem("f_log"), 1)
                    else:
                        for g in range(2):
                            dst = {"q": hq, "fq": fqT, "fk": fkT}[w][:, HALF * k + 2 * g:HALF * k + 2 * g + 2, :]
                            take((w + "T", 2 * k + g), dst, **({"scale": 0.5} if w == "q" else {}))
                for n in HG_SLOT[u]:
                    if n == 0:
                        level_exp(1)
                    elif n + 1 < len(HG_STEPS):
                        level_exp(n + 1)
                    if n == len(HG_STEPS) - 1:
                        def src(tt):
                            for key in (("hgo", a, b) for a in range(2) for b in range(TT)):
                                act.wait_ge(aux_taken[AUX[key][1]], AUX[key][2] + 1)
                            return ho[:, :, tt, :]
                        for tt in range(TT):
                            square_tile("hg", tt, src(tt), junk_h[:, tt, :].rearrange("p (n c) -> p n c", n=2))
                for n in FOX_SLOT[u]:
                    if 1 <= n < HH + 1:
                        take(("fp", n - 1), fpT[:, (n - 1) % 2, :])
                    if n < HH:
                        act.wait_ge(sem("fox_max"), TT * (n + 1))
                        _, bank, _ = AUX["fs", n]
                        out = aux(("fs", n))
                        for tt in range(TT):
                            c0, c1 = (0, P) if tt == 0 else (P, P + S)
                            ins = act.activation(fp[:, n % 2, c0:c1], out[:, c0:c1], ACT.Exp,
                                                 bias=small["negmax"][:, n, tt:tt + 1],
                                                 accum_out=small["expsum"][:, n, tt:tt + 1])
                        ins.then_inc(aux_taken[bank], 1)

            split_to(UNIT["brA"] + 2)
            token_groups("oa")
            split_to(UNIT["brA"] + 4)
            split_to(UNIT["brB"] + 2)
            act.wait_ge(unit_used, filled("brA", 1))
            token_groups("ob")
            act.wait_ge(mem_landed, 16)
            for tt in range(TT):
                square_tile("mem_kv", tt, mem[:, tt, :], junk_m[:, tt, :])
            split_to(UNIT["brB"] + 4)
            split_to(UNIT["wout2"] + 2)
            act.wait_ge(sem("y2_ready"), 2)
            token_groups("memn", mt_high)
            token_groups("y2")
            split_to(UNIT["wout2"] + 4)
            split_to(UNIT["mkv"] + 2)
            for tt in range(TT):
                post_norm("mix_post", "wout2", tt)
                pre_norm("mem_pre", "mix_post", tt)
            split_to(UNIT["mkv"] + 4)
            for j in range(4):
                split_to(UNIT["mkv"] + 2 * j + 4)
                c = slice((j % 2) * NB, (j % 2 + 1) * NB)
                take_block("mkv", j, (mstage if j < 2 else mv)[:, :, c])
            token_groups("mpre")
            for g in range(4):
                take(("mkT", g), mkT[:, 2 * g:2 * g + 2, :])
            split_to(UNIT["mq"] + 4)
            for j in range(2):
                c = slice(j * NB, (j + 1) * NB)
                take_block("mq", j, mstage[:, :, c], scale=S ** -0.5)
            split_to(UNIT["mo"] + 2)
            for g in range(4):
                take(("mqT", g), mqT[:, 2 * g:2 * g + 2, :])
            for n in range(MH + 2):
                if 1 <= n < MH + 1:
                    take(("mp", n - 1), mpT[:, (n - 1) % 2, :, :].rearrange("p t s -> p (t s)"))
                if n < MH:
                    act.wait_ge(sem("mem_max"), n + 1)
                    _, bank, _ = AUX["ms", n]
                    out = aux(("ms", n))
                    for tt in range(TT):
                        ins = act.activation(mp[:, tt, :], out[:, tt * S:(tt + 1) * S], ACT.Exp,
                                             bias=small["negmax"][:, n, tt:tt + 1],
                                             accum_out=small["expsum"][:, n, tt:tt + 1])
                    ins.then_inc(aux_taken[bank], 1)
            split_to(UNIT["mo"] + 4)
            token_groups("om")
            split_to(UNIT["upB"] + 2)
            for tt in range(TT):
                post_norm("mem_post", "mo", tt)
            ffn("upB", "downB", "hB", "ffn2_pre", "mem_post", "f2", "end")
            for tt in range(TT):
                post_norm("ffn2_post", "downB", tt)
            assert split[0] == UNIT["end"]

        @block.vector
        def _(vec):
            split, groups = [0], [0]
            mine = sem("vector_steps")
            steps = [0]

            def step(ins):
                ins.then_inc(mine, 1)
                steps[0] += 1

            def settle():
                vec.wait_ge(mine, steps[0])

            def split_to(n):
                while split[0] < min(n, UNIT["end"]):
                    u = split[0]
                    slot = u % SLOTS
                    vec.wait_ge(unit_high, u + 1)
                    vec.tensor_tensor(rest[:, slot, :], raw[:, slot, :], high[:, slot, :].bitcast(F32),
                                      ALU.subtract).then_inc(unit_rest, 1)
                    split[0] += 1

            def aux(key):
                n, bank, _ = AUX[key]
                vec.wait_ge(aux_done, n + 1)
                return ps[:, bank, :]

            def took(key, ins):
                ins.then_inc(aux_taken[AUX[key][1]], 1)

            def group_to_rest(key, dst_high, dst_rest):
                _, bank, _ = AUX[key]
                groups[0] += 1
                vec.wait_ge(group_high, groups[0])
                src = ps[:, bank, :].rearrange("p (k n) -> p k n", k=dst_high.shape[1])
                vec.tensor_tensor(dst_rest, src, dst_high.bitcast(F32), ALU.subtract).then_inc(aux_taken[bank], 1)

            def tile_groups(name, tt, th=xt_high, tr=xt_rest):
                for q in range(2):
                    at = (slice(None), slice(4 * q, 4 * q + 4), slice(tt * P, (tt + 1) * P))
                    group_to_rest((name, 2 * tt + q), th[at], tr[at])

            def token_groups(name, th=xt_high, tr=xt_rest):
                for tt in range(TT):
                    tile_groups(name, tt, th, tr)

            def block_values(name, j):
                vec.wait_ge(unit_used, filled(name, j))
                return pair_of[taken(name, j)[0]]

            def took_block(name, j, ins):
                ins.then_inc(pair_taken[taken(name, j)[0]], 1)

            def gain(name):
                n = GAINS.index(name)
                vec.wait_ge(gain_landed[n % GSLOTS], 16 * (n // GSLOTS + 1))
                return gains[:, n % GSLOTS, :]

            def recip_roots(name, tt=0, cols=1):
                vec.wait_ge(roots_ready, root_count[name, tt])
                c = NS.get(name, 0) + tt
                step(vec.reciprocal(recips[:, c:c + cols], roots[:, c:c + cols]))
                settle()
                return recips[:, c:c + 1]

            def halves(ap):
                return ap.rearrange("p (n c) -> p n c", n=2)

            def pre_norm(name, tt):
                r, g = recip_roots(name, tt), gain(name)
                vec.scalar_tensor_tensor(y[:, tt, :], x[:, tt, :], r, g, ALU.mult, ALU.mult).then_inc(normed, 1)

            def gained(name, after, tt):
                g = gain(name)
                vec.wait_ge(x_ready, x_count[after] - TT + tt + 1)
                vec.tensor_tensor(y[:, tt, :], x[:, tt, :], g, ALU.mult).then_inc(normed, 1)

            def post_norm(name, scale, tt):
                r, g = recip_roots(name, tt), gain(name)
                for n in range(2):
                    c = slice(n * NB, (n + 1) * NB)
                    ins = vec.scalar_tensor_tensor(y[:, tt, c], pair_of[n][:, tt, :], r, g[:, c], ALU.mult, ALU.mult)
                    if tt == 0:
                        step(ins)
                    else:
                        ins.then_inc(pair_taken[n], 1)
                if tt == 0:
                    settle()
                else:
                    for n in range(2):
                        vec.wait_ge(pair_taken[n], PAIR[post_block[name], n][1] + 1)
                vec.scalar_tensor_tensor(x[:, tt, :], y[:, tt, :], scale, x[:, tt, :], ALU.mult, ALU.add)\
                    .then_inc(x_ready, 1)

            def attention_out(scores, key, dst, width, h):
                _, bank, used = AUX[scores]
                vec.wait_ge(aux_taken[bank], used + 1)
                sums_ = small["expsum"][:, h, :]
                step(vec.reciprocal(sums_, sums_))
                settle()
                src = aux(key)[:, 0:TT * width].rearrange("p (t c) -> p t c", t=TT)
                took(key, vec.tensor_tensor(dst, src, sums_.unsqueeze(2).to_broadcast([P, TT, width]), ALU.mult))

            post_block = {"ffn1_post": "downA", "mix_post": "wout2", "mem_post": "mo", "ffn2_post": "downB"}

            def layer_stats(product, tt):
                if tt == 0:
                    vec.wait_ge(tile_done, tile_count[product])
                else:
                    vec.wait_ge(unit_used, filled(product, 1))
                for n in range(2):
                    c = slice(n * NB, (n + 1) * NB)
                    ins = vec.scalar_tensor_tensor(y[:, tt, c], x[:, tt, c], ALPHA, pair_of[n][:, tt, :], ALU.mult, ALU.add)
                    if tt == 0:
                        step(ins)
                    else:
                        ins.then_inc(pair_taken[n], 1)
                if tt == 0:
                    settle()
                else:
                    for n in range(2):
                        vec.wait_ge(pair_taken[n], PAIR[product, n][1] + 1)
                for n in range(2):
                    step(vec.bn_stats(moments[:, tt, 6 * n:6 * n + 6], y[:, tt, n * NB:(n + 1) * NB]))
                settle()
                vec.bn_aggr(meanvar[:, tt, :], moments[:, tt, :].rearrange("p (n c) -> p n c", n=2)).then_inc(sem("var_ready"), 1)

            def layer_norm(name, tt):
                r, g, b = recip_roots(name, tt), gain(name + "_g"), gain(name + "_b")
                step(vec.scalar_tensor_tensor(y[:, tt, :], y[:, tt, :], meanvar[:, tt, 0:1], g, ALU.subtract, ALU.mult))
                settle()
                vec.scalar_tensor_tensor(x[:, tt, :], y[:, tt, :], r, b, ALU.mult, ALU.add).then_inc(x_ready, 1)

            vec.memset(eps[:, 0:1], LN_EPS).then_inc(eps_ready, 1)
            vec.memset(eps[:, 1:2], RMS_EPS).then_inc(eps_ready, 1)

            split_to(UNIT["win1"] + 1)
            token_groups("x")
            split_to(UNIT["win1"] + 10)
            vec.wait_ge(consts1_landed, 16 * CONSTS1)
            for h in range(RH):
                src = aux(("rscore", h))
                took(("rscore", h), vec.tensor_tensor(rsc[:, h, :], src[:, 0:384], decay[:, h, :], ALU.mult))
            split_to(UNIT["wout1"] + 2)
            for tt in range(TT):
                vec.wait_ge(sem("ret_squares"), tt + 1)
                vec.tensor_reduce(sums[:, RH * tt:RH * tt + RH], rsq[:, tt, :].rearrange("p (h d) -> p h d", h=RH),
                                  AX_X, ALU.add).then_inc(sem("ret_sums"), 1)
            recip_roots("ret", 0, TT * RH)
            for tt in range(TT):
                r4 = recips[:, RH * tt:RH * tt + RH].unsqueeze(2).to_broadcast([P, RH, P])
                o = rout[:, tt, :]
                took(("rout", tt), vec.tensor_tensor(o.rearrange("p (h d) -> p h d", h=RH),
                                                     aux(("rout", tt)).rearrange("p (h d) -> p h d", h=RH), r4, ALU.mult))
                vec.wait_ge(aux_taken[AUX["rout", tt][1]], AUX["rout", tt][2] + 1)
                vec.wait_ge(pair_taken[0], taken("win1", 4)[1])
                vec.tensor_tensor(o, o, rg[:, tt, :], ALU.mult).then_inc(sem("ret_ready"), 1)
            for g in range(2):
                vec.wait_ge(sem("pool_high"), g + 1)
                k = slice(4 + 2 * g, 6 + 2 * g)
                vec.tensor_tensor(xt_rest[:, k, :], pooly[:, 2 * g:2 * g + 2, :], xt_high[:, k, :].bitcast(F32),
                                  ALU.subtract).then_inc(sem("pool_rest"), 1)
            split_to(UNIT["wout1"] + 4)
            for tt in range(TT):
                at = (slice(None), slice(0, 4), slice(tt * P, (tt + 1) * P))
                group_to_rest(("mixr", tt), xt_high[at], xt_rest[at])
            split_to(UNIT["up1"] + 2)
            layer_stats("wout1", 0)
            layer_norm("ln1", 0)
            layer_stats("wout1", 1)
            tile_groups("x1", 0)
            layer_norm("ln1", 1)
            tile_groups("x1", 1)

            def conv_values(j):
                src = aux(("convg", j)).rearrange("p (c s) -> p c s", c=2)
                val = ps[:, 7, :].rearrange("p (c s) -> p c s", c=2)
                vec.wait_ge(sem("conv_last"), 2 * j + 2)
                for tap, back in ((1, 1), (0, 2)):
                    for c in range(2):
                        d = conv[:, j % 2, c, back:S]
                        ins = vec.scalar_tensor_tensor(d, src[:, c, 0:S - back], small["convw"][:, 2 * j + c, tap:tap + 1],
                                                       d, ALU.mult, ALU.add)
                        if (tap, c) == (0, 1):
                            took(("convg", j), ins)
                        else:
                            step(ins)
                    if tap == 1:
                        settle()
                vec.wait_ge(sem("conv_silu"), j + 1)
                aux(("convv", j))
                took(("convv", j), vec.tensor_tensor(conv[:, j % 2, :, :], convs[:, :, :], val, ALU.mult))
                vec.wait_ge(sem("ffn_high"), j + 1)
                k = slice(2 * j, 2 * j + 2)
                vec.tensor_tensor(ht_rest[:, k, :], conv[:, j % 2, :, :], ht_high[:, k, :].bitcast(F32),
                                  ALU.subtract).then_inc(sem("ffn_rest"), 1)

            for j in range(FB):
                split_to(UNIT["up1"] + 2 * j + 4)
                if j:
                    conv_values(j - 1)
            conv_values(FB - 1)
            split_to(UNIT["upA"] + 2)
            layer_stats("down1", 0)
            layer_norm("ln2", 0)
            gained("ffn1_pre", "ln2", 0)
            layer_stats("down1", 1)
            tile_groups("f1", 0)
            layer_norm("ln2", 1)
            gained("ffn1_pre", "ln2", 1)
            tile_groups("f1", 1)

            def ffn(u_name, d_name, h_name, pre, following):
                def hidden_rest(j):
                    k = slice(2 * j, 2 * j + 2)
                    group_to_rest((h_name, j), ht_high[:, k, :], ht_rest[:, k, :])

                split_to(UNIT[u_name] + 4)
                for tt in range(TT):
                    vec.wait_ge(roots_ready, root_count[pre, tt])
                c = NS[pre]
                vec.reciprocal(recips[:, c:c + TT], roots[:, c:c + TT]).then_inc(sem("scales_ready"), 1)
                scales[0] += 1
                vec.wait_ge(sem("scales_ready"), scales[0])
                for j in range(FB):
                    split_to(UNIT[u_name] + 2 * j + 4)
                    values = block_values(u_name, j)[:, :, 256:NB]
                    for tt in range(TT):
                        silus[0] += 1
                        vec.wait_ge(sem("silu_done"), silus[0])
                        ins = vec.scalar_tensor_tensor(hid[:, j % 2, tt, :], values[:, tt, :], recips[:, c + tt:c + tt + 1],
                                                       act_[:, j % 2, tt, :], ALU.mult, ALU.mult)
                        if tt == 0:
                            step(ins)
                    took_block(u_name, j, ins)
                    if j:
                        hidden_rest(j - 1)
                split_to(UNIT[d_name] + 4)
                hidden_rest(FB - 1)
                split_to(UNIT[following] + 2)

            silus, scales = [0], [0]
            ffn("upA", "downA", "hA", "ffn1_pre", "win2")

            post_norm("ffn1_post", 0.5, 0)
            pre_norm("mix_pre", 0)
            post_norm("ffn1_post", 0.5, 1)
            tile_groups("m2", 0)
            pre_norm("mix_pre", 1)
            tile_groups("m2", 1)
            vec.wait_ge(sem("wf_high"), 1)
            vec.tensor_tensor(wf_rest[:, :, :], wf_raw[:, :, :], wf_high[:, :, :].bitcast(F32), ALU.subtract)\
                .then_inc(sem("wf_rest"), 1)
            lbl, lb = small["lbl"], small["lb"]
            vec.wait_ge(consts2_landed, 16 * CONSTS2)
            step(vec.tensor_tensor(lb[:, 2, :], lbl[:, 0, :], lbl[:, 1, :], ALU.max))
            settle()
            vec.tensor_tensor(lbl[:, :, :], lbl[:, :, :], lb[:, 2, :].unsqueeze(1).to_broadcast([P, 2, HH]),
                              ALU.subtract).then_inc(sem("lb_shifted"), 1)
            vec.wait_ge(sem("lb_exp"), 1)
            step(vec.tensor_tensor(lb[:, 2, :], lbl[:, 0, :], lbl[:, 1, :], ALU.add))
            settle()
            step(vec.reciprocal(lb[:, 3, :], lb[:, 2, :]))
            settle()
            for n in range(2):
                step(vec.tensor_tensor(lb[:, n, :], lbl[:, n, :], lb[:, 3, :], ALU.mult))
            settle()
            vec.wait_ge(levels_landed, 16)
            step(vec.tensor_copy(levelmask[:, :, :], levels32[:, :, :]))
            settle()

            def diff(n):
                hf, lv = HG_STEPS[n]
                b = hb[:, HALF * hf:HALF * hf + HALF, :]
                vec.wait_ge(sem("level_ready"), n)
                if lv == 128:
                    cr = small["crossref"]
                    step(vec.tensor_tensor(cr[:, :], b[:, :, CHUNK - 1], b[:, :, P - 1], ALU.add))
                    settle()
                    last = lambda ap: ap.unsqueeze(2).to_broadcast([P, HALF, CHUNK])
                    vec.tensor_tensor(he[:, :, 0:CHUNK], b[:, :, 0:CHUNK], last(cr[:, :]), ALU.subtract)
                    vec.tensor_tensor(he[:, :, CHUNK:P], b[:, :, CHUNK:P], last(b[:, :, P - 1]), ALU.subtract)
                    ins = vec.tensor_tensor(he[:, :, P + CHUNK:S], b[:, :, P + CHUNK:S], last(b[:, :, P + CHUNK - 1]), ALU.add)
                else:
                    e = he[:, :, :].rearrange("p h (n t) -> p (h n) t", t=2 * lv)
                    b = b.rearrange("p h (n t) -> p (h n) t", t=2 * lv)
                    w = lv if lv == 64 else 2 * lv
                    ref = b[:, :, lv - 1].unsqueeze(2).to_broadcast([P, HALF * S // (2 * lv), w])
                    ins = vec.tensor_tensor(e[:, :, 0:w], b[:, :, 0:w], ref, ALU.subtract)
                ins.then_inc(sem("level_diff"), 1)

            def apply_decays(n):
                hf, lv = HG_STEPS[n]
                hs = slice(HALF * hf, HALF * hf + HALF)
                vec.wait_ge(sem("level_exp"), n - hf)
                t = P if lv == 128 else lv
                view = lambda ap: ap.rearrange("p h (n t) -> p (h n) t", t=2 * t)
                e, o, q, k = view(he[:, :, :]), view(hqk[:, :, :]), view(hq[:, hs, :]), view(hk[:, hs, :])
                step(vec.tensor_tensor(o[:, :, 0:t], e[:, :, 0:t], k[:, :, 0:t], ALU.mult))
                settle()
                vec.tensor_tensor(o[:, :, t:2 * t], e[:, :, t:2 * t], q[:, :, t:2 * t], ALU.mult)\
                    .then_inc(sem("level_ready"), 1)

            def place_scores(n):
                hf, lv = HG_STEPS[n]
                if lv == 128:
                    src = aux(("lv", hf, lv, 0)).rearrange("p (h t) -> p h t", h=HALF)
                    took(("lv", hf, lv, 0), vec.tensor_copy(ha[:, :, P:S], src))
                    return
                m = levelmask[:, (0, *LEVELS).index(lv), :].unsqueeze(1).to_broadcast([P, TT, P])
                for g in range(2):
                    src = aux(("lv", hf, lv, g))
                    for c in range(2):
                        d = ha[:, 2 * g + c, :].rearrange("p (t s) -> p t s", t=3)[:, 0:3:2, :]
                        ins = vec.copy_predicated(d, m, src[:, 2 * c * P:2 * (c + 1) * P].rearrange("p (t s) -> p t s", t=2))
                        if c == 0:
                            step(ins)
                    took(("lv", hf, lv, g), ins)
                settle()

            def fox_log_sigmoids():
                step(vec.memset(fones[:, :], 1.0))
                z = aux(("flog", 0))[:, 0:TT * HH].rearrange("p (t h) -> p t h", t=TT)
                took(("flog", 0), vec.tensor_tensor(flog[:, :, :], z, small["flb"][:, :].unsqueeze(1).to_broadcast([P, TT, HH]), ALU.add))
                vec.wait_ge(aux_taken[AUX["flog", 0][1]], AUX["flog", 0][2] + 1)
                step(vec.tensor_scalar(flmin[:, :, :], flog[:, :, :], 0.0, None, ALU.min))
                settle()
                vec.wait_ge(sem("flog_ln"), 1)
                vec.tensor_tensor(flog[:, :, :], flabs[:, :, :], flmin[:, :, :], ALU.subtract).then_inc(sem("flog_ready"), 1)

            for u in range(36):
                split_to(UNIT["win2"] + u + 3)
                j, half = divmod(u, 2)
                what = WIN2[j][0]
                c = slice((j % 2) * NB, (j % 2 + 1) * NB)
                if half:
                    if what == "q":
                        vec.wait_ge(sem("q_tanh"), j % 2 + 1)
                        d = stage[:, j % 2, :, :]
                        took_block("win2", j, vec.scalar_tensor_tensor(d, d, 1.0, block_values("win2", j), ALU.add, ALU.mult))
                    elif what == "g":
                        vec.wait_ge(sem("g_tanh"), j % 2 + 1)
                        d = hg[:, :, c]
                        took_block("win2", j, vec.scalar_tensor_tensor(d, d, 1.0, block_values("win2", j), ALU.add, ALU.mult))
                    elif what == "gate":
                        g = (j - 14) // 2
                        bias = gain(f"gate{g}")[:, c].unsqueeze(1).to_broadcast([P, TT, NB])
                        took_block("win2", j, vec.tensor_tensor(gate[g][:, :, c], block_values("win2", j), bias, ALU.add))
                elif j and WIN2[j - 1][0] == "f":
                    k = (j - 1) % 2
                    if k:
                        vec.wait_ge(sem("f_log"), k)
                    for g in range(2):
                        src = aux(("fT", 2 * k + g))
                        for c in range(2):
                            h = HALF * k + 2 * g + c
                            ins = vec.tensor_scalar(he[:, 2 * g + c, :], src[:, c * S:(c + 1) * S], lb[:, 1, h:h + 1],
                                                    lb[:, 0, h:h + 1], ALU.mult, ALU.add)
                            if c == 0:
                                step(ins)
                        took(("fT", 2 * k + g), ins)
                    settle()
                    for g in range(2):
                        vec.wait_ge(aux_taken[AUX["fT", 2 * k + g][1]], AUX["fT", 2 * k + g][2] + 1)
                    vec.tensor_scalar(hk[:, HALF * k:HALF * k + HALF, :], he[:, :, :], -1.0, 1.0, ALU.mult, ALU.add)\
                        .then_inc(sem("f_ready"), 1)
                    vec.wait_ge(sem("f_log"), k + 1)
                    for h in range(HALF * k, HALF * k + HALF):
                        step(vec.tensor_tensor_scan(hb[:, h, :], scanstart[:, :], hb[:, h, :], 0.0, ALU.mult, ALU.add))
                    settle()
                if u == 2:
                    fox_log_sigmoids()
                if u == 3:
                    src = ps[0:HH, AUX["flog", 1][1], 0:S]
                    aux(("flog", 1))
                    took(("flog", 1), vec.tensor_tensor_scan(fcum[:, :], fones[:, :], src, 0.0, ALU.mult, ALU.add))
                for n in HG_SLOT[u]:
                    hf, lv = HG_STEPS[n]
                    if lv == 0:
                        for g in range(2):
                            key = ("qT", 2 * hf + g)
                            vec.wait_ge(aux_taken[AUX[key][1]], AUX[key][2] + 1)
                        if hf:
                            vec.wait_ge(aux_done, AUX["hgo", 0, 1][0] + 1)
                        vec.memset(ha[:, :, :], 0.0).then_inc(sem("level_ready"), 1)
                    else:
                        apply_decays(n)
                    if n + 1 < len(HG_STEPS) and HG_STEPS[n + 1][1]:
                        diff(n + 1)
                    if lv == 0:
                        vec.wait_ge(sem("level_ready"), n + 1)
                    place_scores(n)
                    if lv == 128:
                        for tt in range(TT):
                            took(("hgo", hf, tt), vec.tensor_copy(ho[:, hf, tt, :], aux(("hgo", hf, tt))))
                if u == 24:
                    r = [recip_roots("hg", tt) for tt in range(TT)]
                    n = NS["hg"]
                    step(vec.tensor_scalar(recips[:, n:n + TT], recips[:, n:n + TT], 0.5, None, ALU.mult))
                    settle()
                    g = gain("hg_norm")
                    for n in range(2):
                        vec.wait_ge(pair_taken[n], taken("win2", 10 + n)[1])
                    for tt in range(TT):
                        o = ho[:, :, tt, :]
                        step(vec.scalar_tensor_tensor(o, o, r[tt], halves(g), ALU.mult, ALU.mult))
                        settle()
                        vec.tensor_tensor(o, o, halves(hg[:, tt, :]), ALU.mult).then_inc(sem("oa_ready"), 1)
                for n in FOX_SLOT[u]:
                    if n < HH:
                        src = aux(("fs", n))
                        for tt in range(TT):
                            c0, c1 = (0, P) if tt == 0 else (P, P + S)
                            ins = vec.tensor_reduce(small["negmax"][:, n, tt:tt + 1], src[:, c0:c1], AX_X, ALU.max, negate=True)
                            ins.then_inc(sem("fox_max"), 1)
                    if n >= 2:
                        attention_out(("fs", n - 2), ("fo", n - 2), fo[:, n - 2, :, :], P, n - 2)

            split_to(UNIT["brA"] + 2)
            token_groups("oa")
            split_to(UNIT["brA"] + 4)
            split_to(UNIT["brB"] + 2)
            for g in range(2):
                vec.wait_ge(sem("gate_tanh"), 2 * g + 2)
                step(vec.tensor_scalar(gate[g][:, :, :], gate[g][:, :, :], 0.5, 0.5, ALU.mult, ALU.add))
            settle()
            for j in range(2):
                d = gate[0][:, :, j * NB:(j + 1) * NB]
                took_block("brA", j, vec.tensor_tensor(d, d, block_values("brA", j), ALU.mult))
            token_groups("ob")
            for tt in range(TT):
                r, g = recip_roots("mem_kv", tt), gain("mem_kv")
                vec.scalar_tensor_tensor(mem[:, tt, :], mem[:, tt, :], r, g, ALU.mult, ALU.mult)\
                    .then_inc(sem("mem_normed"), 1)
            split_to(UNIT["brB"] + 4)
            split_to(UNIT["wout2"] + 2)
            for j in range(2):
                c = slice(j * NB, (j + 1) * NB)
                d = gate[1][:, :, c]
                took_block("brB", j, vec.tensor_tensor(d, d, block_values("brB", j), ALU.mult))
                vec.wait_ge(pair_taken[j], taken("brB", j)[1])
                vec.tensor_tensor(y[:, :, c], gate[0][:, :, c], d, ALU.add).then_inc(sem("y2_ready"), 1)
            token_groups("memn", mt_high, mt_rest)
            token_groups("y2")
            split_to(UNIT["wout2"] + 4)
            split_to(UNIT["mkv"] + 2)
            for tt in range(TT):
                post_norm("mix_post", 1.0, tt)
                pre_norm("mem_pre", tt)
            split_to(UNIT["mkv"] + 4)

            split_to(UNIT["mkv"] + 10)
            token_groups("mpre")
            split_to(UNIT["mq"] + 4)
            split_to(UNIT["mo"] + 2)
            for n in range(MH + 2):
                if n < MH:
                    src = aux(("ms", n)).rearrange("p (t s) -> p t s", t=TT)
                    vec.tensor_reduce(small["negmax"][:, n, :], src, AX_X, ALU.max, negate=True).then_inc(sem("mem_max"), 1)
                if n >= 2:
                    attention_out(("ms", n - 2), ("mo", n - 2), mo[:, :, (n - 2) * S:(n - 1) * S], S, n - 2)
            split_to(UNIT["mo"] + 4)
            token_groups("om")
            split_to(UNIT["upB"] + 2)
            post_norm("mem_post", 1.0, 0)
            gained("ffn2_pre", "mem_post", 0)
            post_norm("mem_post", 1.0, 1)
            tile_groups("f2", 0)
            gained("ffn2_pre", "mem_post", 1)
            tile_groups("f2", 1)
            ffn("upB", "downB", "hB", "ffn2_pre", "end")
            for tt in range(TT):
                post_norm("ffn2_post", 0.5, tt)
            assert split[0] == UNIT["end"]


def constants():
    f32 = np.float32
    tok = np.arange(S)
    out = {"c_ident": np.eye(P, dtype=f32), "c_identb": np.eye(P, dtype=f32).astype(np.dtype("bfloat16"))}
    causal = np.where(np.arange(P)[None, :] <= np.arange(P)[:, None], 0.0, NEG).astype(f32)
    out["c_causal"] = causal.astype(np.dtype("bfloat16"))
    starts = np.broadcast_to((tok % CHUNK != 0).astype(f32), (P, S))
    out["c_starts"] = np.ascontiguousarray(starts).astype(np.dtype("bfloat16"))
    s, t = np.arange(P)[:, None], np.arange(P)[None, :]
    levels = [s == t] + [(s // (2 * n) == t // (2 * n)) & (s % (2 * n) < n) & (t % (2 * n) >= n) for n in LEVELS]
    out["c_levels"] = np.ascontiguousarray(np.stack(levels, 1).astype(f32))
    gamma = 1.0 - 2.0 ** (-5.0 - np.arange(RH))
    i, j = tok[None, :], tok[:, None]
    seen = (i // CHUNK >= j // CHUNK)
    full = np.where(seen, gamma[:, None, None] ** np.abs(i - j), 0.0) * P ** -0.5
    decay = np.concatenate([full[:, 0:P, :], full[:, P:S, P:S]], axis=2)
    out["c_decay"] = np.ascontiguousarray(decay.transpose(1, 0, 2).astype(f32))
    win = []
    for w in (2, 4, 8, 16):
        m = ((j <= i) & (j > i - w)) / np.minimum(i + 1, w) - (i == j)
        win.append(m)
    win = np.stack(win).reshape(RH, TT, P, S).transpose(2, 1, 0, 3)
    out["c_window"] = np.ascontiguousarray(win.astype(f32))
    inv = (f32(10000.0) ** (-np.arange(0, P, 2, dtype=f32) / f32(P))).astype(f32)
    ang = (tok.astype(f32)[:, None] * inv[None, :]).astype(f32).astype(np.float64)
    cos, sin = np.cos(ang), np.sin(ang)
    for name, a, b in (("c_ropec", cos, cos), ("c_ropes", -sin, sin)):
        v = np.concatenate([a, b], axis=1).reshape(TT, P, P).transpose(1, 0, 2)
        out[name] = np.ascontiguousarray(v.astype(f32))
    return out


_VECTORS = {"ln1_g": "ln1_g", "ln1_b": "ln1_b", "ln2_g": "ln2_g", "ln2_b": "ln2_b",
            "ffn1_pre": "ffn1_pre_g_2", "ffn1_post": "ffn1_post_g_2", "mix_pre": "mix_pre_g_2",
            "hg_norm": "hg_norm_g_2", "mem_kv": "mem_kv_g_2", "mix_post": "mix_post_g_2",
            "mem_pre": "mem_pre_g_2", "mem_post": "mem_post_g_2", "ffn2_pre": "ffn2_pre_g_2",
            "ffn2_post": "ffn2_post_g_2"}
_WEIGHTS = ["w_in", "w_out", "w_up", "w_down", "ffn1_w_in_2", "ffn1_w_down_2", "w_in_2", "w_branch_a_2",
            "w_branch_b_2", "w_out_2", "w_mq_2", "w_mkv_2", "w_mo_2", "ffn2_w_in_2", "ffn2_w_down_2", "w_pool"]


def kernel(**inputs):
    import concourse.bacc as _bacc
    from concourse.bass_utils import run_bass_kernel_spmd as _run

    nc = _bacc.Bacc("TRN2", target_bir_lowering=False, num_devices=1)
    laid = {name: np.asarray(inputs[name])[0] for name in _WEIGHTS}
    laid["x"] = np.asarray(inputs["x"])[0]
    laid["mem_2"] = np.asarray(inputs["mem_2"])[0]
    for name, src in _VECTORS.items():
        laid["gain_" + name] = np.asarray(inputs[src])[0]
    bias = np.asarray(inputs["b_gate_2"])[0]
    laid["gain_gate0"], laid["gain_gate1"] = bias[:D], bias[D:]
    laid["fox_f_bias_2"] = np.asarray(inputs["fox_f_bias_2"])[0]
    laid["conv_w"] = np.asarray(inputs["conv_w"])[0].reshape(3, FC, P).transpose(2, 1, 0)
    laid["conv_b"] = np.asarray(inputs["conv_b"])[0].reshape(FC, P).T
    laid["pool_scale"] = np.asarray(inputs["pool_scale"])[0].reshape(RH, P).T
    laid["hg_lb_logits_2"] = np.asarray(inputs["hg_lb_logits_2"]).transpose(2, 0, 1)
    laid.update(constants())
    arrays, dram = {}, {}
    for name, a in laid.items():
        a = np.ascontiguousarray(a)
        arrays[f"in_{name}_dram"] = a
        dram[name] = nc.dram_tensor(f"in_{name}_dram", a.shape, mybir.dt.from_np(a.dtype), kind="ExternalInput").ap()
    out = nc.dram_tensor("out_0_dram", (S, D), F32, kind="ExternalOutput").ap()
    build(nc, dram, out)
    r = _run(nc, [arrays], core_ids=[0])
    return r.results[0]["out_0_dram"].reshape(1, S, D)
```

```python
from contextlib import ExitStack, contextmanager

import numpy as np

import concourse.bass as bass
from concourse import mybir

ALU = mybir.AluOpType
ACT = mybir.ActivationFunctionType
F32 = mybir.dt.float32
F32R = mybir.dt.float32r
BF16 = mybir.dt.bfloat16
U8 = mybir.dt.uint8
AX_X = mybir.AxisListType.X

P = 128
S = 256
TT = S // P
D = 1024
KC = D // P
NB = 512
RH = 4
FF = 2816
FC = FF // P
FB = FF // 256
CHUNK = 64
HH = 8
HALF = HH // 2
MH = 4
ALPHA = 2.0 ** 0.25
LN_EPS, RMS_EPS = 1e-5, 1e-6
SLOTS = 4
GSLOTS = 3
LEVELS = (1, 2, 4, 8, 16, 32, 64)
NEG = -1e30

GAINS = ("ln1_g", "ln1_b", "ln2_g", "ln2_b", "ffn1_pre", "ffn1_post", "mix_pre", "hg_norm", "gate0",
         "gate1", "mem_kv", "mix_post", "mem_pre", "mem_post", "ffn2_pre", "ffn2_post")
NORMS = ("ret0", "ret1", "ret2", "ret3", "ln1", "ln2", "ffn1_pre", "ffn1_post", "mix_pre", "hg",
         "mem_kv", "mix_post", "mem_pre", "mem_post", "ffn2_pre", "ffn2_post")
BLOCKS = (("win1", 5), ("wout1", 2), ("up1", FB), ("down1", 0), ("upA", FB), ("downA", 0),
          ("win2", 18), ("brA", 2), ("brB", 2), ("mk", 2), ("wout2", 2), ("mv", 2), ("mq", 2), ("mo", 2),
          ("upB", FB), ("downB", 0))
WIN1 = (("q", 0), ("k", 512), ("p", 2048), ("v", 1024), ("g", 1536))
WIN2 = (("f", 1024), ("f", 1536), ("q", 0), ("q", 512), ("i", 2048), ("i", 2560),
        ("fq", 4096), ("fq", 4608), ("fk", 5120), ("fk", 5632), ("fv", 6144), ("fv", 6656),
        ("g", 3072), ("g", 3584), ("gate", 7176), ("gate", 7688), ("gate", 8200), ("gate", 8712))
FLOGIT = 7168
HG_STEPS = tuple((hf, lv) for hf in range(2) for lv in (0, *LEVELS, 128))
HG_SLOT = {u: [] for u in range(36)}
for _n, _step in enumerate(HG_STEPS):
    _hf, _k = divmod(_n, len(HG_STEPS) // 2)
    HG_SLOT[8 + len(HG_STEPS) // 2 * _hf + _k].append(_n)
FOX_SLOT = {u: [] for u in range(36)}
for _n in range(HH + 2):
    FOX_SLOT[26 + _n].append(_n)
OA_SLOT = {30 + _g: _g for _g in range(4)}


class Turns:

    def __init__(self, engine):
        self.engine, self.turn = engine, None

    def __call__(self, n, more):
        return n if self.turn is None or more == 0 else self.turn * more + n

    @contextmanager
    def loop(self, times, *counts):
        before = [c[0] for c in counts]
        with self.engine.Fori(0, times) as turn:
            self.turn = turn
            yield
            self.turn = None
        for c, n in zip(counts, before):
            c[0] += (c[0] - n) * (times - 1)


PAIRS = (FB - 1) // 2
CONV_PAIRS = PAIRS - 1


def two_on(key):
    return key[0], key[1] + 2


def unit_starts():
    out, n = {}, 0
    for name, k in BLOCKS:
        out[name] = n
        n += 2 * k if k else FB
    out["end"] = n
    return out


def pair_plan():
    out, used = {}, [0, 0]
    for name, k in BLOCKS:
        for j in range(k or 2):
            out[name, j] = (j % 2, used[j % 2])
            used[j % 2] += 1
    return out


MEM_ORDER = (("mqT", 0), ("mqT", 1), ("ms", 0), ("ms", 1), ("mqT", 2), ("mqT", 3), ("mp", 0), ("ms", 2),
             ("mo", 0), ("mp", 1), ("ms", 3), ("mo", 1), ("om", 0), ("om", 2), ("mp", 2), ("mp", 3),
             ("mo", 2), ("mo", 3), ("om", 1), ("om", 3))


def aux_plan():
    order, out, used = [], {}, [0] * 8

    def use(key, bank=None):
        n = len(order)
        bank = 4 + n % 4 if bank is None else bank
        order.append(key)
        out[key] = (n, bank, used[bank])
        used[bank] += 1

    def splits(name, n=4):
        for g in range(n):
            use((name, g))

    splits("x")
    for what in "qk":
        for g in range(2):
            use(("rT" + what, g))
    for g in range(2):
        use(("poolT", g))
    for h in range(RH):
        use(("rscore", h))
    for g in range(2):
        use(("pooly", g))
    for tt in range(TT):
        use(("rout", tt))
    splits("mixr", 2)
    splits("x1")
    for j in range(FB):
        use(("convg", j), 6)
        use(("convv", j), 7)
    splits("f1")
    for j in range(FB):
        use(("hA", j), 4 + j % 2)
    splits("m2")
    for u in range(36):
        j, last = u // 2, u % 2 == 1
        if u == 1:
            use(("flog", 0))
        if u == 7:
            use(("flog", 1))
        if u >= 2 and last and WIN2[j - 1][0] in ("f", "q", "fq", "fk"):
            for g in range(2):
                use((WIN2[j - 1][0] + "T", 2 * ((j - 1) % 2) + g))
        for n in HG_SLOT[u]:
            hf, lv = HG_STEPS[n]
            for g in range(1 if lv else 2):
                use(("lv", hf, lv, g))
            if lv == 128:
                for tt in range(TT):
                    use(("hgo", hf, tt))
        if u in OA_SLOT:
            use(("oa", OA_SLOT[u]))
        for n in FOX_SLOT[u]:
            if n < HH:
                use(("fs", n))
            if 1 <= n < HH + 1:
                use(("fp", n - 1))
            if n >= 2:
                use(("fo", n - 2))
    splits("ob")
    splits("memn")
    splits("y2")
    for g in range(4):
        use(("mkT", g))
    splits("mpre")
    for key in MEM_ORDER:
        use(key)
    splits("f2")
    for j in range(FB):
        use(("hB", j), 4 + j % 2)
    return out


HALVES = {"wout1": (1, 0), "mo": (0, 1)}
UNIT = unit_starts()
PAIR = pair_plan()
AUX = aux_plan()
NS = {name: TT * n for n, name in enumerate(NORMS)}
NS["mix_half"] = NS["ret0"]


def build(nc, dram, out_dram):
    ctx = ExitStack()
    with ctx:
        nc_sem = {}

        def sem(name):
            if name not in nc_sem:
                nc_sem[name] = ctx.enter_context(nc.semaphore(name))
            return nc_sem[name]

        base = -(-nc.sbuf_base // 32) * 32
        top = nc.sbuf_top
        marks = {}

        def place(name, shape, dt, at):
            size = int(np.prod(shape[1:])) * {F32: 4, F32R: 4, BF16: 2, U8: 1}[dt]
            marks[name] = (at, at + size)
            assert base <= at and at + size <= top, (name, at, size, top)
            return nc.alloc_sbuf_tensor_at(name, shape, dt, offset=at)

        KB = 1024
        raw = place("raw", [P, SLOTS, 4 * NB], F32, base)
        high = place("high", [P, SLOTS, 4 * NB], F32R, base + 32 * KB)
        rest = place("rest", [P, SLOTS, 4 * NB], F32R, base + 64 * KB)
        x = place("x", [P, TT, D], F32, base + 96 * KB)
        y = place("y", [P, TT, D], F32, base + 104 * KB)
        xt_high = place("xt_high", [P, KC, S], F32R, base + 112 * KB)
        xt_rest = place("xt_rest", [P, KC, S], F32R, base + 120 * KB)
        gains = place("gains", [P, GSLOTS, D], F32, base + 128 * KB)
        at = base + 140 * KB
        small = {}
        for name, shape, dt in (
            ("ident", [P, P], F32), ("identb", [P, P], BF16), ("causal", [P, P], BF16),
            ("levelmask", [P, 8, P], U8), ("starts", [P, S], BF16),
            ("sums", [P, TT * len(NORMS)], F32), ("roots", [P, TT * len(NORMS)], F32),
            ("recips", [P, TT * len(NORMS)], F32), ("moments", [P, TT, 12], F32),
            ("meanvar", [P, TT, 2], F32), ("identr", [P, HH], F32R), ("eps", [P, 2 + 2 * TT], F32), ("lbl", [P, 2, HH], F32),
            ("lb", [P, 4, HH], F32), ("flb", [P, HH], F32), ("negmax", [P, HH, 2], F32),
            ("expsum", [P, HH, 2], F32), ("crossref", [P, HALF], F32), ("convw", [P, FC * 3], F32),
            ("convb", [P, FC], F32), ("pscale", [P, 4], F32)):
            small[name] = place(name, shape, dt, at)
            at = -(-marks[name][1] // 32) * 32
        identr = small["identr"]
        partsum = small["eps"][:, 2:2 + 2 * TT].rearrange("p (a t) -> p a t", a=2)
        ident, identb, causal = small["ident"], small["identb"], small["causal"]
        levelmask, scanstart = small["levelmask"], small["starts"]
        sums, roots, recips = small["sums"], small["roots"], small["recips"]
        moments, meanvar, eps = small["moments"], small["meanvar"], small["eps"]
        area = -(-at // 32) * 32

        junk_a = place("junk_a", [P, TT, D], F32, area)
        ht_high = place("ht_high", [P, FC, S], F32R, area)
        ht_rest = place("ht_rest", [P, FC, S], F32R, area + 22 * KB)
        gv = place("gv", [P, 2, TT, NB], F32, area + 44 * KB)
        conv = place("conv", [P, 2, 2, S], F32, area + 52 * KB)
        convs = place("convs", [P, 2, S], F32, area + 56 * KB)
        act_ = place("act", [P, 2, TT, 256], F32, area + 44 * KB)
        hid = place("hid", [P, 2, TT, 256], F32, area + 48 * KB)

        rq = place("rq", [P, TT, NB], F32, area)
        rk = place("rk", [P, TT, NB], F32, area + 4 * KB)
        rv = place("rv", [P, TT, NB], F32, area + 8 * KB)
        rg = place("rg", [P, TT, NB], F32, area + 12 * KB)
        rp = place("rp", [P, TT, NB], F32, area + 16 * KB)
        ra = place("ra", [P, TT, NB], F32, area + 20 * KB)
        pooly = place("pooly", [P, RH, S], F32, area + 20 * KB)
        rqT = place("rqT", [P, RH, S], F32, area + 24 * KB)
        rkT = place("rkT", [P, RH, S], F32, area + 28 * KB)
        rsc = place("rsc", [P, RH, 384], F32, area + 32 * KB)
        decay = place("decay", [P, RH, 384], F32, area + 38 * KB)
        window = place("window", [P, TT, RH, S], F32, area + 44 * KB)
        ropec = place("ropec", [P, TT, P], F32, area + 52 * KB)
        ropes = place("ropes", [P, TT, P], F32, area + 53 * KB)
        wpool = place("wpool", [P, RH, P], F32, area + 54 * KB)
        pooled = place("pooled", [P, RH, S], F32, area + 56 * KB)
        pool_high = place("pool_high", [P, RH, S], F32R, base + 104 * KB)
        pool_rest = place("pool_rest", [P, RH, S], F32R, base + 108 * KB)
        rout = place("rout", [P, TT, NB], F32, area)
        rsq = place("rsq", [P, TT, NB], F32, area + 4 * KB)

        hq = place("hq", [P, HH, S], F32, area)
        hk = place("hk", [P, HH, S], F32, area + 8 * KB)
        hb = place("hb", [P, HH, S], F32, area + 16 * KB)
        he = place("he", [P, HALF, S], F32, area + 24 * KB)
        hqk = place("hqk", [P, HALF, S], F32, area + 28 * KB)
        ha = place("ha", [P, HALF, 384], F32, area + 32 * KB)
        hi_ = place("hi", [P, TT, D], F32, area + 38 * KB)
        fqT = place("fqT", [P, HH, S], F32, area + 46 * KB)
        fkT = place("fkT", [P, HH, S], F32, area + 54 * KB)
        stage = place("stage", [P, 2, TT, NB], F32, base + 104 * KB)
        fv = place("fv", [P, TT, D], F32, base + 104 * KB)
        ho = place("ho", [P, 2, TT, NB], F32, area)
        hg = place("hg", [P, TT, D], F32, area + 16 * KB)
        gate = [place("gate0", [P, TT, D], F32, area + 8 * KB),
                place("gate1", [P, TT, D], F32, area + 24 * KB)]
        fp = place("fp", [P, 2, 384], F32, area + 32 * KB)
        fpT = place("fpT", [P, 2, 384], F32, area + 35 * KB)
        fo = place("fo", [P, HH, TT, P], F32, area + 46 * KB)
        levels32 = place("levels32", [P, 8, P], F32, area + 54 * KB)
        wf_raw = place("wf_raw", [P, KC, HH], F32, area + 62 * KB)
        wf_high = place("wf_high", [P, KC, HH], F32R, area + 62 * KB + 256)
        wf_rest = place("wf_rest", [P, KC, HH], F32R, area + 62 * KB + 512)
        flog = place("flog", [P, TT, HH], F32, area + 62 * KB + 768)
        flabs = place("flabs", [P, TT, HH], F32, area + 62 * KB + 832)
        flmin = place("flmin", [P, TT, HH], F32, area + 62 * KB + 896)
        fcum = place("fcum", [HH, S], F32, area + 41 * KB)
        fones = place("fones", [HH, S], F32, area + 40 * KB)
        junk_h = place("junk_h", [P, TT, D], F32, area + 38 * KB)

        at_high = place("at_high", [P, KC, S], F32R, area + 38 * KB)
        at_rest = place("at_rest", [P, KC, S], F32R, area + 16 * KB)
        fcum_high = place("fcum_high", [HH, S], F32R, area + 63 * KB)
        fcum_rest = place("fcum_rest", [HH, S], F32R, area + 62 * KB)

        junk_m = place("junk_m", [P, TT, NB], F32, area + 8 * KB)
        mem = place("mem", [P, TT, D], F32, area + 54 * KB)
        mt_high = place("mt_high", [P, KC, S], F32R, area + 38 * KB)
        mt_rest = place("mt_rest", [P, KC, S], F32R, area + 16 * KB)
        kstage = place("kstage", [P, TT, D], F32, area)
        mkT = place("mkT", [P, KC, S], F32, area + 46 * KB)
        mv = place("mv", [P, TT, D], F32, area + 8 * KB)
        qstage = place("qstage", [P, TT, D], F32, area + 24 * KB)
        mqT = place("mqT", [P, KC, S], F32, area + 54 * KB)
        mo = place("mo", [P, TT, D], F32, area)
        mp = [place("mp0", [P, TT, S], F32, area + 32 * KB),
              place("mp1", [P, TT, S], F32, area + 62 * KB)]
        mpT = [place("mpT0", [P, TT, TT * S // 2], F32, area + 34 * KB),
               place("mpT1", [P, TT, TT * S // 2], F32, area + 24 * KB)]

        ps = ctx.enter_context(nc.psum_tensor("ps", [P, 8, NB], F32))
        pair_of = [ps[:, 2 * n:2 * n + 2, :] for n in range(2)]

        unit_landed = [sem(f"unit_landed{n}") for n in range(SLOTS)]
        unit_high, unit_rest, unit_used = sem("unit_high"), sem("unit_rest"), sem("unit_used")
        pair_taken = [sem(f"pair_taken{n}") for n in range(2)]
        aux_done = sem("aux_done")
        aux_taken = [None] * 4 + [sem(f"aux_taken{n}") for n in range(4, 8)]
        group_high = sem("group_high")
        gain_landed = [sem(f"gain_landed{n}") for n in range(GSLOTS)]
        x_landed, consts1_landed, consts2_landed = sem("x_landed"), sem("consts1_landed"), sem("consts2_landed")
        mem_landed, out_stored, levels_landed = sem("mem_landed"), sem("out_stored"), sem("levels_landed")
        eps_ready = sem("eps_ready")
        roots_ready = sem("roots_ready")
        tile_done = sem("tile_done")
        x_ready = sem("x_ready")
        normed = sem("normed")
        rope_landed = sem("rope_landed")
        CONSTS1, CONSTS2 = 8, 4

        ROOT_ORDER = (("ret", 0),) + tuple((name, tt) for names in (
            ("ln1",), ("ln2",), ("ffn1_pre",), ("ffn1_post",), ("mix_pre",), ("hg",), ("mem_kv",), ("mix_post", "mem_pre"),
            ("mem_post",), ("ffn2_pre",), ("ffn2_post",)) for tt in range(TT) for name in names)
        root_count = {key: n + 1 for n, key in enumerate(ROOT_ORDER)}
        tile_count = {name: n + 1 for n, name in enumerate(("wout1", "down1", "downA", "wout2", "mo", "downB"))}
        x_count = {name: 2 * TT * (n + 1) for n, name in
                   enumerate(("ln1", "ln2", "ffn1_post", "mix_post", "mem_post", "ffn2_post"))}
        normed_count = {name: 2 * TT * (n + 1) for n, name in
                        enumerate(("ffn1_pre", "mix_pre", "mem_pre", "ffn2_pre"))}

        def x_at(name, tt, q=1):
            return x_count[name] - 2 * TT + 2 * tt + q + 1

        def normed_at(name, tt, q=1):
            return normed_count[name] - 2 * TT + 2 * tt + q + 1

        def gain_free(name):
            if name.startswith("ln"):
                return x_ready, x_count[name[:3]]
            if name in normed_count:
                return normed, normed_count[name]
            if name in x_count:
                return x_ready, x_count[name]
            if name == "hg_norm":
                return sem("oa_ready"), TT
            if name == "mem_kv":
                return sem("mem_normed"), TT
            j = 15 if name == "gate0" else 17
            return pair_taken[j % 2], PAIR["win2", j][1] + 1

        def taken(name, j):
            n, used = PAIR[name, j]
            return n, used + 1

        def filled(name, j):
            if name in HALVES:
                return UNIT[name] + 4
            if dict(BLOCKS)[name]:
                return UNIT[name] + 2 * j + 2
            return UNIT[name] + FB

        block = ctx.enter_context(nc.Block())

        @block.sync
        def _(sync):
            sync.dma_start(small["ident"][:, :], dram["c_ident"]).then_inc(x_landed, 16)
            sync.dma_start(x[:, :, :], dram["x"].rearrange("(t p) c -> p t c", p=P)).then_inc(x_landed, 16)

            turns = Turns(sync)

            def load(u, parts):
                slot = u % SLOTS
                if u >= SLOTS:
                    sync.wait_ge(unit_rest, turns(u - SLOTS + 1, SLOTS))
                for dst, src in parts(raw[:, slot, :]):
                    sync.dma_start(dst, src).then_inc(unit_landed[slot], 16)

            def load_block(units, w, c0, halves=(0, 1)):
                wv = w.rearrange("(k p) n -> p k n", p=P)
                for u, half in zip(units, halves):
                    k = 4 * half
                    load(u, lambda d: [(d.rearrange("p (k n) -> p k n", k=4)[:, n:n + 2, :],
                                        wv[:, k + n:k + n + 2, c0:c0 + NB]) for n in (0, 2)])

            def load_up(u, w, j):
                wv = w.rearrange("(k p) n -> p k n", p=P)
                for half in range(2):
                    k = 4 * half
                    load(u + half, lambda d: [(d.rearrange("p (k g n) -> p k g n", k=4, g=2)[:, :, g, :],
                                               wv[:, k:k + 4, bass.ds(turns(g * FF + 256 * j, 512), 256)])
                                              for g in range(2)])

            def load_down(u, w, i):
                load(u, lambda d: [(d[:, k * D:(k + 1) * D], w[bass.ds(turns((2 * i + k) * P, SLOTS * 2 * P), P), :])
                                   for k in range(2)])

            for name, k in BLOCKS:
                w = dram[{"win1": "w_in", "wout1": "w_out", "up1": "w_up", "down1": "w_down",
                          "upA": "ffn1_w_in_2", "downA": "ffn1_w_down_2", "win2": "w_in_2",
                          "brA": "w_branch_a_2", "brB": "w_branch_b_2", "wout2": "w_out_2",
                          "mk": "w_mkv_2", "mv": "w_mkv_2", "mq": "w_mq_2", "mo": "w_mo_2", "upB": "ffn2_w_in_2",
                          "downB": "ffn2_w_down_2"}[name]]
                u = UNIT[name]
                if name in HALVES:
                    for n, half in enumerate(HALVES[name]):
                        for j in range(2):
                            load_block((u + 2 * n + j,), w, j * NB, (half,))
                    continue
                if name.startswith("up"):
                    load_up(u, w, 0)
                    with turns.loop(PAIRS):
                        for j in (1, 2):
                            load_up(u + 2 * j, w, j)
                    continue
                if name.startswith("down"):
                    with turns.loop(FB // SLOTS):
                        for i in range(SLOTS):
                            load_down(u + i, w, i)
                    for i in range(FB // SLOTS * SLOTS, FB):
                        load_down(u + i, w, i)
                    continue
                for j in range(k):
                    c0 = ({"win1": WIN1, "win2": WIN2}[name][j][1] if name.startswith("win") else
                          j * NB + (D if name == "mv" else 0))
                    load_block((u + 2 * j, u + 2 * j + 1), w, c0)
            for tt in range(TT):
                for q in range(2):
                    c = slice(q * NB, (q + 1) * NB)
                    sync.wait_ge(x_ready, x_at("ffn2_post", tt, q))
                    sync.dma_start(out_dram[tt * P:(tt + 1) * P, c], x[:, tt, c]).then_inc(out_stored, 16)
            sync.wait_ge(out_stored, 16 * 2 * TT)

        @block.gpsimd
        def _(pool):
            pool.wait_ge(unit_landed[SLOTS - 1], 32)
            for t, src in ((ropec, "c_ropec"), (ropes, "c_ropes")):
                pool.dma_start(t[:], dram[src]).then_inc(rope_landed, 16)
            for t, src in ((window, "c_window"), (decay, "c_decay"), (small["pscale"], "pool_scale")):
                pool.dma_start(t[:], dram[src]).then_inc(consts1_landed, 16)
            pool.dma_start(wpool[:, :, :], dram["w_pool"].rearrange("g c d -> c g d")).then_inc(consts1_landed, 16)
            pool.wait_ge(rope_landed, 32)
            rotated = sem("rotated")
            by_head = lambda ap: ap.rearrange("p t (h d) -> p t h d", h=RH)

            def rotate(j, dst):
                pool.wait_ge(pair_taken[j], taken("win1", j)[1])
                if j:
                    pool.wait_ge(sem("rope_done"), j)
                s4, a4, d4 = by_head(stage[:, j, :, :]), by_head(ra[:, :, :]), by_head(dst[:, :, :])
                for tt in range(TT):
                    c4 = ropec[:, tt, :].unsqueeze(1).to_broadcast([P, RH, P])
                    pool.tensor_tensor(d4[:, tt], s4[:, tt], c4, ALU.mult).then_inc(rotated, 1)
                    for half in range(2):
                        o = slice(half * 64, half * 64 + 64)
                        i = slice(64 - half * 64, 128 - half * 64)
                        sn = ropes[:, tt, o].unsqueeze(1).to_broadcast([P, RH, 64])
                        pool.tensor_tensor(a4[:, tt, :, o], s4[:, tt, :, i], sn, ALU.mult).then_inc(rotated, 1)
                pool.wait_ge(rotated, 3 * TT * (j + 1))
                pool.tensor_tensor(dst[:, :, :], dst[:, :, :], ra[:, :, :], ALU.add).then_inc(sem("rope_done"), 1)

            rotate(0, rq)
            for name, src in (("convw", "conv_w"), ("convb", "conv_b"), ("causal", "c_causal"), ("starts", "c_starts")):
                pool.dma_start(small[name][:], dram[src]).then_inc(consts1_landed, 16)
            rotate(1, rk)
            pool.dma_start(small["lbl"][:, :, :], dram["hg_lb_logits_2"]).then_inc(consts2_landed, 16)
            pool.dma_start(small["flb"][:, :], dram["fox_f_bias_2"].partition_broadcast(P)).then_inc(consts2_landed, 16)
            pool.dma_start(wf_raw[:, :, :], dram["w_in_2"].rearrange("(k p) n -> p k n", p=P)
                           [:, :, FLOGIT:FLOGIT + HH]).then_inc(consts2_landed, 16)
            pool.dma_start(identb[:, :], dram["c_identb"]).then_inc(consts2_landed, 16)
            for n, name in enumerate(GAINS):
                if n >= GSLOTS:
                    pool.wait_ge(*gain_free(GAINS[n - GSLOTS]))
                if name == "hg_norm":
                    pool.dma_start(levels32[:, :, :], dram["c_levels"]).then_inc(levels_landed, 16)
                if name == "mem_kv":
                    pool.wait_ge(aux_done, AUX["fo", HH - 1][0] + 1)
                    pool.dma_start(mem[:, :, :], dram["mem_2"].rearrange("(t p) c -> p t c", p=P))\
                        .then_inc(mem_landed, 16)
                pool.dma_start(gains[:, n % GSLOTS, :], dram["gain_" + name].partition_broadcast(P))\
                    .then_inc(gain_landed[n % GSLOTS], 16)

        @block.tensor
        def _(pe):
            done = [0]
            turns = Turns(pe)

            def unit(u, products, wait=None):
                slot = u % SLOTS
                if u:
                    pe.wait_ge(unit_rest, turns(u + 1, SLOTS))
                for n, (sh, sr, c, out, first, last) in enumerate(products):
                    if u == 0 and n % TT == 0:
                        k = n // TT
                        pe.wait_ge(*((sem("lead_rest"), k + 1) if k < 3 else (unit_rest, 1)))
                    wh, wr = high[:, slot, c:c + NB], rest[:, slot, c:c + NB]
                    pe.matmul(out, sh, wh, start=first, stop=False)
                    pe.matmul(out, sh, wr, start=False, stop=False)
                    mm = pe.matmul(out, sr, wh, start=False, stop=last)
                mm.then_inc(unit_used, 1)

            def chunk_products(name, j, half, tt, th=xt_high, tr=xt_rest):
                n, _ = PAIR[name, j]
                if name == "wout1" and half == 0:
                    return [(pool_high[:, k, tt * P:(tt + 1) * P], pool_rest[:, k, tt * P:(tt + 1) * P], k * NB,
                             pair_of[n][:, tt, :], k == 0, False) for k in range(4)]
                at = HALVES.get(name, (0, 1))[half]
                return [(th[:, 4 * at + k, tt * P:(tt + 1) * P], tr[:, 4 * at + k, tt * P:(tt + 1) * P], k * NB,
                         pair_of[n][:, tt, :], half == 0 and k == 0, half == 1 and k == 3) for k in range(4)]

            def wait_pair(name, j):
                n, used = PAIR[name, j]
                if used:
                    pe.wait_ge(pair_taken[n], turns(used, 1))

            def half_block(name, j, half, th=xt_high, tr=xt_rest):
                if half == 0:
                    wait_pair(name, j)
                tiles = [chunk_products(name, j, half, tt, th, tr) for tt in range(TT)]
                unit(UNIT[name] + 2 * j + half, [tiles[tt][k] for k in range(4) for tt in range(TT)])

            def by_tiles(u, products, before=None, signal=False):
                for tt in range(TT):
                    for half in range(2):
                        slot = (u + half) % SLOTS
                        if tt == 0:
                            pe.wait_ge(unit_rest, u + half + 1)
                        if before:
                            before(tt, half)
                        for sh, sr, c, out, first, last in products(half, tt):
                            wh, wr = high[:, slot, c:c + NB], rest[:, slot, c:c + NB]
                            pe.matmul(out, sh, wh, start=first, stop=False)
                            pe.matmul(out, sh, wr, start=False, stop=False)
                            mm = pe.matmul(out, sr, wh, start=False, stop=last)
                        if tt == TT - 1:
                            mm.then_inc(unit_used, 1)
                        elif half == 1 and signal:
                            mm.then_inc(tile_done, 1)

            def first_block(name, key, src, ready):
                def before(tt, half):
                    if half == 0:
                        for q in range(2):
                            ready(tt, q)
                            transposes((key, 2 * tt + q), [src(tt, 4 * q + c) for c in range(4)])
                        if tt == 1:
                            wait_pair(name, 0)
                    wait_taken((key, 2 * tt + half))

                by_tiles(UNIT[name], lambda half, tt: chunk_products(name, 0, half, tt), before)

            def alternate(name, j):
                wait_pair(name, j)
                tiles = [chunk_products(name, j, 0, tt) for tt in range(TT)]
                unit(UNIT[name] + j, [tiles[tt][k] for k in range(4) for tt in range(TT)])

            def last_halves(name):
                by_tiles(UNIT[name] + 2, lambda j, tt: chunk_products(name, j, 1, tt), signal=True)

            def last_block(name, j):
                wait_pair(name, j)
                by_tiles(UNIT[name] + 2 * j, lambda half, tt: chunk_products(name, j, half, tt), signal=True)

            def full_block(name, j, th=xt_high, tr=xt_rest):
                half_block(name, j, 0, th, tr)
                half_block(name, j, 1, th, tr)

            def down_products(i, kc, tt):
                return [(ht_high[:, kc, tt * P:(tt + 1) * P], ht_rest[:, kc, tt * P:(tt + 1) * P],
                         (kc % 2) * 2 * NB + n * NB, pair_of[n][:, tt, :], kc == 0, kc == FC - 1) for n in range(2)]

            def down(name, i):
                if i == 0:
                    for n in range(2):
                        wait_pair(name, n)
                if i < FB - 2:
                    unit(UNIT[name] + i, [p for kc in (2 * i, 2 * i + 1) for tt in range(TT)
                                          for p in down_products(i, kc, tt)])
                elif i == FB - 1:
                    by_tiles(UNIT[name] + i - 1,
                             lambda half, tt: [p for kc in (2 * (i - 1 + half), 2 * (i - 1 + half) + 1)
                                               for p in down_products(i - 1 + half, kc, tt)], signal=True)

            def aux(key):
                n, bank, used = AUX[key]
                assert n == done[0], (key, n, done[0])
                done[0] += 1
                if used:
                    more = AUX[two_on(key)][2] - used if turns.turn is not None else 0
                    pe.wait_ge(aux_taken[bank], turns(used, more))
                return ps[:, bank, :]

            def wait_taken(*keys):
                for key in keys:
                    _, bank, used = AUX[key]
                    pe.wait_ge(aux_taken[bank], used + 1)

            def transposes(key, sources, then=None):
                out = aux(key)
                for n, src in enumerate(sources):
                    mm = pe.transpose(out[:, n * P:(n + 1) * P], src, ident[:, :])
                mm.then_inc(aux_done, 1)

            def token_groups(name, src, wait, kq=2):
                for g in range(TT * kq):
                    tt, q = divmod(g, kq)
                    wait(tt, q)
                    transposes((name, g), [src(tt, 4 * q + c) for c in range(4)])

            def from_x(tt, c):
                return x[:, tt, c * P:(c + 1) * P]

            def from_y(tt, c):
                return y[:, tt, c * P:(c + 1) * P]

            def head_pairs(name, src, g):
                transposes((name, g), [src[:, tt, c * P:(c + 1) * P]
                                       for c in (2 * (g % 2), 2 * (g % 2) + 1) for tt in range(TT)])

            pe.wait_ge(x_landed, 32)
            for g in range(4):
                transposes(("x", g), [from_x(g // 2, 4 * (g % 2) + c) for c in range(4)])
            wait_taken(*(("x", g) for g in range(4)))
            full_block("win1", 0)
            full_block("win1", 1)
            full_block("win1", 2)
            def rotated_transposes(n, what, src):
                pe.wait_ge(sem("rope_done"), n + 1)
                for g in range(2):
                    head_pairs("rT" + what, src, g)

            rotated_transposes(0, "q", rq)
            half_block("win1", 3, 0)
            rotated_transposes(1, "k", rk)
            pe.wait_ge(pair_taken[0], taken("win1", 2)[1])
            pe.wait_ge(consts1_landed, 16 * CONSTS1)
            for g in range(2):
                out = aux(("poolT", g))
                for c in range(2):
                    for tt in range(TT):
                        mm = pe.matmul(out[:, c * S:(c + 1) * S], rp[:, tt, (2 * g + c) * P:(2 * g + c + 1) * P],
                                       window[:, tt, 2 * g + c, :], start=(tt == 0), stop=(tt == TT - 1))
                mm.then_inc(aux_done, 1)
            half_block("win1", 3, 1)
            wait_taken(("rTq", 0), ("rTq", 1), ("rTk", 0), ("rTk", 1))
            for h in range(RH):
                out = aux(("rscore", h))
                pe.matmul(out[:, 0:S], rkT[:, h, 0:P], rqT[:, h, :], start=True, stop=True)
                pe.matmul(out[:, S:S + P], rkT[:, h, P:S], rqT[:, h, P:S], start=True, stop=True)\
                    .then_inc(aux_done, 1)
            half_block("win1", 4, 0)
            wait_taken(("poolT", 0), ("poolT", 1))
            for g in range(2):
                out = aux(("pooly", g))
                for c in range(2):
                    mm = pe.matmul(out[:, c * S:(c + 1) * S], wpool[:, 2 * g + c, :], pooled[:, 2 * g + c, :],
                                   start=True, stop=True)
                mm.then_inc(aux_done, 1)
            wait_taken(*(("rscore", h) for h in range(RH)))
            pe.wait_ge(pair_taken[1], taken("win1", 3)[1])
            for tt in range(TT):
                out = aux(("rout", tt))
                for h in range(RH):
                    o = out[:, h * P:(h + 1) * P]
                    v = [rv[:, t, h * P:(h + 1) * P] for t in range(TT)]
                    if tt == 0:
                        mm = pe.matmul(o, rsc[:, h, 0:P], v[0], start=True, stop=True)
                    else:
                        pe.matmul(o, rsc[:, h, P:S], v[0], start=True, stop=False)
                        mm = pe.matmul(o, rsc[:, h, S:S + P], v[1], start=False, stop=True)
                mm.then_inc(aux_done, 1)
            half_block("win1", 4, 1)
            pe.wait_ge(sem("pool_rest"), 2)
            alternate("wout1", 0)
            for tt in range(TT):
                pe.wait_ge(sem("ret_ready"), tt + 1)
                transposes(("mixr", tt), [rout[:, tt, c * P:(c + 1) * P] for c in range(4)])
            alternate("wout1", 1)
            wait_taken(("mixr", 0), ("mixr", 1))
            last_halves("wout1")

            def conv_transposes(j):
                pe.wait_ge(pair_taken[j % 2], turns(taken("up1", j)[1], 1))
                for key, off in ((("convg", j), 256), (("convv", j), 0)):
                    transposes(key, [gv[:, j % 2, tt, off + c * P:off + (c + 1) * P]
                                     for c in range(2) for tt in range(TT)])

            first_block("up1", "x1", from_x, lambda tt, q: pe.wait_ge(x_ready, x_at("ln1", tt, q)))
            full_block("up1", 1)
            conv_transposes(0)
            full_block("up1", 2)
            conv_transposes(1)
            with turns.loop(CONV_PAIRS, done):
                for j in (3, 4):
                    full_block("up1", j)
                    conv_transposes(j - 1)
            for i in range(FB):
                if i == 2:
                    conv_transposes(FB - 1)
                pe.wait_ge(sem("ffn_rest"), i + 1)
                down("down1", i)

            def ffn(u_name, d_name, h_name, key, pre):
                first_block(u_name, key, from_y, lambda tt, q: pe.wait_ge(normed, normed_at(pre, tt, q)))
                with turns.loop(PAIRS, done):
                    for j in (1, 2):
                        full_block(u_name, j)
                        hidden_transposes(u_name, h_name, j - 1)
                for i in range(FB):
                    if i == 2:
                        hidden_transposes(u_name, h_name, FB - 1)
                    wait_taken((h_name, i))
                    down(d_name, i)

            def hidden_transposes(u_name, h_name, j):
                n, count = taken(u_name, j)
                pe.wait_ge(pair_taken[n], turns(count, 1))
                transposes((h_name, j), [hid[:, j % 2, tt, c * P:(c + 1) * P]
                                         for c in range(2) for tt in range(TT)])

            ffn("upA", "downA", "hA", "f1", "ffn1_pre")

            def fox_logits():
                out = aux(("flog", 0))
                pe.wait_ge(sem("wf_rest"), 1)
                for tt in range(TT):
                    for kc in range(KC):
                        xh, xr = xt_high[:, kc, tt * P:(tt + 1) * P], xt_rest[:, kc, tt * P:(tt + 1) * P]
                        o = out[:, tt * HH:(tt + 1) * HH]
                        pe.matmul(o, xh, wf_high[:, kc, :], start=(kc == 0), stop=False)
                        pe.matmul(o, xh, wf_rest[:, kc, :], start=False, stop=False)
                        mm = pe.matmul(o, xr, wf_high[:, kc, :], start=False, stop=(kc == KC - 1))
                mm.then_inc(aux_done, 1)

            def levels(n):
                hf, lv = HG_STEPS[n]
                pe.wait_ge(sem("level_ready"), n + 1)
                if lv == 0:
                    wait_taken(("qT", 2 * hf), ("qT", 2 * hf + 1))
                if lv in LEVELS:
                    out = aux(("lv", hf, lv, 0))
                    for h in range(HALF):
                        for tt in range(TT):
                            t = slice(tt * P, (tt + 1) * P)
                            q = hqk[:, h, t].rearrange("p (n s) -> p n s", s=2 * lv)[:, :, lv:2 * lv]
                            c = (TT * h + tt) * P // 2
                            mm = pe.matmul(out[:, c:c + P // 2], hqk[:, h, t], q, start=True, stop=True)
                    mm.then_inc(aux_done, 1)
                    return
                for g in range(1 if lv else 2):
                    out = aux(("lv", hf, lv, g))
                    for c in range(4):
                        o = out[:, c * P:(c + 1) * P]
                        h, tt = (c, None) if lv == 128 else (2 * g + c // 2, c % 2)
                        t = slice(0, P) if tt is None else slice(tt * P, (tt + 1) * P)
                        if lv == 0:
                            mm = pe.matmul(o, hk[:, HALF * hf + h, t], hq[:, HALF * hf + h, t], start=True, stop=True)
                        else:
                            mm = pe.matmul(o, hqk[:, h, t], hqk[:, h, P:S] if tt is None else hqk[:, h, t],
                                           start=True, stop=True)
                    mm.then_inc(aux_done, 1)
                if lv == 128:
                    wait_taken(*(("lv", hf, v, g) for v in (0, *LEVELS, 128) for g in range(1 if v else 2)))
                    for tt in range(TT):
                        out = aux(("hgo", hf, tt))
                        for h in range(HALF):
                            o = out[:, h * P:(h + 1) * P]
                            c = slice((HALF * hf + h) * P, (HALF * hf + h + 1) * P)
                            if tt == 0:
                                mm = pe.matmul(o, ha[:, h, 0:P], hi_[:, 0, c], start=True, stop=True)
                            else:
                                pe.matmul(o, ha[:, h, S:S + P], hi_[:, 0, c], start=True, stop=False)
                                mm = pe.matmul(o, ha[:, h, P:S], hi_[:, 1, c], start=False, stop=True)
                        mm.then_inc(aux_done, 1)

            def fox(n):
                if n < HH:
                    out = aux(("fs", n))
                    for tt in range(TT):
                        o = out[:, 0:P] if tt == 0 else out[:, P:P + S]
                        w = (tt + 1) * P
                        pe.matmul(o, fqT[:, n, tt * P:(tt + 1) * P], fkT[:, n, 0:w], start=True, stop=False)
                        for part in (fcum_high, fcum_rest):
                            pe.matmul(o, identr[0:HH, n:n + 1].to_broadcast([HH, P]), part[:, 0:w], start=False, stop=False)
                        mm = pe.matmul(o[:, w - P:w], identb[:, :], causal[:, :], start=False, stop=True)
                    mm.then_inc(aux_done, 1)
                if 1 <= n < HH + 1:
                    h = n - 1
                    wait_taken(("fs", h))
                    transposes(("fp", h), [fp[:, h % 2, c * P:(c + 1) * P] for c in range(3)])
                if n >= 2:
                    h = n - 2
                    wait_taken(("fp", h))
                    out = aux(("fo", h))
                    v = [fv[:, t, h * P:(h + 1) * P] for t in range(TT)]
                    pe.matmul(out[:, 0:P], fpT[:, h % 2, 0:P], v[0], start=True, stop=True)
                    pe.matmul(out[:, P:S], fpT[:, h % 2, P:S], v[0], start=True, stop=False)
                    pe.matmul(out[:, P:S], fpT[:, h % 2, S:S + P], v[1], start=False, stop=True).then_inc(aux_done, 1)

            for u in range(36):
                j, half = divmod(u, 2)
                if u == 0:
                    first_block("win2", "m2", from_y, lambda tt, q: pe.wait_ge(normed, normed_at("mix_pre", tt, q)))
                if u >= 2:
                    half_block("win2", j, half)
                if u == 1:
                    fox_logits()
                if u == 7:
                    out = aux(("flog", 1))
                    pe.wait_ge(sem("flog_ready"), 1)
                    for tt in range(TT):
                        mm = pe.transpose(out[0:HH, tt * P:(tt + 1) * P], flog[:, tt, :], ident[:, :])
                    mm.then_inc(aux_done, 1)
                if u >= 2 and half == 1 and WIN2[j - 1][0] in ("f", "q", "fq", "fk"):
                    n, count = taken("win2", j - 1)
                    pe.wait_ge(pair_taken[n], count)
                    for g in range(2):
                        transposes((WIN2[j - 1][0] + "T", 2 * ((j - 1) % 2) + g),
                                   [stage[:, (j - 1) % 2, tt, c * P:(c + 1) * P]
                                    for c in (2 * g, 2 * g + 1) for tt in range(TT)])
                for n in HG_SLOT[u]:
                    levels(n)
                if u in OA_SLOT:
                    tt, q = divmod(OA_SLOT[u], 2)
                    pe.wait_ge(sem("oa_ready"), tt + 1)
                    transposes(("oa", OA_SLOT[u]), [ho[:, q, tt, c * P:(c + 1) * P] for c in range(4)])
                for n in FOX_SLOT[u]:
                    if n == 0:
                        wait_taken(*((w + "T", g) for w in ("fq", "fk") for g in range(4)))
                        pe.wait_ge(sem("fcum_rest"), 1)
                        pe.wait_ge(consts1_landed, 16 * CONSTS1)
                        pe.wait_ge(consts2_landed, 16 * CONSTS2)
                    fox(n)

            wait_taken(*(("oa", g) for g in range(4)))
            full_block("brA", 0, at_high, at_rest)
            wait_taken(("fo", HH - 1), ("fo", HH - 2))
            token_groups("ob", lambda tt, c: fo[:, c, tt, :], lambda tt, q: None)
            full_block("brA", 1, at_high, at_rest)
            wait_taken(*(("ob", g) for g in range(4)))
            full_block("brB", 0)
            token_groups("memn", lambda tt, c: mem[:, tt, c * P:(c + 1) * P],
                         lambda tt, q: pe.wait_ge(sem("mem_normed"), tt + 1))
            full_block("brB", 1)
            wait_taken(*(("memn", g) for g in range(4)))
            full_block("mk", 0, mt_high, mt_rest)
            token_groups("y2", from_y, lambda tt, q: pe.wait_ge(sem("y2_ready"), 2))
            full_block("mk", 1, mt_high, mt_rest)
            wait_taken(*(("y2", g) for g in range(4)))
            full_block("wout2", 0)
            pe.wait_ge(pair_taken[0], taken("mk", 0)[1])
            pe.wait_ge(pair_taken[1], taken("mk", 1)[1])
            for g in range(4):
                transposes(("mkT", g), [kstage[:, tt, c * P:(c + 1) * P] for c in (2 * g, 2 * g + 1) for tt in range(TT)])
            last_block("wout2", 1)
            full_block("mv", 0, mt_high, mt_rest)
            half_block("mv", 1, 0, mt_high, mt_rest)
            token_groups("mpre", from_y, lambda tt, q: pe.wait_ge(normed, normed_at("mem_pre", tt, q)))
            half_block("mv", 1, 1, mt_high, mt_rest)

            def mem_query_transposes(j):
                n, count = taken("mq", j)
                pe.wait_ge(pair_taken[n], count)
                for g in (2 * j, 2 * j + 1):
                    transposes(("mqT", g), [qstage[:, tt, c * P:(c + 1) * P] for c in (2 * g, 2 * g + 1) for tt in range(TT)])

            def mem_scores(h):
                wait_taken(("mqT", h))
                out = aux(("ms", h))
                for tt in range(TT):
                    for c in range(2):
                        mm = pe.matmul(out[:, tt * S:(tt + 1) * S], mqT[:, 2 * h + c, tt * P:(tt + 1) * P],
                                       mkT[:, 2 * h + c, :], start=(c == 0), stop=(c == 1))
                mm.then_inc(aux_done, 1)

            def mem_transposes(h):
                wait_taken(("ms", h))
                transposes(("mp", h), [mp[h % 2][:, tt, t * P:(t + 1) * P] for t in range(TT) for tt in range(TT)])

            def mem_outputs(h):
                wait_taken(("mp", h))
                out = aux(("mo", h))
                for tt in range(TT):
                    for t in range(TT):
                        mm = pe.matmul(out[:, tt * S:(tt + 1) * S], mpT[h % 2][:, t, tt * P:(tt + 1) * P],
                                       mv[:, t, h * S:(h + 1) * S], start=(t == 0), stop=(t == TT - 1))
                mm.then_inc(aux_done, 1)

            def out_transposes(q):
                wait_taken(("mo", 2 * q), ("mo", 2 * q + 1))
                for tt in range(TT):
                    transposes(("om", 2 * tt + q), [mo[:, tt, c * P:(c + 1) * P] for c in range(4 * q, 4 * q + 4)])

            wait_taken(*(("mpre", g) for g in range(4)))
            full_block("mq", 0)
            half_block("mq", 1, 0)
            mem_query_transposes(0)
            wait_taken(*(("mkT", g) for g in range(4)))
            mem_scores(0)
            half_block("mq", 1, 1)
            mem_scores(1)
            mem_query_transposes(1)
            mem_transposes(0)
            mem_scores(2)
            pe.wait_ge(pair_taken[0], taken("mv", 0)[1])
            pe.wait_ge(pair_taken[1], taken("mv", 1)[1])
            mem_outputs(0)
            mem_transposes(1)
            mem_scores(3)
            mem_outputs(1)
            out_transposes(0)
            wait_taken(("om", 0), ("om", 2))
            alternate("mo", 0)
            mem_transposes(2)
            mem_transposes(3)
            alternate("mo", 1)
            mem_outputs(2)
            mem_outputs(3)
            out_transposes(1)
            wait_taken(("om", 1), ("om", 3))
            last_halves("mo")
            ffn("upB", "downB", "hB", "f2", "ffn2_pre")
            assert done[0] == len(AUX)

        @block.scalar
        def _(act):
            split = [0]
            mine = sem("scalar_steps")
            steps = [0]
            turns = Turns(act)

            def step(ins):
                ins.then_inc(mine, 1)
                steps[0] += 1

            def settle():
                act.wait_ge(mine, steps[0])

            def split_to(n):
                while split[0] < min(n, UNIT["end"]):
                    u = split[0]
                    act.wait_ge(unit_landed[u % SLOTS], turns(32 * (u // SLOTS + 1), 32))
                    if u >= SLOTS:
                        act.wait_ge(unit_used, turns(u - SLOTS + 1, SLOTS))
                    if u == 0:
                        for k in range(3):
                            c = slice(k * NB, (k + 1) * NB)
                            act.activation(high[:, 0, c], raw[:, 0, c], ACT.Copy).then_inc(sem("lead_high"), 1)
                    c = slice(3 * NB if u == 0 else 0, 4 * NB)
                    act.activation(high[:, u % SLOTS, c], raw[:, u % SLOTS, c], ACT.Copy).then_inc(unit_high, 1)
                    split[0] += 1

            def aux(key):
                n, bank, _ = AUX[key]
                more = AUX[two_on(key)][0] - n if turns.turn is not None else 0
                act.wait_ge(aux_done, turns(n + 1, more))
                return ps[:, bank, :]

            def group_to_high(key, dst):
                src = aux(key)
                if len(dst.shape) == 3:
                    src = src.rearrange("p (k n) -> p k n", k=dst.shape[1])
                act.activation(dst, src, ACT.Copy).then_inc(group_high, 1)

            def tile_groups(name, tt, dst=xt_high):
                for q in range(2):
                    group_to_high((name, 2 * tt + q), dst[:, 4 * q:4 * q + 4, tt * P:(tt + 1) * P])

            def first_group(name):
                group_to_high((name, 0), xt_high[:, 0:4, 0:P])

            def other_groups(name):
                group_to_high((name, 1), xt_high[:, 4:8, 0:P])
                tile_groups(name, 1)

            def token_groups(name, dst=xt_high):
                for tt in range(TT):
                    tile_groups(name, tt, dst)

            def take(key, dst, **how):
                _, bank, _ = AUX[key]
                src = aux(key)[:, 0:int(np.prod(dst.shape[1:]))]
                if len(dst.shape) == 3:
                    src = src.rearrange("p (k n) -> p k n", k=dst.shape[1])
                act.activation(dst, src, ACT.Copy, **how).then_inc(aux_taken[bank], 1)

            def block_values(name, j):
                act.wait_ge(unit_used, turns(filled(name, j), SLOTS))
                return pair_of[taken(name, j)[0]]

            def take_block(name, j, dst, func=ACT.Copy, **how):
                n, _ = taken(name, j)
                act.activation(dst, block_values(name, j), func, **how).then_inc(pair_taken[n], 1)

            def roots_of(src, name, tt, width, offset):
                assert ROOT_ORDER[root[0]] == (name, tt), (name, tt, ROOT_ORDER[root[0]])
                root[0] += 1
                c = NS.get(name, 0) + tt
                act.activation(roots[:, c:c + width], src, ACT.Sqrt, bias=offset)\
                    .then_inc(roots_ready, 1)

            root = [0]

            def square_tile(name, tt, src, junk):
                c = NS[name] + tt
                step(act.activation(junk, src, ACT.Square, scale=D ** -0.5, accum_out=sums[:, c:c + 1]))
                settle()
                roots_of(sums[:, c:c + 1], name, tt, 1, eps[:, 1:2])

            def wait_x(after, tt):
                act.wait_ge(x_ready, x_at(after, tt))

            def pre_norm(name, after, tt):
                wait_x(after, tt)
                square_tile(name, tt, x[:, tt, :], y[:, tt, :])

            def late_pre_norm(name, after):
                for tt in range(TT):
                    wait_x(after, tt)
                    square_tile(name, tt, x[:, tt, :], junk_a[:, tt, :])

            def wait_tile(product, tt):
                if tt == 0:
                    act.wait_ge(tile_done, tile_count[product])
                else:
                    act.wait_ge(unit_used, filled(product, 1))

            def part_square(tt, junk, src):
                step(act.activation(junk, src, ACT.Square, scale=D ** -0.5, accum_out=partsum[:, 0, tt:tt + 1]))

            def part_offset(tt):
                step(act.activation(partsum[:, 1, tt:tt + 1], partsum[:, 0, tt:tt + 1], ACT.Identity, bias=eps[:, 1:2]))

            def root_table():
                settle()
                step(act.activation(partsum[:, 0, :], eps[:, 0:2], ACT.Sqrt))
                settle()

            def post_norm(name, product, tt):
                if tt == 0 and name != "mix_post":
                    root_table()
                wait_tile(product, tt)
                if name != "mix_post":
                    part_square(tt, y[:, tt, 0:NB], pair_of[0][:, tt, :])
                c = NS[name] + tt
                step(act.activation(y[:, tt, NB:D], pair_of[1][:, tt, :], ACT.Square, scale=D ** -0.5,
                                    accum_out=sums[:, c:c + 1]))
                if name != "mix_post":
                    act.wait_ge(mine, steps[0] - 1)
                    part_offset(tt)
                settle()
                roots_of(sums[:, c:c + 1], name, tt, 1, partsum[:, 1, tt:tt + 1])

            def layer_root(name, tt):
                act.wait_ge(sem("var_ready"), x_at(name, tt) // 2)
                roots_of(meanvar[:, tt, 1:2], name, tt, 1, eps[:, 0:1])

            act.wait_ge(eps_ready, 2)
            step(act.activation(partsum[:, 0, :], eps[:, 0:2], ACT.Copy))
            token_groups("x")
            for j, dst in enumerate((stage[:, 0, :, :], stage[:, 1, :, :], rp[:, :, :])):
                split_to(UNIT["win1"] + 2 * j + 4)
                take_block("win1", j, dst)
            for g in range(2):
                take(("rTq", g), rqT[:, 2 * g:2 * g + 2, :])
            split_to(UNIT["win1"] + 9)
            for g in range(2):
                take(("rTk", g), rkT[:, 2 * g:2 * g + 2, :])
            for g in range(2):
                take(("poolT", g), pooled[:, 2 * g:2 * g + 2, :])
            split_to(UNIT["win1"] + 10)
            take_block("win1", 3, rv[:, :, :])
            split_to(UNIT["wout1"] + 1)
            for g in range(2):
                out = aux(("pooly", g))
                for c in range(2):
                    ins = act.activation(pooly[:, 2 * g + c, :], out[:, c * S:(c + 1) * S], ACT.Copy,
                                         scale=small["pscale"][:, 2 * g + c:2 * g + c + 1])
                    if c == 0:
                        step(ins)
                ins.then_inc(aux_taken[AUX["pooly", g][1]], 1)
                settle()
                act.wait_ge(aux_taken[AUX["pooly", g][1]], AUX["pooly", g][2] + 1)
                act.activation(pool_high[:, 2 * g:2 * g + 2, :], pooly[:, 2 * g:2 * g + 2, :], ACT.Copy)\
                    .then_inc(sem("pool_high"), 1)
            for tt in range(TT):
                act.activation(rsq[:, tt, :], aux(("rout", tt)), ACT.Square, scale=P ** -0.5).then_inc(sem("ret_squares"), 1)
            act.wait_ge(sem("ret_sums"), TT)
            roots_of(sums[:, 0:TT * RH], "ret", 0, TT * RH, eps[:, 1:2])
            split_to(UNIT["wout1"] + 2)
            take_block("win1", 4, rg[:, :, :], ACT.Silu)
            split_to(UNIT["wout1"] + 4)
            for tt in range(TT):
                group_to_high(("mixr", tt), xt_high[:, 0:4, tt * P:(tt + 1) * P])
            split_to(UNIT["up1"] + 2)
            root_table()
            layer_root("ln1", 0)
            tile_groups("x1", 0)
            layer_root("ln1", 1)
            tile_groups("x1", 1)

            def conv_values(j):
                out = aux(("convg", j))
                if j >= 2:
                    act.wait_ge(sem("ffn_rest"), turns(j - 1, 2))
                for c in range(2):
                    f = 2 * j + c
                    act.activation(conv[:, j % 2, c, :], out[:, c * S:(c + 1) * S], ACT.Identity,
                                   scale=small["convw"][:, bass.ds(turns(3 * f + 2, 12), 1)],
                                   bias=small["convb"][:, bass.ds(turns(f, 4), 1)]).then_inc(sem("conv_last"), 1)
                act.wait_ge(aux_taken[6], turns(AUX["convg", j][2] + 1, 2))
                act.activation(convs[:, :, :], conv[:, j % 2, :, :], ACT.Silu).then_inc(sem("conv_silu"), 1)
                act.wait_ge(aux_taken[7], turns(AUX["convv", j][2] + 1, 2))
                act.activation(ht_high[:, bass.ds(turns(2 * j, 4), 2), :], conv[:, j % 2, :, :], ACT.Copy)\
                    .then_inc(sem("ffn_high"), 1)

            act.wait_ge(consts1_landed, 16 * CONSTS1)
            def up1_block(j):
                split_to(UNIT["up1"] + 2 * j + 4)
                take_block("up1", j, gv[:, j % 2, :, :])
                if j:
                    conv_values(j - 1)

            up1_block(0)
            up1_block(1)
            up1_block(2)
            with turns.loop(CONV_PAIRS, split, steps):
                up1_block(3)
                up1_block(4)
            split_to(UNIT["down1"] + 4)
            conv_values(FB - 1)
            split_to(UNIT["upA"] + 2)
            root_table()
            layer_root("ln2", 0)
            tile_groups("f1", 0)
            layer_root("ln2", 1)
            tile_groups("f1", 1)

            scales = [0]

            def ffn(u_name, d_name, h_name, pre, after, following):
                def hidden_high(j):
                    group_to_high((h_name, j), ht_high[:, bass.ds(turns(2 * j, 4), 2), :])

                split_to(UNIT[u_name] + 4)
                late_pre_norm(pre, after)
                scales[0] += 1
                def up_block(j):
                    split_to(UNIT[u_name] + 2 * j + 4)
                    if j == 0:
                        act.wait_ge(sem("scales_ready"), scales[0])
                    gate_values = block_values(u_name, j)[:, :, 0:256]
                    for tt in range(TT):
                        c = NS[pre] + tt
                        act.activation(act_[:, j % 2, tt, :], gate_values[:, tt, :], ACT.Silu, scale=recips[:, c:c + 1])\
                            .then_inc(sem("silu_done"), 1)
                    if j:
                        hidden_high(j - 1)

                up_block(0)
                with turns.loop(PAIRS, split, steps):
                    up_block(1)
                    up_block(2)
                split_to(UNIT[d_name] + 4)
                hidden_high(FB - 1)
                split_to(UNIT[following] + 2)

            ffn("upA", "downA", "hA", "ffn1_pre", "ln2", "win2")

            act.wait_ge(consts2_landed, 16 * CONSTS2)
            act.activation(wf_high[:, :, :], wf_raw[:, :, :], ACT.Copy).then_inc(sem("wf_high"), 1)
            act.activation(identr[:, :], ident[:, 0:HH], ACT.Copy).then_inc(sem("identr_ready"), 1)
            act.wait_ge(sem("lb_shifted"), 1)
            act.activation(small["lbl"][:, :, :], small["lbl"][:, :, :], ACT.Exp).then_inc(sem("lb_exp"), 1)
            post_norm("ffn1_post", "downA", 0)
            first_group("m2")
            post_norm("ffn1_post", "downA", 1)
            other_groups("m2")
            split_to(UNIT["win2"] + 4)
            late_pre_norm("mix_pre", "ffn1_post")

            def scaled(name, j, dst, func=ACT.Copy, factor="mix_pre", signal=None):
                values = block_values(name, j)
                for tt in range(TT):
                    c = NS[factor] + tt
                    ins = act.activation(dst[:, tt, :], values[:, tt, :], func, scale=recips[:, c:c + 1])
                    if tt == 0:
                        step(ins)
                ins.then_inc(signal or pair_taken[taken(name, j)[0]], 1)

            def fox_log_sigmoids():
                act.wait_ge(aux_taken[AUX["flog", 0][1]], AUX["flog", 0][2] + 1)
                step(act.activation(flabs[:, :, :], flog[:, :, :], ACT.Abs))
                settle()
                act.activation(flabs[:, :, :], flabs[:, :, :], ACT.Exp, scale=-1.0).then_inc(sem("flog_exp"), 1)
                act.wait_ge(sem("flog_exp"), 1)
                act.activation(flabs[:, :, :], flabs[:, :, :], ACT.Ln, bias=1.0).then_inc(sem("flog_ln"), 1)

            def level_exp(n):
                hf, lv = HG_STEPS[n]
                hs = slice(HALF * hf, HALF * hf + HALF)
                if lv == 0:
                    return
                act.wait_ge(sem("level_diff"), n - hf)
                if lv == 128:
                    act.activation(he[:, :, 0:P], he[:, :, 0:P], ACT.Exp, scale=-1.0)
                    act.activation(he[:, :, P:P + CHUNK], hb[:, hs, P:P + CHUNK], ACT.Exp)
                    ins = act.activation(he[:, :, P + CHUNK:S], he[:, :, P + CHUNK:S], ACT.Exp)
                else:
                    e = he[:, :, :].rearrange("p h (n t) -> p (h n) t", t=2 * lv)
                    b = hb[:, hs, :].rearrange("p h (n t) -> p (h n) t", t=2 * lv) if lv == 64 else e
                    act.activation(e[:, :, 0:lv], e[:, :, 0:lv], ACT.Exp, scale=-1.0)
                    ins = act.activation(e[:, :, lv:2 * lv], b[:, :, lv:2 * lv], ACT.Exp)
                ins.then_inc(sem("level_exp"), 1)

            for u in range(36):
                split_to(UNIT["win2"] + u + 4)
                j, half = divmod(u, 2)
                what = WIN2[j][0]
                c = slice((j % 2) * NB, (j % 2 + 1) * NB)
                if u == 0:
                    scales[0] += 1
                    act.wait_ge(sem("scales_ready"), scales[0])
                if u == 3:
                    fox_log_sigmoids()
                if u == 8:
                    act.wait_ge(sem("fcum_ready"), 1)
                    act.activation(fcum_high[:, :], fcum[:, :], ACT.Copy).then_inc(sem("fcum_high"), 1)
                if half and j and WIN2[j - 1][0] in ("f", "q", "fq", "fk"):
                    w, k = WIN2[j - 1][0], (j - 1) % 2
                    if w == "f":
                        act.wait_ge(sem("f_ready"), k + 1)
                        act.activation(hb[:, HALF * k:HALF * k + HALF, :], he[:, :, :], ACT.Ln).then_inc(sem("f_log"), 1)
                    else:
                        for g in range(2):
                            dst = {"q": hq, "fq": fqT, "fk": fkT}[w][:, HALF * k + 2 * g:HALF * k + 2 * g + 2, :]
                            take((w + "T", 2 * k + g), dst, scale={"q": 0.5, "fq": P ** -0.5, "fk": 1.0}[w])
                if half:
                    if what == "f":
                        scaled("win2", j, stage[:, j % 2, :, :], ACT.Sigmoid)
                    elif what == "q":
                        scaled("win2", j, stage[:, j % 2, :, :], ACT.Tanh, "mix_half", sem("q_tanh"))
                    elif what == "g":
                        act.wait_ge(sem("level_exp"), len(HG_STEPS) - 2)
                        scaled("win2", j, hg[:, :, c], ACT.Tanh, "mix_half", sem("g_tanh"))
                    elif what in ("fq", "fk"):
                        scaled("win2", j, stage[:, j % 2, :, :])
                    elif what == "i":
                        scaled("win2", j, hi_[:, :, c])
                    elif what == "fv":
                        scaled("win2", j, fv[:, :, c])
                    else:
                        g = j - 14
                        act.wait_ge(pair_taken[j % 2], taken("win2", j)[1])
                        d = gate[g // 2][:, :, c]
                        act.activation(d, d, ACT.Tanh, scale=0.5).then_inc(sem("gate_tanh"), 1)
                for n in HG_SLOT[u]:
                    if n == 0:
                        level_exp(1)
                    elif n + 1 < len(HG_STEPS):
                        level_exp(n + 1)
                    if n == len(HG_STEPS) - 1:
                        def src(tt):
                            for key in (("hgo", a, b) for a in range(2) for b in range(TT)):
                                act.wait_ge(aux_taken[AUX[key][1]], AUX[key][2] + 1)
                            return ho[:, :, tt, :]
                        for tt in range(TT):
                            square_tile("hg", tt, src(tt), junk_h[:, tt, :].rearrange("p (n c) -> p n c", n=2))
                if u in OA_SLOT:
                    tt, q = divmod(OA_SLOT[u], 2)
                    group_to_high(("oa", OA_SLOT[u]), at_high[:, 4 * q:4 * q + 4, tt * P:(tt + 1) * P])
                for n in FOX_SLOT[u]:
                    if 1 <= n < HH + 1:
                        take(("fp", n - 1), fpT[:, (n - 1) % 2, :])
                    if n < HH:
                        act.wait_ge(sem("fox_max"), TT * (n + 1))
                        _, bank, _ = AUX["fs", n]
                        out = aux(("fs", n))
                        for tt in range(TT):
                            c0, c1 = (0, P) if tt == 0 else (P, P + S)
                            ins = act.activation(fp[:, n % 2, c0:c1], out[:, c0:c1], ACT.Exp,
                                                 bias=small["negmax"][:, n, tt:tt + 1],
                                                 accum_out=small["expsum"][:, n, tt:tt + 1])
                        ins.then_inc(aux_taken[bank], 1)

            split_to(UNIT["brA"] + 4)
            token_groups("ob")
            split_to(UNIT["brB"] + 2)
            act.wait_ge(mem_landed, 16)
            for tt in range(TT):
                square_tile("mem_kv", tt, mem[:, tt, :], y[:, tt, :])
            split_to(UNIT["brB"] + 4)
            token_groups("memn", mt_high)
            split_to(UNIT["mk"] + 4)
            take_block("mk", 0, kstage[:, :, 0:NB])
            token_groups("y2")
            split_to(UNIT["wout2"] + 2)
            take_block("mk", 1, kstage[:, :, NB:D])
            split_to(UNIT["wout2"] + 4)
            for g in range(4):
                take(("mkT", g), mkT[:, 2 * g:2 * g + 2, :])
            act.wait_ge(pair_taken[0], taken("wout2", 0)[1])
            root_table()
            for tt in range(TT):
                part_square(tt, junk_m[:, tt, :], y[:, tt, 0:NB])
            settle()
            for tt in range(TT):
                part_offset(tt)
            split_to(UNIT["mv"] + 2)
            post_norm("mix_post", "wout2", 0)
            pre_norm("mem_pre", "mix_post", 0)
            post_norm("mix_post", "wout2", 1)
            split_to(UNIT["mv"] + 3)
            pre_norm("mem_pre", "mix_post", 1)
            split_to(UNIT["mv"] + 4)
            take_block("mv", 0, mv[:, :, 0:NB])
            split_to(UNIT["mq"] + 2)
            token_groups("mpre")
            take_block("mv", 1, mv[:, :, NB:D])

            split_to(UNIT["mq"] + 4)
            take_block("mq", 0, qstage[:, :, 0:NB], scale=S ** -0.5)
            split_to(UNIT["mo"] + 1)

            def exponentials(h):
                act.wait_ge(sem("mem_max"), h + 1)
                _, bank, _ = AUX["ms", h]
                out = aux(("ms", h))
                for tt in range(TT):
                    ins = act.activation(mp[h % 2][:, tt, :], out[:, tt * S:(tt + 1) * S], ACT.Exp,
                                         bias=small["negmax"][:, h, tt:tt + 1], accum_out=small["expsum"][:, h, tt:tt + 1])
                ins.then_inc(aux_taken[bank], 1)

            def exp_transposes(h):
                take(("mp", h), mpT[h % 2][:, :, :].rearrange("p t s -> p (t s)"))

            def query_transposes(j):
                for g in (2 * j, 2 * j + 1):
                    take(("mqT", g), mqT[:, 2 * g:2 * g + 2, :])

            def out_groups(q):
                for tt in range(TT):
                    group_to_high(("om", 2 * tt + q), xt_high[:, 4 * q:4 * q + 4, tt * P:(tt + 1) * P])

            query_transposes(0)
            exponentials(0)
            split_to(UNIT["mo"] + 2)
            take_block("mq", 1, qstage[:, :, NB:D], scale=S ** -0.5)
            exponentials(1)
            query_transposes(1)
            exp_transposes(0)
            exponentials(2)
            exp_transposes(1)
            exponentials(3)
            out_groups(0)
            split_to(UNIT["mo"] + 4)
            exp_transposes(2)
            exp_transposes(3)
            split_to(UNIT["upB"] + 1)
            out_groups(1)
            split_to(UNIT["upB"] + 2)
            post_norm("mem_post", "mo", 0)
            first_group("f2")
            post_norm("mem_post", "mo", 1)
            other_groups("f2")
            ffn("upB", "downB", "hB", "ffn2_pre", "mem_post", "end")
            for tt in range(TT):
                post_norm("ffn2_post", "downB", tt)
            assert split[0] == UNIT["end"]

        @block.vector
        def _(vec):
            split, groups = [0], [0]
            mine = sem("vector_steps")
            steps = [0]
            turns = Turns(vec)
            steps_a_turn = [0]

            def step(ins):
                ins.then_inc(mine, 1)
                steps[0] += 1

            def settle():
                vec.wait_ge(mine, turns(steps[0], steps_a_turn[0]))

            def split_to(n):
                while split[0] < min(n, UNIT["end"]):
                    u = split[0]
                    slot = u % SLOTS
                    chunks = range(4) if u == 0 else (None,)
                    for k in chunks:
                        c = slice(0, 4 * NB) if k is None else slice(k * NB, (k + 1) * NB)
                        lead = k is not None and k < 3
                        if lead:
                            vec.wait_ge(sem("lead_high"), k + 1)
                        else:
                            vec.wait_ge(unit_high, turns(u + 1, SLOTS))
                        vec.tensor_tensor(rest[:, slot, c], raw[:, slot, c], high[:, slot, c].bitcast(F32),
                                          ALU.subtract).then_inc(sem("lead_rest") if lead else unit_rest, 1)
                    split[0] += 1

            def aux(key):
                n, bank, _ = AUX[key]
                more = AUX[two_on(key)][0] - n if turns.turn is not None else 0
                vec.wait_ge(aux_done, turns(n + 1, more))
                return ps[:, bank, :]

            def took(key, ins):
                ins.then_inc(aux_taken[AUX[key][1]], 1)

            def group_to_rest(key, dst_high, dst_rest):
                _, bank, _ = AUX[key]
                groups[0] += 1
                vec.wait_ge(group_high, turns(groups[0], 2))
                src = ps[:, bank, :].rearrange("p (k n) -> p k n", k=dst_high.shape[1])
                vec.tensor_tensor(dst_rest, src, dst_high.bitcast(F32), ALU.subtract).then_inc(aux_taken[bank], 1)

            def tile_groups(name, tt, th=xt_high, tr=xt_rest, halves_=(0, 1)):
                for q in halves_:
                    at = (slice(None), slice(4 * q, 4 * q + 4), slice(tt * P, (tt + 1) * P))
                    group_to_rest((name, 2 * tt + q), th[at], tr[at])

            def token_groups(name, th=xt_high, tr=xt_rest):
                for tt in range(TT):
                    tile_groups(name, tt, th, tr)

            def block_values(name, j):
                vec.wait_ge(unit_used, turns(filled(name, j), SLOTS))
                return pair_of[taken(name, j)[0]]

            def took_block(name, j, ins):
                ins.then_inc(pair_taken[taken(name, j)[0]], 1)

            def gain(name):
                n = GAINS.index(name)
                vec.wait_ge(gain_landed[n % GSLOTS], 16 * (n // GSLOTS + 1))
                return gains[:, n % GSLOTS, :]

            def recip_roots(name, tt=0, cols=1):
                vec.wait_ge(roots_ready, root_count[name, tt])
                c = NS.get(name, 0) + tt
                step(vec.reciprocal(recips[:, c:c + cols], roots[:, c:c + cols]))
                settle()
                return recips[:, c:c + 1]

            def halves(ap):
                return ap.rearrange("p (n c) -> p n c", n=2)

            halves_of = [slice(0, NB), slice(NB, D)]

            def pre_norm(name, tt):
                r, g = recip_roots(name, tt), gain(name)
                for c in halves_of:
                    vec.scalar_tensor_tensor(y[:, tt, c], x[:, tt, c], r, g[:, c], ALU.mult, ALU.mult).then_inc(normed, 1)

            def gained(name, after, tt, q):
                c, g = halves_of[q], gain(name)
                vec.wait_ge(x_ready, x_at(after, tt, q))
                vec.tensor_tensor(y[:, tt, c], x[:, tt, c], g[:, c], ALU.mult).then_inc(normed, 1)

            def post_norm(name, scale, tt, following=None):
                r, g = recip_roots(name, tt), gain(name)
                for n, c in enumerate(halves_of):
                    if name == "mix_post" and n == 0:
                        step(vec.scalar_tensor_tensor(y[:, tt, c], y[:, tt, c], r, g[:, c], ALU.mult, ALU.mult))
                        settle()
                    else:
                        ins = vec.scalar_tensor_tensor(y[:, tt, c], pair_of[n][:, tt, :], r, g[:, c], ALU.mult, ALU.mult)
                        if tt == 0:
                            step(ins)
                            settle()
                        else:
                            ins.then_inc(pair_taken[n], 1)
                            vec.wait_ge(pair_taken[n], PAIR[post_block[name], n][1] + 1)
                    vec.scalar_tensor_tensor(x[:, tt, c], y[:, tt, c], scale, x[:, tt, c], ALU.mult, ALU.add)\
                        .then_inc(x_ready, 1)
                    if following:
                        gained(following, name, tt, n)

            def attention_out(scores, key, dst, width, h):
                _, bank, used = AUX[scores]
                vec.wait_ge(aux_taken[bank], used + 1)
                sums_ = small["expsum"][:, h, :]
                step(vec.reciprocal(sums_, sums_))
                settle()
                src = aux(key)[:, 0:TT * width].rearrange("p (t c) -> p t c", t=TT)
                took(key, vec.tensor_tensor(dst, src, sums_.unsqueeze(2).to_broadcast([P, TT, width]), ALU.mult))

            post_block = {"ffn1_post": "downA", "mix_post": "wout2", "mem_post": "mo", "ffn2_post": "downB"}

            def layer_stats(product, tt):
                if tt == 0:
                    vec.wait_ge(tile_done, tile_count[product])
                else:
                    vec.wait_ge(unit_used, filled(product, 1))
                for n in range(2):
                    c = slice(n * NB, (n + 1) * NB)
                    ins = vec.scalar_tensor_tensor(y[:, tt, c], x[:, tt, c], ALPHA, pair_of[n][:, tt, :], ALU.mult, ALU.add)
                    if tt == 0:
                        step(ins)
                    else:
                        ins.then_inc(pair_taken[n], 1)
                if tt == 0:
                    settle()
                else:
                    for n in range(2):
                        vec.wait_ge(pair_taken[n], PAIR[product, n][1] + 1)
                for n in range(2):
                    step(vec.bn_stats(moments[:, tt, 6 * n:6 * n + 6], y[:, tt, n * NB:(n + 1) * NB]))
                settle()
                vec.bn_aggr(meanvar[:, tt, :], moments[:, tt, :].rearrange("p (n c) -> p n c", n=2)).then_inc(sem("var_ready"), 1)

            def layer_norm(name, tt, following=None):
                r, g, b = recip_roots(name, tt), gain(name + "_g"), gain(name + "_b")
                for q, c in enumerate(halves_of):
                    step(vec.scalar_tensor_tensor(y[:, tt, c], y[:, tt, c], meanvar[:, tt, 0:1], g[:, c], ALU.subtract, ALU.mult))
                    settle()
                    vec.scalar_tensor_tensor(x[:, tt, c], y[:, tt, c], r, b[:, c], ALU.mult, ALU.add).then_inc(x_ready, 1)
                    if following:
                        gained(following, name, tt, q)

            vec.memset(eps[:, 0:1], LN_EPS).then_inc(eps_ready, 1)
            vec.memset(eps[:, 1:2], RMS_EPS).then_inc(eps_ready, 1)

            token_groups("x")
            split_to(UNIT["win1"] + 10)
            vec.wait_ge(consts1_landed, 16 * CONSTS1)
            for h in range(RH):
                src = aux(("rscore", h))
                took(("rscore", h), vec.tensor_tensor(rsc[:, h, :], src[:, 0:384], decay[:, h, :], ALU.mult))
            split_to(UNIT["wout1"] + 1)
            for g in range(2):
                vec.wait_ge(sem("pool_high"), g + 1)
                k = slice(2 * g, 2 * g + 2)
                vec.tensor_tensor(pool_rest[:, k, :], pooly[:, k, :], pool_high[:, k, :].bitcast(F32), ALU.subtract)\
                    .then_inc(sem("pool_rest"), 1)
            for tt in range(TT):
                vec.wait_ge(sem("ret_squares"), tt + 1)
                vec.tensor_reduce(sums[:, RH * tt:RH * tt + RH], rsq[:, tt, :].rearrange("p (h d) -> p h d", h=RH),
                                  AX_X, ALU.add).then_inc(sem("ret_sums"), 1)
            recip_roots("ret", 0, TT * RH)
            for tt in range(TT):
                r4 = recips[:, RH * tt:RH * tt + RH].unsqueeze(2).to_broadcast([P, RH, P])
                o = rout[:, tt, :]
                took(("rout", tt), vec.tensor_tensor(o.rearrange("p (h d) -> p h d", h=RH),
                                                     aux(("rout", tt)).rearrange("p (h d) -> p h d", h=RH), r4, ALU.mult))
                vec.wait_ge(aux_taken[AUX["rout", tt][1]], AUX["rout", tt][2] + 1)
                vec.wait_ge(pair_taken[0], taken("win1", 4)[1])
                vec.tensor_tensor(o, o, rg[:, tt, :], ALU.mult).then_inc(sem("ret_ready"), 1)
            split_to(UNIT["wout1"] + 2)
            split_to(UNIT["wout1"] + 4)
            for tt in range(TT):
                at = (slice(None), slice(0, 4), slice(tt * P, (tt + 1) * P))
                group_to_rest(("mixr", tt), xt_high[at], xt_rest[at])
            split_to(UNIT["up1"] + 2)
            layer_stats("wout1", 0)
            layer_norm("ln1", 0)
            tile_groups("x1", 0, halves_=(0,))
            layer_stats("wout1", 1)
            tile_groups("x1", 0, halves_=(1,))
            layer_norm("ln1", 1)
            tile_groups("x1", 1)

            def conv_values(j):
                src = aux(("convg", j)).rearrange("p (c s) -> p c s", c=2)
                val = ps[:, 7, :].rearrange("p (c s) -> p c s", c=2)
                vec.wait_ge(sem("conv_last"), turns(2 * j + 2, 4))
                for tap, back in ((1, 1), (0, 2)):
                    for c in range(2):
                        d = conv[:, j % 2, c, back:S]
                        ins = vec.scalar_tensor_tensor(d, src[:, c, 0:S - back], small["convw"][:, bass.ds(turns(3 * (2 * j + c) + tap, 12), 1)],
                                                       d, ALU.mult, ALU.add)
                        if (tap, c) == (0, 1):
                            took(("convg", j), ins)
                        else:
                            step(ins)
                    if tap == 1:
                        settle()
                vec.wait_ge(sem("conv_silu"), turns(j + 1, 2))
                aux(("convv", j))
                took(("convv", j), vec.tensor_tensor(conv[:, j % 2, :, :], convs[:, :, :], val, ALU.mult))
                vec.wait_ge(sem("ffn_high"), turns(j + 1, 2))
                k = bass.ds(turns(2 * j, 4), 2)
                vec.tensor_tensor(ht_rest[:, k, :], conv[:, j % 2, :, :], ht_high[:, k, :].bitcast(F32),
                                  ALU.subtract).then_inc(sem("ffn_rest"), 1)

            def up1_block(j):
                split_to(UNIT["up1"] + 2 * j + 4)
                if j:
                    conv_values(j - 1)

            up1_block(0)
            up1_block(1)
            up1_block(2)
            steps_a_turn[0] = 6
            with turns.loop(CONV_PAIRS, split, steps):
                up1_block(3)
                up1_block(4)
            split_to(UNIT["down1"] + 4)
            conv_values(FB - 1)
            split_to(UNIT["upA"] + 2)
            layer_stats("down1", 0)
            layer_norm("ln2", 0, "ffn1_pre")
            tile_groups("f1", 0, halves_=(0,))
            layer_stats("down1", 1)
            tile_groups("f1", 0, halves_=(1,))
            layer_norm("ln2", 1, "ffn1_pre")
            tile_groups("f1", 1)

            def ffn(u_name, d_name, h_name, pre, following):
                def hidden_rest(j):
                    k = bass.ds(turns(2 * j, 4), 2)
                    group_to_rest((h_name, j), ht_high[:, k, :], ht_rest[:, k, :])

                split_to(UNIT[u_name] + 4)
                for tt in range(TT):
                    vec.wait_ge(roots_ready, root_count[pre, tt])
                c = NS[pre]
                vec.reciprocal(recips[:, c:c + TT], roots[:, c:c + TT]).then_inc(sem("scales_ready"), 1)
                scales[0] += 1
                vec.wait_ge(sem("scales_ready"), scales[0])
                def up_block(j):
                    split_to(UNIT[u_name] + 2 * j + 4)
                    values = block_values(u_name, j)[:, :, 256:NB]
                    for tt in range(TT):
                        silus[0] += 1
                        vec.wait_ge(sem("silu_done"), turns(silus[0], 2 * TT))
                        ins = vec.scalar_tensor_tensor(hid[:, j % 2, tt, :], values[:, tt, :], recips[:, c + tt:c + tt + 1],
                                                       act_[:, j % 2, tt, :], ALU.mult, ALU.mult)
                        if tt == 0:
                            step(ins)
                    took_block(u_name, j, ins)
                    if j:
                        hidden_rest(j - 1)

                up_block(0)
                steps_a_turn[0] = 2
                with turns.loop(PAIRS, split, steps, groups, silus):
                    up_block(1)
                    up_block(2)
                split_to(UNIT[d_name] + 4)
                hidden_rest(FB - 1)
                split_to(UNIT[following] + 2)

            silus, scales = [0], [0]
            ffn("upA", "downA", "hA", "ffn1_pre", "win2")

            vec.wait_ge(sem("wf_high"), 1)
            vec.tensor_tensor(wf_rest[:, :, :], wf_raw[:, :, :], wf_high[:, :, :].bitcast(F32), ALU.subtract)\
                .then_inc(sem("wf_rest"), 1)
            lbl, lb = small["lbl"], small["lb"]
            vec.wait_ge(consts2_landed, 16 * CONSTS2)
            step(vec.tensor_tensor(lb[:, 2, :], lbl[:, 0, :], lbl[:, 1, :], ALU.max))
            settle()
            vec.tensor_tensor(lbl[:, :, :], lbl[:, :, :], lb[:, 2, :].unsqueeze(1).to_broadcast([P, 2, HH]),
                              ALU.subtract).then_inc(sem("lb_shifted"), 1)
            vec.wait_ge(sem("lb_exp"), 1)
            step(vec.tensor_tensor(lb[:, 2, :], lbl[:, 0, :], lbl[:, 1, :], ALU.add))
            settle()
            step(vec.reciprocal(lb[:, 3, :], lb[:, 2, :]))
            settle()
            for n in range(2):
                step(vec.tensor_tensor(lb[:, n, :], lbl[:, n, :], lb[:, 3, :], ALU.mult))
            settle()
            vec.wait_ge(levels_landed, 16)
            step(vec.tensor_copy(levelmask[:, :, :], levels32[:, :, :]))
            settle()

            post_norm("ffn1_post", 0.5, 0, "mix_pre")
            tile_groups("m2", 0)
            post_norm("ffn1_post", 0.5, 1, "mix_pre")
            tile_groups("m2", 1)
            split_to(UNIT["win2"] + 4)
            for tt in range(TT):
                recip_roots("mix_pre", tt)
            factor = [recips[:, NS["mix_pre"] + tt:NS["mix_pre"] + tt + 1] for tt in range(TT)]
            vec.tensor_scalar(recips[:, NS["mix_half"]:NS["mix_half"] + TT], recips[:, NS["mix_pre"]:NS["mix_pre"] + TT],
                              0.5, None, ALU.mult).then_inc(sem("scales_ready"), 1)
            scales[0] += 1

            def take_silu(j, d):
                for tt in range(TT):
                    step(vec.tensor_scalar(d[:, tt, :], d[:, tt, :], 1.0, factor[tt], ALU.add, ALU.mult))
                settle()
                took_block("win2", j, vec.tensor_tensor(d, d, block_values("win2", j), ALU.mult))

            def diff(n):
                hf, lv = HG_STEPS[n]
                b = hb[:, HALF * hf:HALF * hf + HALF, :]
                vec.wait_ge(sem("level_ready"), n)
                if lv == 128:
                    cr = small["crossref"]
                    step(vec.tensor_tensor(cr[:, :], b[:, :, CHUNK - 1], b[:, :, P - 1], ALU.add))
                    settle()
                    last = lambda ap: ap.unsqueeze(2).to_broadcast([P, HALF, CHUNK])
                    vec.tensor_tensor(he[:, :, 0:CHUNK], b[:, :, 0:CHUNK], last(cr[:, :]), ALU.subtract)
                    vec.tensor_tensor(he[:, :, CHUNK:P], b[:, :, CHUNK:P], last(b[:, :, P - 1]), ALU.subtract)
                    ins = vec.tensor_tensor(he[:, :, P + CHUNK:S], b[:, :, P + CHUNK:S], last(b[:, :, P + CHUNK - 1]), ALU.add)
                else:
                    e = he[:, :, :].rearrange("p h (n t) -> p (h n) t", t=2 * lv)
                    b = b.rearrange("p h (n t) -> p (h n) t", t=2 * lv)
                    w = lv if lv == 64 else 2 * lv
                    ref = b[:, :, lv - 1].unsqueeze(2).to_broadcast([P, HALF * S // (2 * lv), w])
                    ins = vec.tensor_tensor(e[:, :, 0:w], b[:, :, 0:w], ref, ALU.subtract)
                ins.then_inc(sem("level_diff"), 1)

            def apply_decays(n):
                hf, lv = HG_STEPS[n]
                hs = slice(HALF * hf, HALF * hf + HALF)
                vec.wait_ge(sem("level_exp"), n - hf)
                t = P if lv == 128 else lv
                view = lambda ap: ap.rearrange("p h (n t) -> p (h n) t", t=2 * t)
                e, o, q, k = view(he[:, :, :]), view(hqk[:, :, :]), view(hq[:, hs, :]), view(hk[:, hs, :])
                step(vec.tensor_tensor(o[:, :, 0:t], e[:, :, 0:t], k[:, :, 0:t], ALU.mult))
                settle()
                vec.tensor_tensor(o[:, :, t:2 * t], e[:, :, t:2 * t], q[:, :, t:2 * t], ALU.mult)\
                    .then_inc(sem("level_ready"), 1)

            def place_scores(n):
                hf, lv = HG_STEPS[n]
                if lv == 128:
                    src = aux(("lv", hf, lv, 0)).rearrange("p (h t) -> p h t", h=HALF)
                    took(("lv", hf, lv, 0), vec.tensor_copy(ha[:, :, S:S + P], src))
                    return
                m = levelmask[:, (0, *LEVELS).index(lv), :]
                if lv:
                    view = lambda ap: ap.rearrange("p h (n s) -> p h n s", s=lv)
                    d = ha[:, :, 0:S].rearrange("p h (n s) -> p h n s", s=2 * lv)[:, :, :, lv:2 * lv]
                    src = view(aux(("lv", hf, lv, 0)).rearrange("p (h t) -> p h t", h=HALF))
                    took(("lv", hf, lv, 0), vec.copy_predicated(d, view(m.unsqueeze(1).to_broadcast([P, HALF, P])), src))
                    vec.wait_ge(aux_taken[AUX["lv", hf, lv, 0][1]], AUX["lv", hf, lv, 0][2] + 1)
                    return
                for g in range(2):
                    src = aux(("lv", hf, 0, g)).rearrange("p (h t s) -> p h t s", h=2, t=TT)
                    for c in range(2):
                        d = ha[:, 2 * g + c, 0:S].rearrange("p (t s) -> p t s", t=TT)
                        ins = vec.copy_predicated(d, m.unsqueeze(1).to_broadcast([P, TT, P]), src[:, c])
                        if c == 0:
                            step(ins)
                    took(("lv", hf, 0, g), ins)
                settle()

            def fox_log_sigmoids():
                step(vec.memset(fones[:, :], 1.0))
                z = aux(("flog", 0))[:, 0:TT * HH].rearrange("p (t h) -> p t h", t=TT)
                for tt in range(TT):
                    ins = vec.scalar_tensor_tensor(flog[:, tt, :], z[:, tt, :], factor[tt], small["flb"][:, :], ALU.mult, ALU.add)
                    if tt == 0:
                        step(ins)
                took(("flog", 0), ins)
                vec.wait_ge(aux_taken[AUX["flog", 0][1]], AUX["flog", 0][2] + 1)
                step(vec.tensor_scalar(flmin[:, :, :], flog[:, :, :], 0.0, None, ALU.min))
                settle()

            for u in range(36):
                for n in HG_SLOT[u]:
                    hf, lv = HG_STEPS[n]
                    if lv == 0:
                        for g in range(2):
                            key = ("qT", 2 * hf + g)
                            vec.wait_ge(aux_taken[AUX[key][1]], AUX[key][2] + 1)
                    else:
                        apply_decays(n)
                    if n + 1 < len(HG_STEPS) and HG_STEPS[n + 1][1]:
                        diff(n + 1)
                split_to(UNIT["win2"] + u + 4)
                j, half = divmod(u, 2)
                what = WIN2[j][0]
                c = slice((j % 2) * NB, (j % 2 + 1) * NB)
                if half and j and WIN2[j - 1][0] == "f":
                    k = (j - 1) % 2
                    if k:
                        vec.wait_ge(sem("f_log"), k)
                    for g in range(2):
                        src = aux(("fT", 2 * k + g))
                        for c in range(2):
                            h = HALF * k + 2 * g + c
                            ins = vec.tensor_scalar(he[:, 2 * g + c, :], src[:, c * S:(c + 1) * S], lb[:, 1, h:h + 1],
                                                    lb[:, 0, h:h + 1], ALU.mult, ALU.add)
                            if c == 0:
                                step(ins)
                        took(("fT", 2 * k + g), ins)
                    settle()
                    for g in range(2):
                        vec.wait_ge(aux_taken[AUX["fT", 2 * k + g][1]], AUX["fT", 2 * k + g][2] + 1)
                    vec.tensor_scalar(hk[:, HALF * k:HALF * k + HALF, :], he[:, :, :], -1.0, 1.0, ALU.mult, ALU.add)\
                        .then_inc(sem("f_ready"), 1)
                    vec.wait_ge(sem("f_log"), k + 1)
                    for h in range(HALF * k, HALF * k + HALF):
                        step(vec.tensor_tensor_scan(hb[:, h, :], scanstart[:, :], hb[:, h, :], 0.0, ALU.mult, ALU.add))
                    settle()
                for n in HG_SLOT[u]:
                    hf, lv = HG_STEPS[n]
                    if lv == 0:
                        vec.wait_ge(sem("level_ready"), n + 1)
                    place_scores(n)
                    if lv == 128:
                        for tt in range(TT):
                            took(("hgo", hf, tt), vec.tensor_copy(ho[:, hf, tt, :], aux(("hgo", hf, tt))))
                        if hf == 0:
                            vec.memset(ha[:, :, :], 0.0).then_inc(sem("level_ready"), 1)
                if half:
                    if what == "q":
                        vec.wait_ge(sem("q_tanh"), j % 2 + 1)
                        take_silu(j, stage[:, j % 2, :, :])
                    elif what == "g":
                        vec.wait_ge(sem("g_tanh"), j % 2 + 1)
                        take_silu(j, hg[:, :, c])
                    elif what == "gate":
                        g = (j - 14) // 2
                        bias, values = gain(f"gate{g}")[:, c], block_values("win2", j)
                        for tt in range(TT):
                            ins = vec.scalar_tensor_tensor(gate[g][:, tt, c], values[:, tt, :], factor[tt], bias, ALU.mult, ALU.add)
                            if tt == 0:
                                step(ins)
                        took_block("win2", j, ins)
                if u == 2:
                    fox_log_sigmoids()
                if u == 4:
                    vec.wait_ge(sem("flog_ln"), 1)
                    vec.tensor_tensor(flog[:, :, :], flabs[:, :, :], flmin[:, :, :], ALU.subtract).then_inc(sem("flog_ready"), 1)
                if u == 7:
                    src = ps[0:HH, AUX["flog", 1][1], 0:S]
                    aux(("flog", 1))
                    took(("flog", 1), vec.tensor_tensor_scan(fcum[:, :], fones[:, :], src, 0.0, ALU.mult, ALU.add))
                    vec.wait_ge(aux_taken[AUX["flog", 1][1]], AUX["flog", 1][2] + 1)
                    vec.sem_inc(sem("fcum_ready"), 1)
                if u == 5:
                    vec.memset(ha[:, :, :], 0.0).then_inc(sem("level_ready"), 1)
                if u == 8:
                    vec.wait_ge(sem("fcum_high"), 1)
                    vec.tensor_tensor(fcum_rest[:, :], fcum[:, :], fcum_high[:, :].bitcast(F32), ALU.subtract)\
                        .then_inc(sem("fcum_rest"), 1)
                if u in (26, 28):
                    tt = (u - 26) // 2
                    n = NS["hg"] + tt
                    recip_roots("hg", tt)
                    step(vec.tensor_scalar(recips[:, n:n + 1], recips[:, n:n + 1], 0.5, None, ALU.mult))
                    settle()
                    g = gain("hg_norm")
                    o = ho[:, :, tt, :]
                    step(vec.scalar_tensor_tensor(o, o, recips[:, n:n + 1], halves(g), ALU.mult, ALU.mult))
                if u in (27, 29):
                    for pair in range(2):
                        vec.wait_ge(pair_taken[pair], taken("win2", 12 + pair)[1])
                    settle()
                    tt = (u - 27) // 2
                    o = ho[:, :, tt, :]
                    vec.tensor_tensor(o, o, halves(hg[:, tt, :]), ALU.mult).then_inc(sem("oa_ready"), 1)
                if u in OA_SLOT:
                    tt, q = divmod(OA_SLOT[u], 2)
                    at = (slice(None), slice(4 * q, 4 * q + 4), slice(tt * P, (tt + 1) * P))
                    group_to_rest(("oa", OA_SLOT[u]), at_high[at], at_rest[at])
                for n in FOX_SLOT[u]:
                    if n < HH:
                        src = aux(("fs", n))
                        for tt in range(TT):
                            c0, c1 = (0, P) if tt == 0 else (P, P + S)
                            ins = vec.tensor_reduce(small["negmax"][:, n, tt:tt + 1], src[:, c0:c1], AX_X, ALU.max, negate=True)
                            ins.then_inc(sem("fox_max"), 1)
                    if n >= 2:
                        attention_out(("fs", n - 2), ("fo", n - 2), fo[:, n - 2, :, :], P, n - 2)

            for g in range(2):
                vec.wait_ge(sem("gate_tanh"), 2 * g + 2)
                step(vec.tensor_scalar(gate[g][:, :, :], gate[g][:, :, :], 0.5, 0.5, ALU.mult, ALU.add))
            settle()
            split_to(UNIT["brA"] + 4)
            for j in range(2):
                if j:
                    token_groups("ob")
                    split_to(UNIT["brB"] + 2)
                d = gate[0][:, :, j * NB:(j + 1) * NB]
                took_block("brA", j, vec.tensor_tensor(d, d, block_values("brA", j), ALU.mult))
            for tt in range(TT):
                r, g = recip_roots("mem_kv", tt), gain("mem_kv")
                vec.scalar_tensor_tensor(mem[:, tt, :], mem[:, tt, :], r, g, ALU.mult, ALU.mult)\
                    .then_inc(sem("mem_normed"), 1)
            split_to(UNIT["brB"] + 4)
            for j in range(2):
                c = slice(j * NB, (j + 1) * NB)
                d = gate[1][:, :, c]
                took_block("brB", j, vec.tensor_tensor(d, d, block_values("brB", j), ALU.mult))
                vec.wait_ge(pair_taken[j], taken("brB", j)[1])
                vec.tensor_tensor(y[:, :, c], gate[0][:, :, c], d, ALU.add).then_inc(sem("y2_ready"), 1)
                if j == 0:
                    token_groups("memn", mt_high, mt_rest)
                    split_to(UNIT["mk"] + 2)
            split_to(UNIT["mk"] + 4)
            token_groups("y2")
            split_to(UNIT["wout2"] + 4)
            took_block("wout2", 0, vec.tensor_copy(y[:, :, 0:NB], block_values("wout2", 0)))
            split_to(UNIT["mv"] + 2)
            post_norm("mix_post", 1.0, 0)
            pre_norm("mem_pre", 0)
            post_norm("mix_post", 1.0, 1)
            split_to(UNIT["mv"] + 3)
            pre_norm("mem_pre", 1)
            split_to(UNIT["mq"] + 2)
            token_groups("mpre")
            split_to(UNIT["mq"] + 4)
            split_to(UNIT["mo"] + 1)

            def maxima(h):
                src = aux(("ms", h)).rearrange("p (t s) -> p t s", t=TT)
                vec.tensor_reduce(small["negmax"][:, h, :], src, AX_X, ALU.max, negate=True).then_inc(sem("mem_max"), 1)

            def outputs(h):
                attention_out(("ms", h), ("mo", h), mo[:, :, h * S:(h + 1) * S], S, h)

            def out_groups(q):
                for tt in range(TT):
                    at = (slice(None), slice(4 * q, 4 * q + 4), slice(tt * P, (tt + 1) * P))
                    group_to_rest(("om", 2 * tt + q), xt_high[at], xt_rest[at])

            maxima(0)
            split_to(UNIT["mo"] + 2)
            maxima(1)
            maxima(2)
            outputs(0)
            maxima(3)
            outputs(1)
            out_groups(0)
            split_to(UNIT["mo"] + 4)
            outputs(2)
            outputs(3)
            out_groups(1)
            split_to(UNIT["upB"] + 2)
            post_norm("mem_post", 1.0, 0, "ffn2_pre")
            tile_groups("f2", 0)
            post_norm("mem_post", 1.0, 1, "ffn2_pre")
            tile_groups("f2", 1)
            ffn("upB", "downB", "hB", "ffn2_pre", "end")
            for tt in range(TT):
                post_norm("ffn2_post", 0.5, tt)
            assert split[0] == UNIT["end"]


def constants():
    f32 = np.float32
    tok = np.arange(S)
    out = {"c_ident": np.eye(P, dtype=f32), "c_identb": np.eye(P, dtype=f32).astype(np.dtype("bfloat16"))}
    causal = np.where(np.arange(P)[None, :] <= np.arange(P)[:, None], 0.0, NEG).astype(f32)
    out["c_causal"] = causal.astype(np.dtype("bfloat16"))
    starts = np.broadcast_to((tok % CHUNK != 0).astype(f32), (P, S))
    out["c_starts"] = np.ascontiguousarray(starts).astype(np.dtype("bfloat16"))
    s, t = np.arange(P)[:, None], np.arange(P)[None, :]
    levels = [s == t]
    for n in LEVELS:
        pairs = (s // (2 * n) == t // (2 * n)) & (s % (2 * n) < n)
        levels.append(np.tile(pairs[:, t[0] % (2 * n) >= n], (1, TT)))
    out["c_levels"] = np.ascontiguousarray(np.stack(levels, 1).astype(f32))
    gamma = 1.0 - 2.0 ** (-5.0 - np.arange(RH))
    i, j = tok[None, :], tok[:, None]
    seen = (i // CHUNK >= j // CHUNK)
    full = np.where(seen, gamma[:, None, None] ** np.abs(i - j), 0.0) * P ** -0.5
    decay = np.concatenate([full[:, 0:P, :], full[:, P:S, P:S]], axis=2)
    out["c_decay"] = np.ascontiguousarray(decay.transpose(1, 0, 2).astype(f32))
    win = []
    for w in (2, 4, 8, 16):
        m = ((j <= i) & (j > i - w)) / np.minimum(i + 1, w) - (i == j)
        win.append(m)
    win = np.stack(win).reshape(RH, TT, P, S).transpose(2, 1, 0, 3)
    out["c_window"] = np.ascontiguousarray(win.astype(f32))
    inv = (f32(10000.0) ** (-np.arange(0, P, 2, dtype=f32) / f32(P))).astype(f32)
    ang = (tok.astype(f32)[:, None] * inv[None, :]).astype(f32).astype(np.float64)
    cos, sin = np.cos(ang), np.sin(ang)
    for name, a, b in (("c_ropec", cos, cos), ("c_ropes", -sin, sin)):
        v = np.concatenate([a, b], axis=1).reshape(TT, P, P).transpose(1, 0, 2)
        out[name] = np.ascontiguousarray(v.astype(f32))
    return out


_VECTORS = {"ln1_g": "ln1_g", "ln1_b": "ln1_b", "ln2_g": "ln2_g", "ln2_b": "ln2_b",
            "ffn1_pre": "ffn1_pre_g_2", "ffn1_post": "ffn1_post_g_2", "mix_pre": "mix_pre_g_2",
            "hg_norm": "hg_norm_g_2", "mem_kv": "mem_kv_g_2", "mix_post": "mix_post_g_2",
            "mem_pre": "mem_pre_g_2", "mem_post": "mem_post_g_2", "ffn2_pre": "ffn2_pre_g_2",
            "ffn2_post": "ffn2_post_g_2"}
_WEIGHTS = ["w_in", "w_out", "w_up", "w_down", "ffn1_w_in_2", "ffn1_w_down_2", "w_in_2", "w_branch_a_2",
            "w_branch_b_2", "w_out_2", "w_mq_2", "w_mkv_2", "w_mo_2", "ffn2_w_in_2", "ffn2_w_down_2", "w_pool"]


def kernel(**inputs):
    import concourse.bacc as _bacc
    from concourse.bass_utils import run_bass_kernel_spmd as _run

    nc = _bacc.Bacc("TRN2", target_bir_lowering=False, num_devices=1)
    laid = {name: np.asarray(inputs[name])[0] for name in _WEIGHTS}
    laid["x"] = np.asarray(inputs["x"])[0]
    laid["mem_2"] = np.asarray(inputs["mem_2"])[0]
    for name, src in _VECTORS.items():
        laid["gain_" + name] = np.asarray(inputs[src])[0]
    bias = np.asarray(inputs["b_gate_2"])[0]
    laid["gain_gate0"], laid["gain_gate1"] = bias[:D], bias[D:]
    laid["fox_f_bias_2"] = np.asarray(inputs["fox_f_bias_2"])[0]
    laid["conv_w"] = np.asarray(inputs["conv_w"])[0].reshape(3, FC, P).transpose(2, 1, 0).reshape(P, FC * 3)
    laid["conv_b"] = np.asarray(inputs["conv_b"])[0].reshape(FC, P).T
    laid["pool_scale"] = np.asarray(inputs["pool_scale"])[0].reshape(RH, P).T
    laid["hg_lb_logits_2"] = np.asarray(inputs["hg_lb_logits_2"]).transpose(2, 0, 1)
    laid.update(constants())
    arrays, dram = {}, {}
    for name, a in laid.items():
        a = np.ascontiguousarray(a)
        arrays[f"in_{name}_dram"] = a
        dram[name] = nc.dram_tensor(f"in_{name}_dram", a.shape, mybir.dt.from_np(a.dtype), kind="ExternalInput").ap()
    out = nc.dram_tensor("out_0_dram", (S, D), F32, kind="ExternalOutput").ap()
    build(nc, dram, out)
    r = _run(nc, [arrays], core_ids=[0])
    return r.results[0]["out_0_dram"].reshape(1, S, D)
```
